# Optimizing a Trainium2 kernel written in Bass

```python
import math, functools
import jax, jax.numpy as jnp
from jax import lax
import numpy as np

D_MODEL = 1024
BATCH = 1
SEQ = 1024
DEPTH = 1
DEC_BATCH = 8
DEC_SEQ = 8
PAST_LEN = 256
PAGE_SIZE = 128

D_MIX = D_MODEL
D_CONV = D_MIX // 2
CONV_W = 3
N_HEADS = 8
HEAD_DIM = (D_MIX - D_CONV) // N_HEADS
N_IDX_HEADS = 8
IDX_DIM = 64
TOPK_MAX = 256
Q_BLOCK = 128
ROPE_THETA = 10000.0
N_MEM = 256
MEM_HEADS = 4
MEM_HEAD_DIM = D_MODEL // MEM_HEADS
D_FF = 2816
EPS = 1e-6
ATTN_SCALE = HEAD_DIM ** -0.5
MEM_SCALE = MEM_HEAD_DIM ** -0.5
IDX_SCALE = (N_IDX_HEADS * IDX_DIM) ** -0.5
PROJ_SIZES = (D_CONV, D_CONV, D_CONV, N_HEADS * HEAD_DIM, N_HEADS * HEAD_DIM, N_HEADS * HEAD_DIM, N_IDX_HEADS * IDX_DIM, IDX_DIM, N_IDX_HEADS)
D_IN = 3 * D_CONV + 3 * N_HEADS * HEAD_DIM + N_IDX_HEADS * IDX_DIM + IDX_DIM + N_IDX_HEADS

kernel_name = 'hybrid_conv_dsa_memory_convffn_step'

def rms_norm(x, g):
    xf = x.astype(jnp.float32)
    y = xf * lax.rsqrt(jnp.mean(xf * xf, axis=-1, keepdims=True) + EPS)
    return (y * g.astype(jnp.float32)).astype(x.dtype)

def rope(x, pos):
    d = x.shape[-1]
    half = d // 2
    inv = jnp.exp(jnp.arange(half, dtype=jnp.float32) * (-2.0 * math.log(ROPE_THETA) / d))
    ang = pos.astype(jnp.float32)[:, None] * inv[None, :]
    shape = (ang.shape[0],) + (1,) * (x.ndim - 3) + (half,)
    cos = jnp.cos(ang).reshape(shape)
    sin = jnp.sin(ang).reshape(shape)
    xf = x.astype(jnp.float32)
    x1, x2 = xf[..., :half], xf[..., half:]
    return jnp.concatenate([x1 * cos - x2 * sin, x2 * cos + x1 * sin], axis=-1).astype(x.dtype)

def causal_dwconv3(u, prev, w):
    t = u.shape[1]
    ext = jnp.concatenate([prev.astype(u.dtype), u], axis=1)
    y = sum(ext[:, j:j + t] * w[j] for j in range(CONV_W))
    return y, ext[:, t:]

def split_projection(z, pos, q_g, k_g):
    b, t = z.shape[:2]
    cuts = np.cumsum(PROJ_SIZES)[:-1].tolist()
    cb, cc, ch, q, k, v, qi, ki, iw = jnp.split(z, cuts, axis=-1)
    q = rope(rms_norm(q.reshape(b, t, N_HEADS, HEAD_DIM), q_g), pos)
    k = rope(rms_norm(k.reshape(b, t, N_HEADS, HEAD_DIM), k_g), pos)
    v = v.reshape(b, t, N_HEADS, HEAD_DIM)
    qi = rope(qi.reshape(b, t, N_IDX_HEADS, IDX_DIM), pos)
    ki = rope(ki, pos)
    return cb, cc, ch, q, k, v, qi, ki, iw

def indexer_scores(qi, iw, ki):
    dots = jnp.einsum('bthd,bsd->bths', qi, ki, preferred_element_type=jnp.float32)
    return jnp.einsum('bths,bth->bts', jax.nn.relu(dots), iw.astype(jnp.float32)) * IDX_SCALE

def prompt_sparse_attention(q, k, v, qi, ki, iw):
    b, s = q.shape[:2]
    topk = min(TOPK_MAX, s // 4)
    key_pos = jnp.arange(s)
    gather_rows = jax.vmap(lambda rows, idx: rows[idx])

    def block(i):
        t0 = i * Q_BLOCK
        qb = lax.dynamic_slice_in_dim(q, t0, Q_BLOCK, axis=1)
        qib = lax.dynamic_slice_in_dim(qi, t0, Q_BLOCK, axis=1)
        iwb = lax.dynamic_slice_in_dim(iw, t0, Q_BLOCK, axis=1)
        q_pos = t0 + jnp.arange(Q_BLOCK)
        sc = indexer_scores(qib, iwb, ki)
        sc = jnp.where(key_pos[None, None, :] <= q_pos[None, :, None], sc, -jnp.inf)
        _, sel = lax.top_k(sc, topk)
        valid = sel <= q_pos[None, :, None]
        ks = gather_rows(k, sel)
        vs = gather_rows(v, sel)
        logits = jnp.einsum('bthd,btkhd->bthk', qb, ks, preferred_element_type=jnp.float32) * ATTN_SCALE
        p = jax.nn.softmax(jnp.where(valid[:, :, None, :], logits, -jnp.inf), axis=-1)
        o = jnp.einsum('bthk,btkhd->bthd', p.astype(vs.dtype), vs)
        return o.reshape(b, Q_BLOCK, N_HEADS * HEAD_DIM)

    out = lax.map(block, jnp.arange(s // Q_BLOCK))
    return out.transpose(1, 0, 2, 3).reshape(b, s, N_HEADS * HEAD_DIM)

def sample_sparse_attention(q, k, v, qi, ki, iw, pool_k, pool_v, pool_idx_k, page_table):
    b, t = q.shape[:2]
    past = page_table.shape[1] * PAGE_SIZE
    topk = min(TOPK_MAX, (past + t) // 4)
    ki_past = pool_idx_k[page_table].reshape(b, past, IDX_DIM).astype(ki.dtype)
    ki_all = jnp.concatenate([ki_past, ki], axis=1)
    q_pos = past + jnp.arange(t)
    key_pos = jnp.arange(past + t)
    sc = indexer_scores(qi, iw, ki_all)
    sc = jnp.where(key_pos[None, None, :] <= q_pos[None, :, None], sc, -jnp.inf)
    _, sel = lax.top_k(sc, topk)
    in_past = sel < past
    logical = jnp.minimum(sel, past - 1)
    phys = jax.vmap(lambda pt, idx: pt[idx])(page_table, logical // PAGE_SIZE)
    off = logical % PAGE_SIZE
    kp = pool_k[phys, off]
    vp = pool_v[phys, off]
    new_pos = past + jnp.arange(t)
    sel_new = jnp.any(sel[..., None] == new_pos, axis=2)
    sel_new = sel_new & (new_pos[None, None, :] <= q_pos[None, :, None])
    lp = jnp.einsum('bthd,btkhd->bthk', q, kp, preferred_element_type=jnp.float32)
    ln = jnp.einsum('bthd,bjhd->bthj', q, k, preferred_element_type=jnp.float32)
    logits = jnp.concatenate([lp, ln], axis=-1) * ATTN_SCALE
    mask = jnp.concatenate([in_past, sel_new], axis=-1)[:, :, None, :]
    p = jax.nn.softmax(jnp.where(mask, logits, -jnp.inf), axis=-1).astype(v.dtype)
    o = (jnp.einsum('bthk,btkhd->bthd', p[..., :topk], vp.astype(v.dtype))
         + jnp.einsum('bthj,bjhd->bthd', p[..., topk:], v))
    return o.reshape(b, t, N_HEADS * HEAD_DIM)

def mixer_sublayer(h, pos, conv_prev, attend, g, w_in, conv_w, q_g, k_g, w_out):
    xn = rms_norm(h, g)
    cb, cc, ch, q, k, v, qi, ki, iw = split_projection(xn @ w_in, pos, q_g, k_g)
    conv_out, conv_state = causal_dwconv3(cc * ch, conv_prev, conv_w)
    att = attend(q, k, v, qi, ki, iw)
    y = jnp.concatenate([cb * conv_out, att.astype(h.dtype)], axis=-1) @ w_out
    return h + y, conv_state, k, v, ki

def memory_kv(mem, g_src, w_kv, k_g):
    b, m, _ = mem.shape
    mk, mv = jnp.split(rms_norm(mem, g_src) @ w_kv, 2, axis=-1)
    mk = rms_norm(mk.reshape(b, m, MEM_HEADS, MEM_HEAD_DIM), k_g)
    return mk, mv.reshape(b, m, MEM_HEADS, MEM_HEAD_DIM)

def memory_sublayer(h, mk, mv, g, w_q, q_g, w_o):
    b, t, _ = h.shape
    q = rms_norm((rms_norm(h, g) @ w_q).reshape(b, t, MEM_HEADS, MEM_HEAD_DIM), q_g)
    logits = jnp.einsum('bthd,bmhd->bhtm', q, mk, preferred_element_type=jnp.float32) * MEM_SCALE
    p = jax.nn.softmax(logits, axis=-1).astype(mv.dtype)
    o = jnp.einsum('bhtm,bmhd->bthd', p, mv).reshape(b, t, MEM_HEADS * MEM_HEAD_DIM)
    return h + (o @ w_o).astype(h.dtype)

def ffn_sublayer(h, prev, g, w_gu, conv_w, conv_b, w_down):
    gate, up = jnp.split(rms_norm(h, g) @ w_gu, 2, axis=-1)
    gate_c, state = causal_dwconv3(gate, prev, conv_w)
    return h + (jax.nn.silu(gate_c + conv_b) * up) @ w_down, state

def setup_inputs(seed: int = 0) -> dict:
    key = jax.random.key(seed)
    ks = jax.random.split(key, 32)

    def nrm(i, shape, scale):
        return jax.random.normal(ks[i], shape, jnp.float32) * scale

    def gain(i, n):
        return 1.0 + 0.1 * jax.random.normal(ks[i], (DEPTH, n), jnp.float32)

    n_pages = PAST_LEN // PAGE_SIZE
    n_used = DEC_BATCH * n_pages
    n_pool = n_used + n_used // 4
    page_table = jax.random.permutation(ks[0], n_pool)[:n_used].reshape(DEC_BATCH, n_pages).astype(jnp.int32)
    return {
        'x_prompt': nrm(1, (BATCH, SEQ, D_MODEL), 1.0),
        'x_sample': nrm(2, (DEC_BATCH, DEC_SEQ, D_MODEL), 1.0),
        'cache_k': nrm(3, (DEPTH, n_pool, PAGE_SIZE, N_HEADS, HEAD_DIM), 1.0),
        'cache_v': nrm(4, (DEPTH, n_pool, PAGE_SIZE, N_HEADS, HEAD_DIM), 1.0),
        'cache_idx_k': nrm(5, (DEPTH, n_pool, PAGE_SIZE, IDX_DIM), 1.0),
        'state_conv_mix': nrm(6, (DEPTH, DEC_BATCH, CONV_W - 1, D_CONV), 1.0),
        'state_conv_ffn': nrm(7, (DEPTH, DEC_BATCH, CONV_W - 1, D_FF), 1.0),
        'cache_mem_k': nrm(8, (DEPTH, DEC_BATCH, N_MEM, MEM_HEADS, MEM_HEAD_DIM), 1.0),
        'cache_mem_v': nrm(9, (DEPTH, DEC_BATCH, N_MEM, MEM_HEADS, MEM_HEAD_DIM), 1.0),
        'page_table': page_table,
        'mem_prompt': nrm(10, (BATCH, N_MEM, D_MODEL), 1.0),
        'g_mix': gain(11, D_MODEL),
        'w_in': nrm(12, (DEPTH, D_MODEL, D_IN), D_MODEL ** -0.5),
        'conv_mix_w': nrm(13, (DEPTH, CONV_W, D_CONV), CONV_W ** -0.5),
        'q_norm_g': gain(14, HEAD_DIM),
        'k_norm_g': gain(15, HEAD_DIM),
        'w_out': nrm(16, (DEPTH, D_MIX, D_MODEL), D_MIX ** -0.5),
        'g_mem': gain(17, D_MODEL),
        'g_mem_src': gain(18, D_MODEL),
        'w_q_mem': nrm(19, (DEPTH, D_MODEL, MEM_HEADS * MEM_HEAD_DIM), D_MODEL ** -0.5),
        'w_kv_mem': nrm(20, (DEPTH, D_MODEL, 2 * MEM_HEADS * MEM_HEAD_DIM), D_MODEL ** -0.5),
        'mq_norm_g': gain(21, MEM_HEAD_DIM),
        'mk_norm_g': gain(22, MEM_HEAD_DIM),
        'w_o_mem': nrm(23, (DEPTH, MEM_HEADS * MEM_HEAD_DIM, D_MODEL), (MEM_HEADS * MEM_HEAD_DIM) ** -0.5),
        'g_ffn': gain(24, D_MODEL),
        'w_gu': nrm(25, (DEPTH, D_MODEL, 2 * D_FF), D_MODEL ** -0.5),
        'conv_ffn_w': nrm(26, (DEPTH, CONV_W, D_FF), CONV_W ** -0.5),
        'conv_ffn_b': nrm(27, (DEPTH, D_FF), 0.02),
        'w_down': nrm(28, (DEPTH, D_FF, D_MODEL), D_FF ** -0.5),
    }

def reference(x_prompt, x_sample, cache_k, cache_v, cache_idx_k, state_conv_mix, state_conv_ffn,
              cache_mem_k, cache_mem_v, page_table, mem_prompt,
              g_mix, w_in, conv_mix_w, q_norm_g, k_norm_g, w_out,
              g_mem, g_mem_src, w_q_mem, w_kv_mem, mq_norm_g, mk_norm_g, w_o_mem,
              g_ffn, w_gu, conv_ffn_w, conv_ffn_b, w_down):
    b, s, _ = x_prompt.shape
    past = page_table.shape[1] * PAGE_SIZE
    pos_p = jnp.arange(s)
    pos_s = past + jnp.arange(x_sample.shape[1])
    zero_mix = jnp.zeros((b, CONV_W - 1, D_CONV), x_prompt.dtype)
    zero_ffn = jnp.zeros((b, CONV_W - 1, D_FF), x_prompt.dtype)
    hp, hs = x_prompt, x_sample
    kp_l, vp_l, ikp_l, cmp_l, cfp_l, mkp_l, mvp_l = [], [], [], [], [], [], []
    ks_l, vs_l, iks_l, cms_l, cfs_l = [], [], [], [], []
    for l in range(DEPTH):
        hp, c_mix, k_new, v_new, ik_new = mixer_sublayer(
            hp, pos_p, zero_mix, prompt_sparse_attention,
            g_mix[l], w_in[l], conv_mix_w[l], q_norm_g[l], k_norm_g[l], w_out[l])
        mk, mv = memory_kv(mem_prompt, g_mem_src[l], w_kv_mem[l], mk_norm_g[l])
        hp = memory_sublayer(hp, mk, mv, g_mem[l], w_q_mem[l], mq_norm_g[l], w_o_mem[l])
        hp, c_ffn = ffn_sublayer(hp, zero_ffn, g_ffn[l], w_gu[l], conv_ffn_w[l], conv_ffn_b[l], w_down[l])
        kp_l.append(k_new); vp_l.append(v_new); ikp_l.append(ik_new)
        cmp_l.append(c_mix); cfp_l.append(c_ffn); mkp_l.append(mk); mvp_l.append(mv)

        attend_s = functools.partial(sample_sparse_attention, pool_k=cache_k[l], pool_v=cache_v[l],
                                     pool_idx_k=cache_idx_k[l], page_table=page_table)
        hs, c_mix_s, k_s, v_s, ik_s = mixer_sublayer(
            hs, pos_s, state_conv_mix[l], attend_s,
            g_mix[l], w_in[l], conv_mix_w[l], q_norm_g[l], k_norm_g[l], w_out[l])
        hs = memory_sublayer(hs, cache_mem_k[l], cache_mem_v[l], g_mem[l], w_q_mem[l], mq_norm_g[l], w_o_mem[l])
        hs, c_ffn_s = ffn_sublayer(hs, state_conv_ffn[l], g_ffn[l], w_gu[l], conv_ffn_w[l], conv_ffn_b[l], w_down[l])
        ks_l.append(k_s); vs_l.append(v_s); iks_l.append(ik_s); cms_l.append(c_mix_s); cfs_l.append(c_ffn_s)

    return (hp, hs,
            jnp.stack(kp_l), jnp.stack(vp_l), jnp.stack(ikp_l), jnp.stack(cmp_l), jnp.stack(cfp_l),
            jnp.stack(mkp_l), jnp.stack(mvp_l),
            jnp.stack(ks_l), jnp.stack(vs_l), jnp.stack(iks_l), jnp.stack(cms_l), jnp.stack(cfs_l))


_drawn_inputs = setup_inputs


def setup_inputs(seed=0):
    import zlib

    import numpy as np

    out = dict(_drawn_inputs(seed))
    spreads = {}
    factors = {'q_norm_g': 5.189, 'g_mem': 6.254, 'mq_norm_g': 6.235, 'conv_ffn_b': 6.641}
    for name, (base, spread) in spreads.items():
        noise = np.random.default_rng([zlib.crc32(name.encode()), seed]).standard_normal(out[name].shape)
        drawn = base * np.exp(spread * noise) if base else spread * noise
        out[name] = __import__('jax').numpy.asarray(drawn.astype(out[name].dtype))
    for name, factor in factors.items():
        out[name] = (out[name] * factor).astype(out[name].dtype)
    return out
```

```python
from contextlib import ExitStack
import math

import numpy as np
import concourse.bass as bass
from concourse import mybir

F32 = mybir.dt.float32
F16 = mybir.dt.float16
BF16 = mybir.dt.bfloat16
I32 = mybir.dt.int32
ALU = mybir.AluOpType
ACT = mybir.ActivationFunctionType
AX = mybir.AxisListType

P = 128
D = 1024
KT = D // P
SEQ = 1024
DEC_B, DEC_T = 8, 8
NS = DEC_B * DEC_T
T = SEQ + NS
NT = 9
NB = SEQ // P
PAST, PAGE = 256, 128
NPG = PAST // PAGE
N_POOL = 20
H, HD = 8, 64
DA = H * HD
DC = 512
NC_T = DC // P
D_IN = 3656
MH, MD = 4, 256
NMEM = 256
DFF = 2816
FT = DFF // P
TOPK = 256
S_KEYS = PAST + DEC_T
TOPK_S = S_KEYS // 4
EPS = 1e-6
ATT_SCALE = HD ** -0.5
MEM_SCALE = MD ** -0.5
IDX_SCALE = (H * HD) ** -0.5
NEG = -3.0e38
MASKED = -1.0e30
GW = SEQ + 2 + DEC_B * (DEC_T + 2)
CW = GW - 2
SB0 = SEQ + 2
STR = DEC_T + 2
DIAG = NS + DEC_T
QB, KB, VB, QIB, KIB = 1536, 2048, 2560, 3072, 3584


def rows(j):
    return P if j < NB else NS


def token_chunks():
    return [(0, 512), (512, 512), (1024, NS)]


def topk_cols(i):
    return sum((k + 1) * P for k in range(2, i))


def build(nc, io):
    ctx = ExitStack()
    with ctx:
        sems = {}

        on = {}
        for what in ("ss", "rt", "rc", "xn", "tp", "hi", "lo"):
            on |= {f"n2_{what}": (f"n1_{what}", NT), f"nm_{what}": (f"n1_{what}", 2 * NT),
                   f"n3_{what}": (f"n1_{what}", 2 * NT + 2)}
        for what, a, b in (("hi", 18, 34), ("lo", 18, 34), ("ld0", 272, 400), ("ld1", 272, 400)):
            on |= {f"wb_{what}": (f"wa_{what}", a), f"wc_{what}": (f"wa_{what}", b)}
        for what in ("ss", "rt"):
            on |= {f"mk_{what}": (f"s2_{what}", 2 * NT), f"q7_{what}": (f"s2_{what}", 2 * NT + 4)}
        for k in range(2):
            on |= {f"mkb_ld{k}": (f"kb_ld{k}", 128), f"mvb_ld{k}": (f"vb_ld{k}", 128), f"dw_ld{k}": (f"fw_ld{k}", 16 * FT)}
        on |= {"dw_hi": ("fw_hi", 2 * FT), "dw_lo": ("fw_lo", 2 * FT), "l8_mm": ("l6_mm", 2 * NT),
               "l8_ev": ("l6_ev", 2 * NT), "mkb_tp": ("kb_tp", 16), "mkb_ev": ("kb_ev", 16),
               "q7_tp": ("s2_tp", 4 * NT), "q7_te": ("s2_te", 4 * NT), "q7_raw": ("s2_raw", 4 * NT),
               "q7_n": ("s2_roped", 4 * NT), "ffnst_tp": ("mixst_tp", 1), "ffnst_ev": ("mixst_ev", 1)}
        for what, a in (("qk", 64), ("exp", 64), ("hi", 8), ("lo", 8), ("nm", 64), ("pte", 64), ("pv", 64), ("tt", 64)):
            on[f"ma_{what}"] = (f"at_{what}", a)

        def sem(name):
            name = on.get(name, (name, 0))[0]
            if name not in sems:
                sems[name] = ctx.enter_context(nc.semaphore(name))
            return sems[name]

        def upto(name, count):
            return on.get(name, (name, 0))[1] + count

        def sb(name, shape, dt):
            return ctx.enter_context(nc.sbuf_tensor(name, shape, dt))

        ident = sb("ident", [P, P], F32)
        mask01 = sb("mask01", [P, 2 * P], F32)
        smask = sb("smask", [P, DEC_T], F32)
        cos_t = sb("cos_t", [P, NT, 32], F32)
        sin_t = sb("sin_t", [P, NT, 32], F32)
        gb = sb("gb", [P, D], F32)
        qkg = sb("qkg", [P, 2, HD], F32)
        mqkg = sb("mqkg", [P, 2, MD], F32)
        mix_sw = sb("mix_sw", [P, NC_T, 20], F32)
        ffn_sw = sb("ffn_sw", [P, FT, 20], F32)
        stat = sb("stat", [P, 96], F32)
        att_st = sb("att_st", [P, 2, 4], F32)
        sat_st = sb("sat_st", [NS, 4, H], F32)
        eps = sb("eps", [P, 1], F32)
        iwt = sb("iwt", [P, NT, H], F32)
        pts = sb("pts", [1, DEC_B * NPG], I32)
        m8 = sb("m8", [P, 8], F32)

        sizes = [("XA", 2 * KT * T * 2), ("H", NT * D * 4), ("QK", 2 * KT * T * 2), ("QI", 4 * T * 4),
                 ("KI", T * 4), ("CT", 2 * NC_T * T * 2), ("W", 49152), ("SP", 4416)]
        off, at = {}, 0
        for name, size in sizes:
            off[name] = at
            at += size
        arena = sb("arena", [P, at // 4], F32)

        def view(region, shift, shape, dt=F32, parts=P):
            size = {F32: 4, F16: 2, BF16: 2}[dt]
            n = int(np.prod(shape))
            a = (off[region] + shift) // 4
            v = arena[0:parts, a:a + n * size // 4]
            if dt != F32:
                v = v.bitcast(dt)
            if len(shape) == 2:
                v = v.rearrange("p (a b) -> p a b", a=shape[0])
            if len(shape) == 3:
                v = v.rearrange("p (a b c) -> p a b c", a=shape[0], b=shape[1])
            return v

        PS = ctx.enter_context(nc.psum_tensor("PS", [P, 8, 512], F32))

        xa_hi, xa_lo = view("XA", 0, [KT, T], F16), view("XA", KT * T * 2, [KT, T], BF16)
        xb_hi, xb_lo = view("QK", 0, [KT, T], F16), view("QK", KT * T * 2, [KT, T], BF16)
        ct_hi, ct_lo = view("CT", 0, [NC_T, T], F16), view("CT", NC_T * T * 2, [NC_T, T], BF16)
        h = view("H", 0, [NT, D])
        V = view("H", 0, [NT, DA])
        work = view("H", NT * DA * 4, [4224])
        work_s = view("H", NT * DA * 4 + 4224 * 4, [S_KEYS + 8], parts=NS)
        qT = view("QK", 0, [4, T])
        kT = view("QK", 4 * T * 4, [4, T])
        qiT = view("QI", 0, [4, T])
        kiT = view("KI", 0, [T])
        raw = view("CT", 0, [3, 512])
        rope1 = view("CT", 6144, [512])
        rope2 = view("CT", 8192, [512])
        roped = view("CT", 10240, [3, 512])
        relu = view("CT", 0, [2, SEQ])
        idx_raw = view("CT", 8192, [2 * DEC_B * NPG // 2, P])
        kiTb = view("H", 0, [DEC_B, S_KEYS])
        qm_i = view("H", 8448 + 64, [4 * 512 + 64])
        cb_s = view("QI", 0, [CW])
        cc_s = view("QI", 4 * CW, [GW])
        ch_s = view("QI", 8 * CW, [CW])
        u_s = view("QI", 12 * CW, [GW])
        tap2 = view("SP", 0, [CW])
        u_state = view("H", NT * DA * 4 + 4224 * 4 + 1088, [NC_T, 18])
        kTb = view("W", 0, [4, DEC_B * S_KEYS])
        logit = view("W", 33792, [2, SEQ])
        pT = view("QI", 0, [2, NB, P])
        p_s = view("QI", 8192, [H, S_KEYS], parts=NS)
        pT_s = view("W", 41984, [H, 3, NS])
        kpage = view("SP", 0, [2, DA])
        vpage = view("KI", 0, [2, DA])
        v_new = view("H", NT * DA * 4, [DEC_B, DA], parts=DEC_T)
        qm_a = view("XA", NC_T * T * 2, [4 * 512 + 64])
        xm_hi, xm_lo = view("CT", 0, [KT, NMEM], F16), view("CT", KT * NMEM * 2, [KT, NMEM], BF16)
        memx = view("XA", 0, [2, D])
        mraw = view("XA", 8192, [4, 512])
        mtmp = view("XA", 16384, [512])
        mkT = view("QI", 0, [KT, NMEM])
        mv = view("QI", 8192, [2, D])
        qraw = view("CT", 8192, [3, 512])
        qtmp = view("CT", 8192 + 6144, [512])
        mat_st = view("CT", 16384, [2, 4, MH])
        mqT = view("XA", 0, [KT, T])
        mlog = view("CT", 0, [2, D])
        mpT = view("CT", 8192, [2, KT, P])
        mKT = view("W", 0, [2, 2, DEC_B * NMEM])
        mkpage = view("W", 32768, [2, 2, MD])
        mvpage = view("W", 32768 + 4096, [2, 2, MD])
        qm_m = view("W", 40960, [2 * 512 + 64])
        mpT_s = view("W", 45312, [4, 2 * NS])
        mp_s = view("W", 47360, [NMEM], parts=NS)
        st_mix = view("QK", 0, [DC], parts=20)
        st_ffn = view("QK", 2048, [DFF], parts=20)
        ffn_hi = view("H", 0, [FT, T], F16)
        ffn_lo = view("H", FT * T * 2, [FT, T], BF16)
        fbase = 2 * FT * T * 2
        gate_s = view("H", fbase, [GW + 6])
        conv_s = view("H", fbase + 4448, [2, GW + 6])
        fst = view("H", fbase + 4448 * 3, [2, KT, P])
        fw_hi = view("H", fbase + 4448 * 3 + 8192, [2, 2, KT * P], F16)
        fw_lo = view("H", fbase + 4448 * 3 + 16384, [2, 2, KT * P], BF16)
        g_state = view("H", fbase + 45056 + 11264, [FT, 18])
        dbase = fbase
        dst = view("XA", 0, [2, 11, 256])
        dw_hi = view("H", dbase, [2, FT * 256], F16)
        dw_lo = view("H", dbase + 22528, [2, FT * 256], BF16)
        res = view("XA", 22528, [4, 256])
        outb = view("XA", 22528 + 4096, [4, 256])

        wst = [view("W", 8192 * k, [4, 512]) for k in range(2)]
        w_hi = [view("W", 16384 + 8192 * k, [KT, 512], F16) for k in range(2)]
        w_lo = [view("W", 32768 + 8192 * k, [KT, 512], BF16) for k in range(2)]

        def mask_view(buf, pair):
            return buf[:, pair * 512:pair * 512 + 8 * DIAG].rearrange("p (b c) -> p b c", c=DIAG)[:, :, 0:DEC_T]

        class Weights:

            def __init__(self, name, chunks, used):
                self.name, self.chunks, self.used = name, chunks, used

            def n(self, what):
                return f"{self.name}_{what}"

            def s(self, what):
                return sem(self.n(what))

            def load(self, e, n):
                src, width = self.chunks[n]
                for half in range(2):
                    if n >= 1:
                        e.wait_ge(sem(self.n("lo")), upto(self.n("lo"), 2 * (n - 1) + half + 1))
                    parts = src if isinstance(src, list) else [src]
                    c = 0
                    for k, part in enumerate(parts):
                        w = part.shape[1]
                        e.dma_start(wst[half][:, :, c:c + w],
                                    part.rearrange("(k p) n -> p k n", p=P)[:, 4 * half:4 * half + 4, :]
                                    ).then_inc(self.s(f"ld{half}"), 16)
                        c += w

            def split_hi(self, e, n):
                if n >= len(self.chunks):
                    return
                src, width = self.chunks[n]
                loads = sum(len(c[0]) if isinstance(c[0], list) else 1 for c in self.chunks[:n + 1])
                if n >= 2:
                    name, count = self.used(n - 2)
                    e.wait_ge(sem(name), upto(name, count))
                for half in range(2):
                    e.wait_ge(sem(self.n(f"ld{half}")), upto(self.n(f"ld{half}"), 16 * loads))
                    e.activation(w_hi[n % 2][:, 4 * half:4 * half + 4, 0:width], wst[half][:, :, 0:width],
                                 ACT.Copy).then_inc(self.s("hi"), 1)

            def split_lo(self, e, n):
                src, width = self.chunks[n]
                for half in range(2):
                    e.wait_ge(sem(self.n("hi")), upto(self.n("hi"), 2 * n + half + 1))
                    e.tensor_tensor(w_lo[n % 2][:, 4 * half:4 * half + 4, 0:width], wst[half][:, :, 0:width],
                                    w_hi[n % 2][:, 4 * half:4 * half + 4, 0:width],
                                    ALU.subtract).then_inc(self.s("lo"), 1)

            def ready(self, e, n):
                e.wait_ge(sem(self.n("lo")), upto(self.n("lo"), 2 * (n + 1)))

        w_in, w_out = io["w_in"][0], io["w_out"][0]
        w_kv, w_q, w_o = io["w_kv_mem"][0], io["w_q_mem"][0], io["w_o_mem"][0]
        w_gu, w_down = io["w_gu"][0], io["w_down"][0]

        A = Weights("wa", [(w_in[:, QB:QB + 512], 512), (w_in[:, KB:KB + 512], 512), (w_in[:, QIB:QIB + 512], 512),
                           (w_in[:, KIB:D_IN], D_IN - KIB), (w_in[:, VB:VB + 512], 512)]
                    + [([w_in[:, g * DC + f * P:g * DC + (f + 1) * P] for g in range(3)], 3 * P)
                       for f in range(NC_T)],
                    lambda n: ("s2_mm", NT * (n + 1)) if n < 4 else ("s4_mm", NT * (n - 3)))
        B = Weights("wb", [(w_out[:, c * 512:c * 512 + 512], 512) for c in range(2)]
                    + [(w_kv[:, c * 512:c * 512 + 512], 512) for c in range(4)]
                    + [(w_q[:, c * 512:c * 512 + 512], 512) for c in range(2)],
                    lambda n: ("l6_mm", NT * (n + 1)) if n < 2 else ("mkv_mm", 2 * (n - 1)) if n < 6 else ("q7_mm", NT * (n - 5)))
        C = Weights("wc", [(w_o[:, c * 512:c * 512 + 512], 512) for c in range(2)], None)

        def split_product(e, out, pairs, lhs_first=True):
            n = len(pairs)
            for k, (ah, al, bh, bl) in enumerate(pairs):
                e.matmul(out, ah, bh, start=(k == 0), stop=False)
                e.matmul(out, al, bh, start=False, stop=False)
                mm = e.matmul(out, ah, bl, start=False, stop=(k == n - 1))
            return mm

        class Norm:
            def __init__(self, name, tiles, src, hi, lo, ready):
                self.name, self.tiles, self.src, self.hi, self.lo, self.ready = name, tiles, src, hi, lo, ready

            def n(self, what):
                return f"{self.name}_{what}"

            def s(self, what):
                return sem(self.n(what))

            def bank(self, j):
                return 4 + 2 * (j % 2)

            def act_root(self, e, j):
                n = self.tiles[j]
                self.ready(e, j)
                b = self.bank(j)
                if j >= 2:
                    e.wait_ge(sem(self.n("lo")), upto(self.n("lo"), j - 1))
                e.activation(PS[0:n, b:b + 2, :].rearrange("p a b -> p (a b)"), self.src(j), ACT.Square,
                             accum_out=stat[0:n, j:j + 1]).then_inc(self.s("ss"), 1)
                e.wait_ge(sem(self.n("ss")), upto(self.n("ss"), j + 1))
                e.activation(stat[0:n, 16 + j:17 + j], stat[0:n, j:j + 1], ACT.Sqrt, bias=eps[0:n, :],
                             scale=1.0 / D).then_inc(self.s("rt"), 1)

            def dve_norm(self, e, j, out):
                n = self.tiles[j]
                e.wait_ge(sem(self.n("rt")), upto(self.n("rt"), j + 1))
                e.reciprocal(stat[0:n, 32 + j:33 + j], stat[0:n, 16 + j:17 + j]).then_inc(self.s("rc"), 1)
                e.wait_ge(sem(self.n("rc")), upto(self.n("rc"), j + 1))
                e.scalar_tensor_tensor(out(j), self.src(j), stat[0:n, 32 + j:33 + j], gb[0:n, :],
                                       ALU.mult, ALU.mult).then_inc(self.s("xn"), 1)

            def pe_turn(self, e, j, out):
                n = self.tiles[j]
                b = self.bank(j)
                e.wait_ge(sem(self.n("xn")), upto(self.n("xn"), j + 1))
                for k in range(KT):
                    t = e.transpose(PS[:, b + k // 4, (k % 4) * P:(k % 4) * P + n], out(j)[:, k * P:(k + 1) * P],
                                    ident[0:n, 0:n])
                t.then_inc(self.s("tp"), 1)

            def parts(self, j):
                n = self.tiles[j]
                b = self.bank(j)
                t = PS[:, b:b + 2, :].rearrange("p a (c q) -> p (a c) q", q=P)[:, :, 0:n]
                return t, self.hi[:, :, j * P:j * P + n], self.lo[:, :, j * P:j * P + n]

            def act_hi(self, e, j):
                e.wait_ge(sem(self.n("tp")), upto(self.n("tp"), j + 1))
                t, hi, lo = self.parts(j)
                e.activation(hi, t, ACT.Copy).then_inc(self.s("hi"), 1)

            def dve_lo(self, e, j):
                e.wait_ge(sem(self.n("hi")), upto(self.n("hi"), j + 1))
                t, hi, lo = self.parts(j)
                e.tensor_tensor(lo, t, hi, ALU.subtract).then_inc(self.s("lo"), 1)

        tiles = [rows(j) for j in range(NT)]
        N1 = Norm("n1", tiles, lambda j: h[0:rows(j), j, :], xa_hi, xa_lo,
                  lambda e, j: e.wait_ge(sem(f"x_ld{j // 3}"), upto(f"x_ld{j // 3}", 48)))

        block = ctx.enter_context(nc.Block())
        new_k = [io["o_kp"][0, 0].rearrange("t h d -> t (h d)"), io["o_ks"][0].rearrange("b t h d -> (b t) (h d)")]
        new_v = [io["o_vp"][0, 0].rearrange("t h d -> t (h d)"), io["o_vs"][0].rearrange("b t h d -> (b t) (h d)")]
        new_ki = [io["o_ikp"][0, 0], io["o_iks"][0].rearrange("b t d -> (b t) d")]
        xs = io["x_sample"].rearrange("b t d -> (b t) d")
        ys = io["o_ys"].rearrange("b t d -> (b t) d")

        def dram_rows(pair, j):
            return pair[0][j * P:(j + 1) * P, :] if j < NB else pair[1]

        ITEMS = [(c, j) for c in range(4) for j in range(NT)]
        NI = len(ITEMS)
        STORED = [k for k, (c, j) in enumerate(ITEMS) if c in (1, 3)]

        def stores_of_slot(k):
            return len([m for m in STORED if m % 3 == k % 3 and m < k])

        DOTS = [(i, hh) for i in range(2, NB) for hh in range(H)]
        ND = len(DOTS)
        L4 = [("v", j) for j in range(NT)] + [("c", f, t, g) for f in range(NC_T) for t in range(3) for g in range(3)]
        ATT = [(i, hh) for i in range(NB) for hh in range(H)]
        NA = len(ATT)

        B_OUT, B_KV, B_Q = 0, 2, 6

        L6 = [(c, j) for c in range(2) for j in range(NT)]
        N2 = Norm("n2", tiles, lambda j: h[0:rows(j), j, :], xb_hi, xb_lo, None)
        N3 = Norm("n3", tiles, lambda j: h[0:rows(j), j, :], xa_hi, xa_lo, None)
        NM = Norm("nm", [P, P], lambda j: memx[:, j, :], xm_hi, xm_lo,
                  lambda e, j: e.wait_ge(sem("memx_ld"), 32))
        xnorm = view("QI", 0, [2, D])
        mixst = view("XA", 26112, [DC], parts=18)
        ffnst = view("H", fbase + 45056, [DFF], parts=18)
        h3 = nc.dram_tensor("h3_scratch", [T, D], F32, kind="Internal").ap()
        CONSTS = 17

        def down_store(e, c):
            for j in range(NT):
                n = c * NT + j
                e.wait_ge(sem("down_ev"), n + 1)
                dstv = io["o_yp"][0, j * P:(j + 1) * P, c * 256:(c + 1) * 256] if j < NB else ys[:, c * 256:(c + 1) * 256]
                e.dma_start(dstv, outb[0:rows(j), n % 4, :]).then_inc(sem(f"y_st{n % 4}"), 16)

        @block.sync
        def _(e):
            def const(dst, src):
                e.dma_start(dst, src).then_inc(sem("const"), 16)
            const(gb[:, :], io["g_mix"].broadcast_to([P, D]))
            for j in range(NT):
                e.dma_start(h[0:rows(j), j, :], dram_rows([io["x_prompt"][0], xs], j)).then_inc(sem(f"x_ld{j // 3}"), 16)
                if j == 0:
                    const(ident[:, :], io["c_ident"])
            A.load(e, 0)
            const(mask01[:, :], io["c_mask"])
            const(smask[0:NS, :], io["c_smask"])
            const(cos_t[:, :, :], io["c_cos"].rearrange("(j p) d -> p j d", p=P))
            const(sin_t[:, :, :], io["c_sin"].rearrange("(j p) d -> p j d", p=P))
            const(qkg[:, 0, :], io["q_norm_g"].broadcast_to([P, HD]))
            const(qkg[:, 1, :], io["k_norm_g"].broadcast_to([P, HD]))
            const(mqkg[:, 0, :], io["mq_norm_g"].broadcast_to([P, MD]))
            const(mqkg[:, 1, :], io["mk_norm_g"].broadcast_to([P, MD]))
            const(st_mix[0:16, :], io["state_conv_mix"][0].rearrange("b t d -> (b t) d"))
            const(st_mix[16:19, :], io["conv_mix_w"][0])
            const(st_mix[19:20, :], io["conv_mix_w"][0, 0:1, :])
            const(st_ffn[0:16, :], io["state_conv_ffn"][0].rearrange("b t d -> (b t) d"))
            const(st_ffn[16:19, :], io["conv_ffn_w"][0])
            const(st_ffn[19:20, :], io["conv_ffn_b"])
            const(pts[:, :], io["page_table"].rearrange("a b -> (a b)")[None, :])
            A.load(e, 1)
            A.load(e, 2)

            def store_roped(c):
                for k in STORED:
                    if ITEMS[k][0] == c:
                        j = ITEMS[k][1]
                        n = rows(j)
                        e.wait_ge(sem("s2_roped"), k + 1)
                        if c == 1:
                            e.dma_start(dram_rows(new_k, j), roped[0:n, k % 3, :]).then_inc(sem(f"s2_st{k % 3}"), 16)
                        else:
                            e.dma_start(dram_rows(new_ki, j), roped[0:n, k % 3, 0:HD]).then_inc(sem(f"s2_st{k % 3}"), 16)

            A.load(e, 3)
            store_roped(1)
            A.load(e, 4)
            e.wait_ge(sem("const"), 16 * CONSTS)
            pages = [e.value_load(pts[0:1, n:n + 1], min_val=0, max_val=N_POOL - 1) for n in range(DEC_B * NPG)]
            A.load(e, 5)
            store_roped(3)
            e.wait_ge(sem("s2_tp"), NI)
            for k in range(3):
                e.wait_ge(sem(f"s2_st{k}"), upto(f"s2_st{k}", 16 * len([m for m in STORED if m % 3 == k])))
            for n, page in enumerate(pages):
                for twice in range(2):
                    e.dma_start(idx_raw[:, n, twice * HD:(twice + 1) * HD],
                                io["cache_idx_k"][0][bass.ds(page, 1)].rearrange("a p d -> (a p) d")
                                ).then_inc(sem("idx_ld"), 16)
            A.load(e, 6)
            for j in range(NT):
                e.wait_ge(sem("s4_ev"), j + 1)
                e.dma_start(dram_rows(new_v, j), V[0:rows(j), j, :]).then_inc(sem("v_st"), 16)
            A.load(e, 7)
            A.load(e, 8)
            for n, page in enumerate(pages):
                if n >= 2:
                    e.wait_ge(sem("kb_tp"), n - 1)
                else:
                    e.wait_ge(sem("conv_lo"), NC_T)
                e.dma_start(kpage[:, n % 2, :],
                            io["cache_k"][0][bass.ds(page, 1)].rearrange("a p h d -> (a p) (h d)")
                            ).then_inc(sem(f"kb_ld{n % 2}"), 16)
            e.wait_ge(sem("mixst_ev"), 1)
            e.dma_start(io["o_cmp"][0, 0], mixst[16:18, :]).then_inc(sem("st_out"), 16)
            e.dma_start(io["o_cms"][0].rearrange("b t d -> (b t) d"), mixst[0:16, :]).then_inc(sem("st_out"), 16)
            e.wait_ge(sem("at_tt"), NA)
            for b in range(DEC_B):
                e.dma_start(v_new[0:DEC_T, b, :], V[b * DEC_T:(b + 1) * DEC_T, NB, :]).then_inc(sem("vn_ld"), 16)
            for n, page in enumerate(pages):
                if n >= 2:
                    e.wait_ge(sem("sv_used"), n // 2)
                e.dma_start(vpage[:, n % 2, :],
                            io["cache_v"][0][bass.ds(page, 1)].rearrange("a p h d -> (a p) (h d)")
                            ).then_inc(sem(f"vb_ld{n % 2}"), 16)
            e.wait_ge(sem("sa_lo"), 1)
            e.wait_ge(sem("v_st"), 16 * NT)
            e.wait_ge(sem("sv_used"), DEC_B)
            e.dma_start(gb[:, :], io["g_mem"].broadcast_to([P, D])).then_inc(sem("g_ld"), 16)
            B.load(e, 0)
            for j in range(NT):
                e.dma_start(h[0:rows(j), j, :], dram_rows([io["x_prompt"][0], xs], j)).then_inc(sem("x2_ld"), 16)
            B.load(e, 1)
            B.load(e, 2)
            e.wait_ge(sem("l6_mm"), 2 * NT)
            e.wait_ge(sem("st_out"), 32)
            for j in range(2):
                e.dma_start(memx[:, j, :], io["mem_prompt"][0, j * P:(j + 1) * P, :]).then_inc(sem("memx_ld"), 16)
            e.wait_ge(sem("n2_xn"), upto("n2_xn", NT))
            e.dma_start(gb[:, :], io["g_mem_src"].broadcast_to([P, D])).then_inc(sem("g_ld"), 16)
            B.load(e, 3)
            for n in range(4, 8):
                for j in range(2):
                    it = (n - 4) * 2 + j
                    c = n - 4
                    if c < 2:
                        e.wait_ge(sem("mk_out"), upto("mk_out", it + 1))
                    else:
                        e.wait_ge(sem("mkv_ev"), it + 1)
                    if c < 2:
                        e.dma_start(io["o_mk"][0, 0, j * P:(j + 1) * P].rearrange("t h d -> t (h d)")[:, c * 512:(c + 1) * 512],
                                    mraw[:, it, :]).then_inc(sem("mk_st"), 16)
                    else:
                        e.dma_start(io["o_mv"][0, 0, j * P:(j + 1) * P].rearrange("t h d -> t (h d)")[:, (c - 2) * 512:(c - 1) * 512],
                                    mv[:, j, (c - 2) * 512:(c - 1) * 512]).then_inc(sem("mv_st"), 16)
                if n == 4:
                    B.load(e, 4)
                    B.load(e, 5)
                if n == 5:
                    B.load(e, 6)
                if n == 6:
                    B.load(e, 7)
            e.wait_ge(sem("q7_mm"), upto("q7_mm", 2 * NT))
            e.dma_start(gb[:, :], io["g_ffn"].broadcast_to([P, D])).then_inc(sem("g_ld"), 16)
            for hh in range(MH):
                for b in range(DEC_B):
                    n = hh * DEC_B + b
                    if n >= 2:
                        e.wait_ge(sem("mkb_tp"), upto("mkb_tp", n - 1))
                    e.dma_start(mkpage[:, n % 2, :, :],
                                io["cache_mem_k"][0, b, :, hh, :].rearrange("(c p) d -> p c d", p=P)
                                ).then_inc(sem(f"mkb_ld{n % 2}"), 16)
                for b in range(DEC_B):
                    n = hh * DEC_B + b
                    if n >= 2:
                        e.wait_ge(sem("mvb_used"), upto("mvb_used", n - 1))
                    e.dma_start(mvpage[:, n % 2, :, :],
                                io["cache_mem_v"][0, b, :, hh, :].rearrange("(c p) d -> p c d", p=P)
                                ).then_inc(sem(f"mvb_ld{n % 2}"), 16)
            e.wait_ge(sem("mvb_used"), upto("mvb_used", MH * DEC_B))
            e.wait_ge(sem("sm_lo"), 1)
            C.load(e, 0)
            C.load(e, 1)
            for j in range(NT):
                e.wait_ge(sem("l8_ev"), upto("l8_ev", NT + j + 1))
                e.dma_start(h3[j * P:j * P + rows(j), :], h[0:rows(j), j, :]).then_inc(sem("h3_st"), 16)
            e.wait_ge(sem("h3_st"), 16 * NT)
            e.wait_ge(sem("n3_lo"), upto("n3_lo", NT))
            for f in range(FT):
                for g in range(2):
                    n = 2 * f + g
                    if n >= 2:
                        e.wait_ge(sem("fw_lo"), n - 1)
                    e.dma_start(fst[:, g, :, :],
                                w_gu[:, g * DFF + f * P:g * DFF + (f + 1) * P].rearrange("(k p) n -> p k n", p=P)
                                ).then_inc(sem(f"fw_ld{g}"), 16)
            e.wait_ge(sem("gu_mm"), 2 * FT)
            for c in range(4):
                for half in range(2):
                    n = 2 * c + half
                    if n >= 2:
                        e.wait_ge(sem("dw_lo"), upto("dw_lo", n - 1))
                    e.dma_start(dst[:, half, :, :],
                                w_down[half * 11 * P:(half + 1) * 11 * P, c * 256:(c + 1) * 256]
                                .rearrange("(k p) n -> p k n", p=P)).then_inc(sem(f"dw_ld{half}"), 16)
                if c == 0:
                    continue
                down_store(e, c - 1)
            down_store(e, 3)
            e.wait_ge(sem("ffnst_ev"), upto("ffnst_ev", 1))
            e.dma_start(io["o_cfp"][0, 0], ffnst[16:18, :]).then_inc(sem("st_out"), 16)
            e.dma_start(io["o_cfs"][0].rearrange("b t d -> (b t) d"), ffnst[0:16, :]).then_inc(sem("st_out"), 16)
            e.wait_ge(sem("st_out"), 64)
            for k in range(4):
                e.wait_ge(sem(f"y_st{k}"), upto(f"y_st{k}", 16 * 9))
            for k in range(3):
                e.wait_ge(sem(f"s2_st{k}"), upto(f"s2_st{k}", 16 * len([m for m in STORED if m % 3 == k])))
            e.wait_ge(sem("mk_st"), upto("mk_st", 64))
            e.wait_ge(sem("mv_st"), 64)
            e.wait_ge(sem("v_st"), 16 * NT)

        def chain(e, ins, name, count):
            ins.then_inc(sem(name), 1)
            count[0] += 1
            e.wait_ge(sem(name), upto(name, count[0]))

        def lin(e, out, x_hi, x_lo, wh, wl, ks, cols):
            n = len(ks)
            for q, k in enumerate(ks):
                e.matmul(out, x_hi(k)[:, cols], wh[:, q, :], start=(q == 0), stop=False)
                e.matmul(out, x_lo(k)[:, cols], wh[:, q, :], start=False, stop=False)
                mm = e.matmul(out, x_hi(k)[:, cols], wl[:, q, :], start=False, stop=(q == n - 1))
            return mm

        def tcols(j):
            return slice(j * P, j * P + rows(j))

        @block.tensor
        def _(e):
            e.wait_ge(sem("const"), 16 * CONSTS)
            for f in range(NC_T):
                e.transpose(PS[:, 0, f * 20:f * 20 + 20], st_mix[:, f * P:(f + 1) * P], ident[0:20, 0:20])
            for f in range(FT):
                t = e.transpose(PS[:, 1, f * 20:f * 20 + 20], st_ffn[:, f * P:(f + 1) * P], ident[0:20, 0:20])
            t.then_inc(sem("st_tp"), 1)
            for j in range(NT + 2):
                if j >= 2:
                    N1.pe_turn(e, j - 2, lambda j: h[0:rows(j), j, :])

            def turn_item(L):
                c, j = ITEMS[L]
                n = rows(j)
                e.wait_ge(sem("s2_roped"), L + 1)
                if L >= 2:
                    e.wait_ge(sem("s2_te"), L - 1)
                if L == 0:
                    e.wait_ge(sem("n1_lo"), NT)
                for p in range(4 if c < 3 else 1):
                    t = e.transpose(PS[:, 4 + L % 2, p * P:p * P + n], roped[0:n, L % 3, p * P:(p + 1) * P],
                                    ident[0:n, 0:n])
                t.then_inc(sem("s2_tp"), 1)

            e.wait_ge(sem("st_ev"), 2)
            for L in range(NI + 2):
                if L < NI:
                    c, j = ITEMS[L]
                    if j == 0:
                        A.ready(e, c)
                    if c == 0:
                        e.wait_ge(sem("n1_lo"), j + 1)
                    if L >= 4:
                        e.wait_ge(sem("s2_raw"), L - 3)
                    w = A.chunks[c][1]
                    mm = lin(e, PS[0:rows(j), L % 4, 0:w], lambda k: xa_hi[:, k, :], lambda k: xa_lo[:, k, :],
                             w_hi[c % 2][:, :, 0:w], w_lo[c % 2][:, :, 0:w], range(KT), tcols(j))
                    mm.then_inc(sem("s2_mm"), 1)
                if L >= 2:
                    turn_item(L - 2)

            e.wait_ge(sem("s2_raw"), NI)
            e.wait_ge(sem("s2_te"), NI)
            for m, (i, hh) in enumerate(DOTS):
                if m >= 2:
                    e.wait_ge(sem("s3_relu"), m - 1)
                r = slice((hh % 2) * HD, (hh % 2 + 1) * HD)
                n = (i + 1) * P
                for a in range(0, n, 512):
                    b = min(n, a + 512)
                    mm = e.matmul(PS[:, 2 * (m % 2) + a // 512, 0:b - a], qiT[r, hh // 2, i * P:(i + 1) * P],
                                  kiT[r, a:b], start=True, stop=True)
                mm.then_inc(sem("s3_mm"), 1)
            e.wait_ge(sem("idx_ld"), 16 * 2 * DEC_B * NPG)
            for n in range(DEC_B * NPG):
                t = e.transpose(PS[:, 4 + n // 4, (n % 4) * P:(n % 4 + 1) * P], idx_raw[:, n, :], ident[:, :])
            t.then_inc(sem("ik_tp"), 1)
            e.wait_ge(sem("ik_ev"), 2)
            e.wait_ge(sem("qmi"), 5)
            for hh in range(H):
                m = ND + hh
                e.wait_ge(sem("s3_relu"), m - 1)
                r = slice((hh % 2) * HD, (hh % 2 + 1) * HD)
                for b in range(DEC_B):
                    a = (hh // 2) * 512 + b * NS
                    mm = e.matmul(PS[0:NS, 2 * (m % 2), 0:S_KEYS], qm_i[r, a:a + NS], kiTb[r, b, :],
                                  start=(b == 0), stop=(b == DEC_B - 1))
                mm.then_inc(sem("s3_mm"), 1)

            e.wait_ge(sem("s3_relu"), ND + H)
            for x, item in enumerate(L4):
                if x >= 8:
                    e.wait_ge(sem("s4_ev"), x - 7)
                if item[0] == "v":
                    j = item[1]
                    if j == 0:
                        A.ready(e, 4)
                    mm = lin(e, PS[0:rows(j), x % 8, :], lambda k: xa_hi[:, k, :], lambda k: xa_lo[:, k, :],
                             w_hi[0], w_lo[0], range(KT), tcols(j))
                    last = j == NT - 1
                else:
                    _, f, t, g = item
                    c = 5 + f
                    if t == 0 and g == 0:
                        A.ready(e, c)
                    t0, tn = token_chunks()[t]
                    for k in range(KT):
                        wh, wl = (w[c % 2][:, k, g * P:(g + 1) * P] for w in (w_hi, w_lo))
                        xh, xl = xa_hi[:, k, t0:t0 + tn], xa_lo[:, k, t0:t0 + tn]
                        out = PS[:, x % 8, 0:tn]
                        e.matmul(out, wh, xh, start=(k == 0), stop=False)
                        e.matmul(out, wh, xl, start=False, stop=False)
                        mm = e.matmul(out, wl, xh, start=False, stop=(k == KT - 1))
                    last = t == 2 and g == 2
                mm.then_inc(sem("s4_mm"), 1)
            e.wait_ge(sem("s4_ev"), len(L4))
            for n in range(DEC_B * NPG):
                e.wait_ge(sem(f"kb_ld{n % 2}"), upto(f"kb_ld{n % 2}", 16 * (n // 2 + 1)))
                if n >= 2:
                    e.wait_ge(sem("kb_ev"), n - 1)
                for p in range(4):
                    t = e.transpose(PS[:, 6 + n % 2, p * P:(p + 1) * P], kpage[:, n % 2, p * P:(p + 1) * P], ident[:, :])
                t.then_inc(sem("kb_tp"), 1)
            e.wait_ge(sem("conv_lo"), NC_T)
            for f in range(NC_T):
                t = e.transpose(PS[0:18, 0, f * P:(f + 1) * P], u_state[:, f, :], ident[:, :])
            t.then_inc(sem("mixst_tp"), 1)
            e.wait_ge(sem("mixst_ev"), 1)
            e.wait_ge(sem("kb_ev"), DEC_B * NPG)

            def scores(m):
                i, hh = ATT[m]
                if m >= 2:
                    e.wait_ge(sem("at_max"), m - 1)
                r = slice((hh % 2) * HD, (hh % 2 + 1) * HD)
                n = (i + 1) * P
                for a in range(0, n, 512):
                    b = min(n, a + 512)
                    mm = e.matmul(PS[:, 2 * (m % 2) + a // 512, 0:b - a], qT[r, hh // 2, i * P:(i + 1) * P],
                                  kT[r, hh // 2, a:b], start=True, stop=True)
                mm.then_inc(sem("at_qk"), 1)

            def turn_probs(m):
                i, hh = ATT[m]
                e.wait_ge(sem("at_p"), m + 1)
                if m >= 1:
                    e.wait_ge(sem("at_pte"), m)
                for c in range(i + 1):
                    t = e.transpose(PS[:, 4 + c // 4, (c % 4) * P:(c % 4 + 1) * P], logit[:, m % 2, c * P:(c + 1) * P],
                                    ident[:, :])
                t.then_inc(sem("at_tt"), 1)

            def values(m):
                i, hh = ATT[m]
                e.wait_ge(sem("at_pte"), m + 1)
                if hh == 0 and i >= 2:
                    e.wait_ge(sem("at_lo"), i - 1)
                r = slice((hh % 2) * HD, (hh % 2 + 1) * HD)
                for c in range(i + 1):
                    mm = e.matmul(PS[r, 6 + i % 2, (hh // 2) * P:(hh // 2 + 1) * P], V[:, c, hh * HD:(hh + 1) * HD],
                                  pT[:, m % 2, c, :], start=(c == 0), stop=(c == i))
                mm.then_inc(sem("at_pv"), 1)

            for m in range(NA + 2):
                if m < NA:
                    scores(m)
                if 1 <= m <= NA:
                    turn_probs(m - 1)
                if m >= 2:
                    values(m - 2)

            e.wait_ge(sem("at_max"), NA)
            e.wait_ge(sem("at_lo"), NB)
            e.wait_ge(sem("qma"), 9)
            for hh in range(H):
                if hh >= 2:
                    e.wait_ge(sem("sa_max"), hh - 1)
                r = slice((hh % 2) * HD, (hh % 2 + 1) * HD)
                for b in range(DEC_B):
                    a = (hh // 2) * 512 + b * NS
                    mm = e.matmul(PS[0:NS, hh % 2, 0:S_KEYS], qm_a[r, a:a + NS],
                                  kTb[r, hh // 2, b * S_KEYS:(b + 1) * S_KEYS], start=(b == 0), stop=(b == DEC_B - 1))
                mm.then_inc(sem("sa_qk"), 1)
            e.wait_ge(sem("sa_p"), 1)
            for hh in range(H):
                for c in range(3):
                    w = min(P, S_KEYS - c * P)
                    a = (hh % 2) * 3 * NS + c * NS
                    t = e.transpose(PS[0:w, 2 + hh // 2, a:a + NS], p_s[:, hh, c * P:c * P + w], ident[0:NS, 0:NS])
            t.then_inc(sem("sa_tt"), 1)
            e.wait_ge(sem("sa_pte"), 2)
            e.wait_ge(sem("vn_ld"), 16 * DEC_B)
            for b in range(DEC_B):
                for s in range(2):
                    e.wait_ge(sem(f"vb_ld{s}"), upto(f"vb_ld{s}", 16 * (b + 1)))
                for hh in range(H):
                    r = slice((hh % 2) * HD, (hh % 2 + 1) * HD)
                    out = PS[r, 6, (hh // 2) * NS + b * DEC_T:(hh // 2) * NS + (b + 1) * DEC_T]
                    d = slice(hh * HD, (hh + 1) * HD)
                    q = slice(b * DEC_T, (b + 1) * DEC_T)
                    e.matmul(out, vpage[:, 0, d], pT_s[:, hh, 0, q], start=True, stop=False)
                    e.matmul(out, vpage[:, 1, d], pT_s[:, hh, 1, q], start=False, stop=False)
                    mm = e.matmul(out, v_new[0:DEC_T, b, d], pT_s[0:DEC_T, hh, 2, q], start=False, stop=True)
                mm.then_inc(sem("sv_used"), 1)

            e.wait_ge(sem("sa_lo"), 1)
            for L in range(len(L6) + 2):
                if L < len(L6):
                    c, j = L6[L]
                    if j == 0:
                        B.ready(e, B_OUT + c)
                    if L >= 4:
                        e.wait_ge(sem("l6_ev"), L - 3)
                    mm = lin(e, PS[0:rows(j), L % 4, :], lambda k: ct_hi[:, k, :] if k < 4 else xa_hi[:, k - 4, :],
                             lambda k: ct_lo[:, k, :] if k < 4 else xa_lo[:, k - 4, :],
                             w_hi[c], w_lo[c], range(KT), tcols(j))
                    mm.then_inc(sem("l6_mm"), 1)
                if L >= NT + 2:
                    N2.pe_turn(e, L - NT - 2, lambda j: xnorm[0:rows(j), j % 2, :])

            for j in range(2):
                NM.pe_turn(e, j, lambda j: memx[:, j, :])
            e.wait_ge(sem("l6_ev"), len(L6))
            for it in range(8):
                c, j = it // 2, it % 2
                if j == 0:
                    B.ready(e, B_KV + c)
                if it == 0:
                    e.wait_ge(sem("nm_lo"), upto("nm_lo", 2))
                if it >= 4:
                    e.wait_ge(sem("mkv_ev"), it - 3)
                mm = lin(e, PS[:, it % 4, :], lambda k: xm_hi[:, k, :], lambda k: xm_lo[:, k, :],
                         w_hi[c % 2], w_lo[c % 2], range(KT), tcols(j))
                mm.then_inc(sem("mkv_mm"), 1)
                if it in (4, 5, 6, 7):
                    q = it - 4
                    c, j = q // 2, q % 2
                    e.wait_ge(sem("mk_out"), upto("mk_out", q + 1))
                    if q >= 2:
                        e.wait_ge(sem("mk_te"), upto("mk_te", q - 1))
                    for p in range(4):
                        t = e.transpose(PS[:, 4 + q % 2, p * P:(p + 1) * P], mraw[:, q, p * P:(p + 1) * P], ident[:, :])
                    t.then_inc(sem("mk_tp"), 1)
            e.wait_ge(sem("mkv_ev"), 8)
            e.wait_ge(sem("mk_te"), upto("mk_te", 4))
            for L in range(len(L6) + 2):
                if L < len(L6):
                    c, j = L6[L]
                    if j == 0:
                        B.ready(e, B_Q + c)
                    if L >= 4:
                        e.wait_ge(sem("q7_raw"), upto("q7_raw", L - 3))
                    mm = lin(e, PS[0:rows(j), L % 4, :], lambda k: xb_hi[:, k, :], lambda k: xb_lo[:, k, :],
                             w_hi[c], w_lo[c], range(KT), tcols(j))
                    mm.then_inc(sem("q7_mm"), 1)
                if L >= 2:
                    q = L - 2
                    n = rows(L6[q][1])
                    e.wait_ge(sem("q7_n"), upto("q7_n", q + 1))
                    if q >= 2:
                        e.wait_ge(sem("q7_te"), upto("q7_te", q - 1))
                    for p in range(4):
                        t = e.transpose(PS[:, 4 + q % 2, p * P:p * P + n], qraw[0:n, q % 3, p * P:(p + 1) * P],
                                        ident[0:n, 0:n])
                    t.then_inc(sem("q7_tp"), 1)
            e.wait_ge(sem("q7_raw"), upto("q7_raw", len(L6)))
            e.wait_ge(sem("q7_te"), upto("q7_te", len(L6)))
            for j in range(NB + 2):
                if j < NB:
                    if j >= 2:
                        e.wait_ge(sem("ma_exp"), upto("ma_exp", j - 1))
                    for hh in range(MH):
                        out = PS[:, 2 * (j % 2) + hh // 2, (hh % 2) * NMEM:(hh % 2 + 1) * NMEM]
                        e.matmul(out, mqT[:, 2 * hh, tcols(j)], mkT[:, 2 * hh, :], start=True, stop=False)
                        mm = e.matmul(out, mqT[:, 2 * hh + 1, tcols(j)], mkT[:, 2 * hh + 1, :], start=False, stop=True)
                    mm.then_inc(sem("ma_qk"), 1)
                if 1 <= j <= NB:
                    q = j - 1
                    e.wait_ge(sem("ma_p"), upto("ma_p", q + 1))
                    if q >= 1:
                        e.wait_ge(sem("ma_pte"), upto("ma_pte", q))
                    for c in range(8):
                        t = e.transpose(PS[:, 4 + c // 4, (c % 4) * P:(c % 4 + 1) * P],
                                        mlog[:, q % 2, c * P:(c + 1) * P], ident[:, :])
                    t.then_inc(sem("ma_tt"), 1)
                if j >= 2:
                    q = j - 2
                    e.wait_ge(sem("ma_pte"), upto("ma_pte", q + 1))
                    if q >= 1:
                        e.wait_ge(sem("ma_lo"), upto("ma_lo", q))
                    for c in range(8):
                        hh = c // 2
                        out = PS[:, 6 + c // 4, (c % 4) * P:(c % 4 + 1) * P]
                        e.matmul(out, mv[:, 0, c * P:(c + 1) * P], mpT[:, q % 2, 2 * hh, :], start=True, stop=False)
                        mm = e.matmul(out, mv[:, 1, c * P:(c + 1) * P], mpT[:, q % 2, 2 * hh + 1, :], start=False, stop=True)
                    mm.then_inc(sem("ma_pv"), 1)
            e.wait_ge(sem("ma_lo"), upto("ma_lo", NB))
            for hh in range(MH):
                for b in range(DEC_B):
                    n = hh * DEC_B + b
                    e.wait_ge(sem(f"mkb_ld{n % 2}"), upto(f"mkb_ld{n % 2}", 16 * (n // 2 + 1)))
                    if n >= 2:
                        e.wait_ge(sem("mkb_ev"), upto("mkb_ev", n - 1))
                    for kk in range(2):
                        for c in range(2):
                            t = e.transpose(PS[:, 4 + n % 2, kk * 256 + c * P:kk * 256 + (c + 1) * P],
                                            mkpage[:, n % 2, c, kk * P:(kk + 1) * P], ident[:, :])
                    t.then_inc(sem("mkb_tp"), 1)
                e.wait_ge(sem("mkb_ev"), upto("mkb_ev", (hh + 1) * DEC_B))
                e.wait_ge(sem("qmm"), hh + 1)
                for b in range(DEC_B):
                    for kk in range(2):
                        mm = e.matmul(PS[0:NS, hh % 2, 0:NMEM], qm_m[:, kk * 512 + b * NS:kk * 512 + (b + 1) * NS],
                                      mKT[:, hh % 2, kk, b * NMEM:(b + 1) * NMEM],
                                      start=(b == 0 and kk == 0), stop=(b == DEC_B - 1 and kk == 1))
                mm.then_inc(sem("ms_qk"), 1)
                e.wait_ge(sem("ms_p"), hh + 1)
                for c in range(2):
                    t = e.transpose(PS[:, 2, c * NS:(c + 1) * NS], mp_s[:, c * P:(c + 1) * P], ident[0:NS, 0:NS])
                t.then_inc(sem("ms_tt"), 1)
                e.wait_ge(sem("ms_pte"), hh + 1)
                for b in range(DEC_B):
                    n = hh * DEC_B + b
                    e.wait_ge(sem(f"mvb_ld{n % 2}"), upto(f"mvb_ld{n % 2}", 16 * (n // 2 + 1)))
                    for dd in range(2):
                        out = PS[:, 3, (hh * 2 + dd) * NS + b * DEC_T:(hh * 2 + dd) * NS + (b + 1) * DEC_T]
                        for mc in range(2):
                            mm = e.matmul(out, mvpage[:, n % 2, mc, dd * P:(dd + 1) * P],
                                          mpT_s[:, hh, mc * NS + b * DEC_T:mc * NS + (b + 1) * DEC_T],
                                          start=(mc == 0), stop=(mc == 1))
                    mm.then_inc(sem("mvb_used"), 1)
            e.wait_ge(sem("sm_lo"), 1)
            for L in range(len(L6) + 2):
                if L < len(L6):
                    c, j = L6[L]
                    if j == 0:
                        C.ready(e, c)
                    if L >= 4:
                        e.wait_ge(sem("l8_ev"), upto("l8_ev", L - 3))
                    mm = lin(e, PS[0:rows(j), L % 4, :], lambda k: xb_hi[:, k, :], lambda k: xb_lo[:, k, :],
                             w_hi[c], w_lo[c], range(KT), tcols(j))
                    mm.then_inc(sem("l8_mm"), 1)
                if L >= NT + 2:
                    N3.pe_turn(e, L - NT - 2, lambda j: xnorm[0:rows(j), j % 2, :])

            e.wait_ge(sem("n3_lo"), upto("n3_lo", NT))
            e.wait_ge(sem("l8_ev"), upto("l8_ev", len(L6)))
            for f in range(FT):
                for g in range(2):
                    n = 2 * f + g
                    e.wait_ge(sem("fw_lo"), n + 1)
                    if f >= 1:
                        e.wait_ge(sem("f_gate" if g == 0 else "f_mul"), upto("f_gate" if g == 0 else "f_mul", f))
                    for t, (t0, tn) in enumerate(token_chunks()):
                        out = PS[:, 3 * g + t, 0:tn]
                        for k in range(KT):
                            wh, wl = (w[:, f % 2, g, k * P:(k + 1) * P] for w in (fw_hi, fw_lo))
                            e.matmul(out, wh, xa_hi[:, k, t0:t0 + tn], start=(k == 0), stop=False)
                            e.matmul(out, wh, xa_lo[:, k, t0:t0 + tn], start=False, stop=False)
                            mm = e.matmul(out, wl, xa_hi[:, k, t0:t0 + tn], start=False, stop=(k == KT - 1))
                    mm.then_inc(sem("gu_mm"), 1)
            e.wait_ge(sem("f_mul"), FT)
            e.wait_ge(sem("f_st"), FT)
            for f in range(FT):
                t = e.transpose(PS[0:18, f // 4, (f % 4) * P:(f % 4 + 1) * P], g_state[:, f, :], ident[:, :])
            t.then_inc(sem("ffnst_tp"), 1)
            e.wait_ge(sem("ffnst_ev"), upto("ffnst_ev", 1))
            e.wait_ge(sem("f_lo"), FT)
            for c in range(4):
                e.wait_ge(sem("dw_lo"), upto("dw_lo", 2 * c + 2))
                for j in range(NT):
                    n = c * NT + j
                    if n >= 4:
                        e.wait_ge(sem("down_ev"), n - 3)
                    mm = lin(e, PS[0:rows(j), n % 4, 0:256], lambda k: ffn_hi[:, k, :], lambda k: ffn_lo[:, k, :],
                             dw_hi[:, c % 2, :].rearrange("p (k n) -> p k n", n=256),
                             dw_lo[:, c % 2, :].rearrange("p (k n) -> p k n", n=256), range(FT), tcols(j))
                    mm.then_inc(sem("down_mm"), 1)

        @block.scalar
        def _(e):
            def copy(out, in_, name, **kw):
                e.activation(out, in_, ACT.Copy, **kw).then_inc(sem(name), 1)

            e.wait_ge(sem("const"), 16 * CONSTS)
            e.wait_ge(sem("eps"), 1)
            A.split_hi(e, 0)
            e.wait_ge(sem("st_tp"), 1)
            copy(mix_sw[:, :, :].rearrange("p a b -> p (a b)"), PS[:, 0, 0:NC_T * 20], "st_ev")
            copy(ffn_sw[:, :, :].rearrange("p a b -> p (a b)"), PS[:, 1, 0:FT * 20], "st_ev")
            for j in range(NT + 2):
                if j >= 2:
                    N1.act_hi(e, j - 2)
                if j < NT:
                    N1.act_root(e, j)
            for L in range(NI + 2):
                if L < NI:
                    c, j = ITEMS[L]
                    n, w = rows(j), A.chunks[c][1]
                    e.wait_ge(sem("s2_mm"), L + 1)
                    if L >= 3:
                        e.wait_ge(sem("s2_roped"), L - 2)
                    copy(raw[0:n, L % 3, 0:w], PS[0:n, L % 4, 0:w], "s2_raw")
                    if j == 0:
                        A.split_hi(e, c + 1)
                if L >= 2:
                    q = L - 2
                    c, j = ITEMS[q]
                    n = rows(j)
                    e.wait_ge(sem("s2_tp"), q + 1)
                    if c < 3:
                        copy((qT, kT, qiT)[c][:, :, tcols(j)],
                             PS[:, 4 + q % 2, :].rearrange("p (a b) -> p a b", b=P)[:, :, 0:n], "s2_te")
                    else:
                        copy(kiT[:, tcols(j)], PS[:, 4 + q % 2, 0:n], "s2_te")
                if L < NI and ITEMS[L][0] < 2:
                    n = rows(ITEMS[L][1])
                    e.wait_ge(sem("s2_ss"), L + 1)
                    e.activation(stat[0:n, 72:80], stat[0:n, 64:72], ACT.Sqrt, bias=eps[0:n, :],
                                 scale=1.0 / HD).then_inc(sem("s2_rt"), 1)
            for m in range(ND + H):
                if m == ND:
                    e.wait_ge(sem("ik_tp"), 1)
                    e.wait_ge(sem("s2_te"), NI)
                    copy(kiTb[:, :, 0:PAST], PS[:, 4:8, :].rearrange("p a (b c) -> p (a b) c", c=PAST), "ik_ev")
                    copy(kiTb[:, :, PAST:S_KEYS], kiT[:, SEQ:T].rearrange("p (b c) -> p b c", c=DEC_T), "ik_ev")
                e.wait_ge(sem("s3_mm"), m + 1)
                if m >= 2:
                    e.wait_ge(sem("s3_acc"), m - 1)
                if m < ND:
                    n = (DOTS[m][0] + 1) * P
                    src = PS[:, 2 * (m % 2):2 * (m % 2) + 2, :].rearrange("p a b -> p (a b)")[:, 0:n]
                    out = relu[:, m % 2, 0:n]
                else:
                    src, out = PS[0:NS, 2 * (m % 2), 0:S_KEYS], relu[0:NS, m % 2, 0:S_KEYS]
                e.activation(out, src, ACT.Relu).then_inc(sem("s3_relu"), 1)
            for x, item in enumerate(L4):
                if item[0] == "v":
                    j = item[1]
                    e.wait_ge(sem("s4_mm"), x + 1)
                    copy(V[0:rows(j), j, :], PS[0:rows(j), x % 8, :], "s4_ev")
                    if j == 0:
                        A.split_hi(e, 5)
                    continue
                _, f, t, g = item
                t0, tn = token_chunks()[t]
                if t == 0 and g == 0:
                    if f >= 1:
                        e.wait_ge(sem("conv_lo"), f)
                e.wait_ge(sem("s4_mm"), x + 1)
                copy((cb_s, cc_s, ch_s)[g][:, t0:t0 + tn], PS[:, x % 8, 0:tn], "s4_ev")
                if t == 0 and g == 0:
                    A.split_hi(e, 6 + f)
                if t == 2 and g == 2:
                    e.wait_ge(sem("conv_u"), f + 1)
                    for tap, out in enumerate((cc_s, ch_s, tap2)):
                        copy(out[:, 0:CW], u_s[:, tap:tap + CW], "conv_t", scale=mix_sw[:, f, 16 + tap:17 + tap])
                    e.wait_ge(sem("conv_y"), f + 1)
                    e.wait_ge(sem("s3_acc"), ND + H)
                    copy(ct_hi[:, f, :], ch_s[:, 0:T], "conv_hi")
            for n in range(DEC_B * NPG):
                b, pg = n // NPG, n % NPG
                e.wait_ge(sem("kb_tp"), n + 1)
                copy(kTb[:, :, b * S_KEYS + pg * PAGE:b * S_KEYS + (pg + 1) * PAGE],
                     PS[:, 6 + n % 2, :].rearrange("p (a b) -> p a b", b=P), "kb_ev")
            e.wait_ge(sem("mixst_tp"), 1)
            copy(mixst[:, :], PS[0:18, 0, :], "mixst_ev")
            for m in range(NA + 3):
                if m < NA:
                    i, hh = ATT[m]
                    n = (i + 1) * P
                    e.wait_ge(sem("at_nm"), m + 1)
                    e.activation(logit[:, m % 2, 0:n], logit[:, m % 2, 0:n], ACT.Exp, bias=att_st[:, m % 2, 1:2],
                                 scale=ATT_SCALE, accum_out=att_st[:, m % 2, 2:3]).then_inc(sem("at_exp"), 1)
                if 1 <= m <= NA:
                    q = m - 1
                    i = ATT[q][0]
                    e.wait_ge(sem("at_tt"), q + 1)
                    if q >= 2:
                        e.wait_ge(sem("at_pv"), q - 1)
                    copy(pT[:, q % 2, 0:i + 1, :],
                         PS[:, 4:6, :].rearrange("p a (c q) -> p (a c) q", q=P)[:, 0:i + 1, :], "at_pte")
                if m >= 3 and m - 3 < NA and ATT[m - 3][1] == H - 1:
                    i = ATT[m - 3][0]
                    e.wait_ge(sem("at_pv"), m - 2)
                    copy(xa_hi[:, 0:4, tcols(i)], PS[:, 6 + i % 2, :].rearrange("p (a b) -> p a b", b=P), "at_hi")
            for hh in range(H):
                if hh == 0:
                    e.wait_ge(sem("sa_nm"), 1)
                e.activation(p_s[:, hh, :], p_s[:, hh, :], ACT.Exp, bias=sat_st[:, 1, hh:hh + 1], scale=ATT_SCALE,
                             accum_out=sat_st[:, 2, hh:hh + 1]).then_inc(sem("sa_exp"), 1)
            e.wait_ge(sem("sa_tt"), 1)
            src = PS[:, 2:6, 0:6 * NS].rearrange("p a (b c q) -> p a b c q", b=2, c=3)
            for hh2 in range(2):
                e.activation(pT_s[:, hh2:H:2, 0:2, :], src[:, :, hh2, 0:2, :], ACT.Copy).then_inc(sem("sa_ptx"), 1)
                e.activation(pT_s[0:DEC_T, hh2:H:2, 2, :], src[0:DEC_T, :, hh2, 2, :], ACT.Copy).then_inc(sem("sa_pte"), 1)
            e.wait_ge(sem("sv_used"), DEC_B)
            copy(xa_hi[:, 0:4, SEQ:T], PS[:, 6, 0:4 * NS].rearrange("p (a b) -> p a b", b=NS), "sa_hi")
            B.split_hi(e, 0)
            B.split_hi(e, 1)
            B.split_hi(e, 2)
            N2.ready = lambda e, j: e.wait_ge(sem("l6_ev"), NT + j + 1)
            for j in range(NT + 2):
                if j >= 2:
                    N2.act_hi(e, j - 2)
                if j < NT:
                    N2.act_root(e, j)
            B.split_hi(e, 3)
            e.wait_ge(sem("n2_lo"), upto("n2_lo", NT))
            for j in range(2):
                NM.act_root(e, j)
            for j in range(2):
                NM.act_hi(e, j)

            for it in range(8):
                c, j = it // 2, it % 2
                e.wait_ge(sem("mkv_mm"), it + 1)
                if c < 2:
                    copy(mraw[:, it, :], PS[:, it % 4, :], "mkv_ev")
                    e.wait_ge(sem("mk_ss"), upto("mk_ss", it + 1))
                    e.activation(stat[:, 72:74], stat[:, 64:66], ACT.Sqrt, bias=eps[:, :],
                                 scale=1.0 / MD).then_inc(sem("mk_rt"), 1)
                else:
                    copy(mv[:, j, (c - 2) * 512:(c - 1) * 512], PS[:, it % 4, :], "mkv_ev")
                if j == 0 and 4 + c < 8:
                    B.split_hi(e, 4 + c) if c >= 1 else None
                if j == 1 and c == 0:
                    B.split_hi(e, 4)
                if it >= 4:
                    q = it - 4
                    cq, jq = q // 2, q % 2
                    e.wait_ge(sem("mk_tp"), upto("mk_tp", q + 1))
                    copy(mkT[:, 4 * cq:4 * cq + 4, jq * P:(jq + 1) * P],
                         PS[:, 4 + q % 2, :].rearrange("p (a b) -> p a b", b=P), "mk_te")
            e.wait_ge(sem("mk_st"), upto("mk_st", 64))
            for L in range(len(L6) + 2):
                if L < len(L6):
                    n = rows(L6[L][1])
                    e.wait_ge(sem("q7_mm"), upto("q7_mm", L + 1))
                    if L >= 3:
                        e.wait_ge(sem("q7_tp"), upto("q7_tp", L - 2))
                    copy(qraw[0:n, L % 3, :], PS[0:n, L % 4, :], "q7_raw")
                if L >= 2:
                    q = L - 2
                    c, j = L6[q]
                    e.wait_ge(sem("q7_tp"), upto("q7_tp", q + 1))
                    copy(mqT[:, 4 * c:4 * c + 4, tcols(j)],
                         PS[:, 4 + q % 2, :].rearrange("p (a b) -> p a b", b=P)[:, :, 0:rows(j)], "q7_te")
                if L < len(L6):
                    e.wait_ge(sem("q7_ss"), upto("q7_ss", L + 1))
                    e.activation(stat[0:n, 72:74], stat[0:n, 64:66], ACT.Sqrt, bias=eps[0:n, :],
                                 scale=1.0 / MD).then_inc(sem("q7_rt"), 1)
            for j in range(NB + 3):
                if j < NB:
                    e.wait_ge(sem("ma_nm"), upto("ma_nm", j + 1))
                    if j >= 2:
                        e.wait_ge(sem("ma_tt"), upto("ma_tt", j - 1))
                    for hh in range(MH):
                        x = e.activation(mlog[:, j % 2, hh * NMEM:(hh + 1) * NMEM],
                                         PS[:, 2 * (j % 2) + hh // 2, (hh % 2) * NMEM:(hh % 2 + 1) * NMEM], ACT.Exp,
                                         bias=mat_st[:, j % 2, 1, hh:hh + 1], scale=MEM_SCALE,
                                         accum_out=mat_st[:, j % 2, 2, hh:hh + 1])
                    x.then_inc(sem("ma_exp"), 1)
                if 1 <= j <= NB:
                    q = j - 1
                    e.wait_ge(sem("ma_tt"), upto("ma_tt", q + 1))
                    if q >= 2:
                        e.wait_ge(sem("ma_pv"), upto("ma_pv", q - 1))
                    copy(mpT[:, q % 2, :, :].rearrange("p a b -> p (a b)"),
                         PS[:, 4:6, :].rearrange("p a b -> p (a b)"), "ma_pte")
                if j >= 3:
                    q = j - 3
                    e.wait_ge(sem("ma_pv"), upto("ma_pv", q + 1))
                    copy(xb_hi[:, :, tcols(q)], PS[:, 6:8, :].rearrange("p a (c q) -> p (a c) q", q=P), "ma_hi")
            for hh in range(MH):
                for b in range(DEC_B):
                    n = hh * DEC_B + b
                    e.wait_ge(sem("mkb_tp"), upto("mkb_tp", n + 1))
                    copy(mKT[:, hh % 2, :, b * NMEM:(b + 1) * NMEM],
                         PS[:, 4 + n % 2, :].rearrange("p (a b) -> p a b", a=2), "mkb_ev")
                e.wait_ge(sem("ms_nm"), hh + 1)
                if hh >= 1:
                    e.wait_ge(sem("ms_tt"), hh)
                e.activation(mp_s[:, :], PS[0:NS, hh % 2, 0:NMEM], ACT.Exp, bias=sat_st[:, 1, hh:hh + 1],
                             scale=MEM_SCALE, accum_out=sat_st[:, 2, hh:hh + 1]).then_inc(sem("ms_exp"), 1)
                e.wait_ge(sem("ms_tt"), hh + 1)
                copy(mpT_s[:, hh, :], PS[:, 2, 0:2 * NS], "ms_pte")
            e.wait_ge(sem("mvb_used"), upto("mvb_used", MH * DEC_B))
            copy(xb_hi[:, :, SEQ:T], PS[:, 3, :].rearrange("p (a b) -> p a b", b=NS), "sm_hi")
            C.split_hi(e, 0)
            C.split_hi(e, 1)
            N3.ready = lambda e, j: e.wait_ge(sem("l8_ev"), upto("l8_ev", NT + j + 1))
            for j in range(NT + 2):
                if j >= 2:
                    N3.act_hi(e, j - 2)
                if j < NT:
                    N3.act_root(e, j)

            def gu_hi(n):
                f, g = n // 2, n % 2
                e.wait_ge(sem(f"fw_ld{g}"), upto(f"fw_ld{g}", 16 * (f + 1)))
                if n >= 4:
                    e.wait_ge(sem("gu_mm"), n - 3)
                copy(fw_hi[:, f % 2, g, :], fst[:, g, :, :].rearrange("p a b -> p (a b)"), "fw_hi")

            gu_hi(0)
            gu_hi(1)
            e.wait_ge(sem("h3_st"), 16 * NT)
            for f in range(FT):
                if f + 1 < FT:
                    gu_hi(2 * f + 2)
                    gu_hi(2 * f + 3)
                e.wait_ge(sem("gu_mm"), 2 * f + 1)
                if f >= 1:
                    e.wait_ge(sem("f_conv"), f)
                    e.wait_ge(sem("f_st"), f)
                e.activation(gate_s[:, 2:2 + SEQ], PS[:, 0:2, :].rearrange("p a b -> p (a b)"), ACT.Copy)
                copy(gate_s[:, SB0:SB0 + DEC_B * STR].rearrange("p (b c) -> p b c", c=STR)[:, :, 2:STR],
                     PS[:, 2, 0:NS].rearrange("p (b c) -> p b c", c=DEC_T), "f_gate")
                e.wait_ge(sem("f_conv"), f + 1)
                e.activation(conv_s[:, f % 2, 0:CW], conv_s[:, f % 2, 0:CW], ACT.Silu,
                             bias=ffn_sw[:, f, 19:20]).then_inc(sem("f_silu"), 1)
                e.wait_ge(sem("f_mul"), f + 1)
                e.activation(ffn_hi[:, f, 0:SEQ], conv_s[:, f % 2, 0:SEQ], ACT.Copy)
                copy(ffn_hi[:, f, SEQ:T].rearrange("p (b c) -> p b c", c=DEC_T),
                     conv_s[:, f % 2, SB0:SB0 + DEC_B * STR].rearrange("p (b c) -> p b c", c=STR)[:, :, 0:DEC_T],
                     "f_hi")
            e.wait_ge(sem("ffnst_tp"), upto("ffnst_tp", 1))
            e.activation(ffnst[:, 0:2560], PS[0:18, 0:5, :].rearrange("p a b -> p (a b)"), ACT.Copy)
            copy(ffnst[:, 2560:DFF], PS[0:18, 5, 0:DFF - 2560], "ffnst_ev")
            e.wait_ge(sem("f_lo"), FT)
            for c in range(4):
                if c >= 2:
                    e.wait_ge(sem("down_mm"), NT * (c - 1))
                for half in range(2):
                    e.wait_ge(sem(f"dw_ld{half}"), upto(f"dw_ld{half}", 16 * (c + 1)))
                    copy(dw_hi[:, c % 2, half * 11 * 256:(half + 1) * 11 * 256],
                         dst[:, half, :, :].rearrange("p a b -> p (a b)"), "dw_hi")

        @block.vector
        def _(e):
            cnt = [0]

            def link(ins):
                chain(e, ins, "dve", cnt)

            e.memset(eps[:, :], EPS).then_inc(sem("eps"), 1)
            e.wait_ge(sem("const"), 16 * CONSTS)
            for j in range(NT + 2):
                if 1 <= j <= NT:
                    N1.dve_norm(e, j - 1, lambda j: h[0:rows(j), j, :])
                if j >= 2:
                    N1.dve_lo(e, j - 2)

            def head_norm(L, n, v, heads, width, gain, tmp, s_ss, s_rt, last=None):
                vh = v.rearrange("p (a d) -> p a d", d=width)
                link(e.tensor_tensor(tmp[0:n, :], v, v, ALU.mult))
                e.tensor_reduce(stat[0:n, 64:64 + heads], tmp[0:n, :].rearrange("p (a d) -> p a d", d=width), AX.X,
                                ALU.add).then_inc(sem(s_ss), 1)
                e.wait_ge(sem(s_rt), upto(s_rt, L + 1))
                link(e.reciprocal(stat[0:n, 80:80 + heads], stat[0:n, 72:72 + heads]))
                link(e.tensor_tensor(vh, vh, stat[0:n, 80:80 + heads][:, :, None].broadcast_to([n, heads, width]),
                                     ALU.mult))
                x = e.tensor_tensor(vh, vh, gain[:, None, :].broadcast_to([n, heads, width]), ALU.mult)
                if last:
                    x.then_inc(sem(last), 1)
                else:
                    link(x)

            for L in range(NI):
                c, j = ITEMS[L]
                n = rows(j)
                e.wait_ge(sem("s2_raw"), L + 1)
                if c < 2:
                    head_norm(L, n, raw[0:n, L % 3, :], H, HD, qkg[0:n, c, :], rope1, "s2_ss", "s2_rt")
                groups = H if c < 3 else 1
                w = groups * HD
                r = raw[0:n, L % 3, 0:w].rearrange("p (a d) -> p a d", d=32)
                rr = raw[0:n, L % 3, 0:w].rearrange("p (a two d) -> p a two d", two=2, d=32)
                t2 = rope2[0:n, 0:w].rearrange("p (a two d) -> p a two d", two=2, d=32)
                cs = cos_t[0:n, j, :][:, None, :].broadcast_to([n, 2 * groups, 32])
                sn = sin_t[0:n, j, :][:, None, :].broadcast_to([n, groups, 32])
                e.tensor_tensor(rope1[0:n, 0:w].rearrange("p (a d) -> p a d", d=32), r, cs, ALU.mult)
                e.scalar_tensor_tensor(t2[:, :, 0, :], rr[:, :, 1, :], -1.0, sn, ALU.mult, ALU.mult)
                link(e.tensor_tensor(t2[:, :, 1, :], rr[:, :, 0, :], sn, ALU.mult))
                if L >= 3:
                    e.wait_ge(sem("s2_tp"), L - 2)
                if stores_of_slot(L):
                    e.wait_ge(sem(f"s2_st{L % 3}"), upto(f"s2_st{L % 3}", 16 * stores_of_slot(L)))
                if c == 3:
                    link(e.tensor_scalar(iwt[0:n, j, :], raw[0:n, L % 3, HD:HD + H], IDX_SCALE, None, ALU.mult))
                    link(e.tensor_tensor(roped[0:n, L % 3, HD:2 * HD], rope1[0:n, 0:w], rope2[0:n, 0:w], ALU.add))
                e.tensor_tensor(roped[0:n, L % 3, 0:w], rope1[0:n, 0:w], rope2[0:n, 0:w], ALU.add
                                ).then_inc(sem("s2_roped"), 1)
                e.wait_ge(sem("s2_roped"), L + 1)

            for m in range(ND + H):
                e.wait_ge(sem("s3_relu"), m + 1)
                if m < ND:
                    i, hh = DOTS[m]
                    n = (i + 1) * P
                    out = work[:, topk_cols(i):topk_cols(i) + n]
                    src, w = relu[:, m % 2, 0:n], iwt[:, i, hh:hh + 1]
                else:
                    hh = m - ND
                    out, src, w = work_s[:, 0:S_KEYS], relu[0:NS, m % 2, 0:S_KEYS], iwt[0:NS, NB, hh:hh + 1]
                if hh == 0:
                    x = e.tensor_scalar(out, src, w, None, ALU.mult)
                else:
                    x = e.scalar_tensor_tensor(out, src, w, out, ALU.mult, ALU.add)
                x.then_inc(sem("s3_acc"), 1)
                e.wait_ge(sem("s3_acc"), m + 1)
                if hh == H - 1 and m < ND:
                    d = work[:, topk_cols(i) + i * P:topk_cols(i) + n]
                    link(e.tensor_tensor(d, d, mask01[:, P:2 * P], ALU.add))
                elif hh == H - 1:
                    d = work_s[:, PAST:S_KEYS]
                    link(e.tensor_tensor(d, d, smask[0:NS, :], ALU.add))

            def select(v, n, count, name):
                for r in range((count + 7) // 8):
                    link(e.max(m8[0:n, :], v))
                    left = count - 8 * r
                    if left < 8:
                        link(e.memset(m8[0:n, left:8], NEG))
                    link(e.match_replace(v, m8[0:n, :], v, NEG))
                e.tensor_scalar(v, v, NEG, MASKED, ALU.not_equal, ALU.mult).then_inc(sem("topk"), 1)

            e.memset(work_s[:, S_KEYS:S_KEYS + 8], NEG).then_inc(sem("pad"), 1)
            e.wait_ge(sem("pad"), 1)
            for i in range(2, NB):
                select(work[:, topk_cols(i):topk_cols(i) + (i + 1) * P], P, TOPK, "topk")
            select(work_s[:, :], NS, TOPK_S, "topk")

            for m in range(NA + 3):
                if m < NA:
                    i, hh = ATT[m]
                    n = (i + 1) * P
                    mask = mask01[:, P:2 * P] if i == 0 else mask01[:, :] if i == 1 else \
                        work[:, topk_cols(i):topk_cols(i) + n]
                    if i >= 2 and hh == 0:
                        e.wait_ge(sem("topk"), i - 1)
                    e.wait_ge(sem("at_qk"), m + 1)
                    if m >= 2:
                        e.wait_ge(sem("at_tt"), m - 1)
                    e.tensor_tensor_reduce(logit[:, m % 2, 0:n],
                                           PS[:, 2 * (m % 2):2 * (m % 2) + 2, :].rearrange("p a b -> p (a b)")[:, 0:n],
                                           mask, 1.0, NEG, ALU.add, ALU.max,
                                           att_st[:, m % 2, 0:1]).then_inc(sem("at_max"), 1)
                    e.wait_ge(sem("at_max"), m + 1)
                    e.tensor_scalar(att_st[:, m % 2, 1:2], att_st[:, m % 2, 0:1], -ATT_SCALE, None, ALU.mult
                                    ).then_inc(sem("at_nm"), 1)
                    e.wait_ge(sem("at_exp"), m + 1)
                    e.reciprocal(att_st[:, m % 2, 3:4], att_st[:, m % 2, 2:3]).then_inc(sem("at_rc"), 1)
                if m >= 3 and ATT[m - 3][1] == H - 1:
                    i = ATT[m - 3][0]
                    e.wait_ge(sem("at_hi"), i + 1)
                    e.tensor_tensor(xa_lo[:, 0:4, tcols(i)], PS[:, 6 + i % 2, :].rearrange("p (a b) -> p a b", b=P),
                                    xa_hi[:, 0:4, tcols(i)], ALU.subtract).then_inc(sem("at_lo"), 1)
            e.wait_ge(sem("topk"), NB - 1)
            for hh in range(H):
                e.wait_ge(sem("sa_qk"), hh + 1)
                e.tensor_tensor_reduce(p_s[:, hh, :], PS[0:NS, hh % 2, 0:S_KEYS], work_s[:, 0:S_KEYS], 1.0, NEG,
                                       ALU.add, ALU.max, sat_st[:, 0, hh:hh + 1]).then_inc(sem("sa_max"), 1)
            e.wait_ge(sem("sa_max"), H)
            e.tensor_scalar(sat_st[:, 1, :], sat_st[:, 0, :], -ATT_SCALE, None, ALU.mult).then_inc(sem("sa_nm"), 1)
            e.wait_ge(sem("sa_exp"), H)
            link(e.reciprocal(sat_st[:, 3, :], sat_st[:, 2, :]))
            e.tensor_tensor(p_s[:, :, :], p_s[:, :, :], sat_st[:, 3, :][:, :, None].broadcast_to([NS, H, S_KEYS]),
                            ALU.mult).then_inc(sem("sa_p"), 1)
            e.wait_ge(sem("sa_hi"), 1)
            e.tensor_tensor(xa_lo[:, 0:4, SEQ:T], PS[:, 6, 0:4 * NS].rearrange("p (a b) -> p a b", b=NS),
                            xa_hi[:, 0:4, SEQ:T], ALU.subtract).then_inc(sem("sa_lo"), 1)

            def residual(name, norm, first_ready, gsem):
                for L in range(len(L6) + 2):
                    if L < len(L6):
                        c, j = L6[L]
                        n = rows(j)
                        e.wait_ge(sem(f"{name}_mm"), upto(f"{name}_mm", L + 1))
                        first_ready(L, j)
                        v = h[0:n, j, c * 512:(c + 1) * 512]
                        e.tensor_tensor(v, PS[0:n, L % 4, :], v, ALU.add).then_inc(sem(f"{name}_ev"), 1)
                    if NT + 1 <= L <= 2 * NT:
                        if L == NT + 1:
                            e.wait_ge(sem("g_ld"), gsem)
                        norm.dve_norm(e, L - NT - 1, lambda j: xnorm[0:rows(j), j % 2, :])
                    if L >= NT + 2:
                        norm.dve_lo(e, L - NT - 2)

            residual("l6", N2, lambda L, j: e.wait_ge(sem("x2_ld"), 16 * NT), 16)
            e.wait_ge(sem("g_ld"), 32)
            for j in range(2):
                NM.dve_norm(e, j, lambda j: memx[:, j, :])
            for j in range(2):
                NM.dve_lo(e, j)
            for it in range(4):
                e.wait_ge(sem("mkv_ev"), it + 1)
                head_norm(it, P, mraw[:, it, :], 2, MD, mqkg[:, 1, :], mtmp, "mk_ss", "mk_rt", "mk_out")
            for L in range(len(L6)):
                n = rows(L6[L][1])
                e.wait_ge(sem("q7_raw"), upto("q7_raw", L + 1))
                head_norm(L, n, qraw[0:n, L % 3, :], 2, MD, mqkg[0:n, 0, :], qtmp, "q7_ss", "q7_rt", "q7_n")
            for j in range(NB + 3):
                if j < NB:
                    e.wait_ge(sem("ma_qk"), upto("ma_qk", j + 1))
                    link(e.tensor_reduce(mat_st[:, j % 2, 0, :],
                                         PS[:, 2 * (j % 2):2 * (j % 2) + 2, :].rearrange("p a (b c) -> p (a b) c", b=2),
                                         AX.X, ALU.max))
                    e.tensor_scalar(mat_st[:, j % 2, 1, :], mat_st[:, j % 2, 0, :], -MEM_SCALE, None, ALU.mult
                                    ).then_inc(sem("ma_nm"), 1)
                    e.wait_ge(sem("ma_exp"), upto("ma_exp", j + 1))
                    link(e.reciprocal(mat_st[:, j % 2, 3, :], mat_st[:, j % 2, 2, :]))
                    v = mlog[:, j % 2, :].rearrange("p (a b) -> p a b", b=NMEM)
                    e.tensor_tensor(v, v, mat_st[:, j % 2, 3, :][:, :, None].broadcast_to([P, MH, NMEM]), ALU.mult
                                    ).then_inc(sem("ma_p"), 1)
                if j >= 3:
                    q = j - 3
                    e.wait_ge(sem("ma_hi"), upto("ma_hi", q + 1))
                    e.tensor_tensor(xb_lo[:, :, tcols(q)], PS[:, 6:8, :].rearrange("p a (c q) -> p (a c) q", q=P),
                                    xb_hi[:, :, tcols(q)], ALU.subtract).then_inc(sem("ma_lo"), 1)
            for hh in range(MH):
                e.wait_ge(sem("ms_qk"), hh + 1)
                link(e.tensor_reduce(sat_st[:, 0, hh:hh + 1], PS[0:NS, hh % 2, 0:NMEM], AX.X, ALU.max))
                e.tensor_scalar(sat_st[:, 1, hh:hh + 1], sat_st[:, 0, hh:hh + 1], -MEM_SCALE, None, ALU.mult
                                ).then_inc(sem("ms_nm"), 1)
                e.wait_ge(sem("ms_exp"), hh + 1)
                link(e.reciprocal(sat_st[:, 3, hh:hh + 1], sat_st[:, 2, hh:hh + 1]))
                e.tensor_scalar(mp_s[:, :], mp_s[:, :], sat_st[:, 3, hh:hh + 1], None, ALU.mult
                                ).then_inc(sem("ms_p"), 1)
            e.wait_ge(sem("sm_hi"), 1)
            e.tensor_tensor(xb_lo[:, :, SEQ:T], PS[:, 3, :].rearrange("p (a b) -> p a b", b=NS),
                            xb_hi[:, :, SEQ:T], ALU.subtract).then_inc(sem("sm_lo"), 1)
            residual("l8", N3, lambda L, j: None, 48)
            for f in range(FT):
                e.wait_ge(sem("f_gate"), f + 1)
                e.wait_ge(sem("f_pre"), f + 1)
                if f >= 2:
                    e.wait_ge(sem("f_lo"), f - 1)
                cv = conv_s[:, f % 2, 0:CW]
                link(e.tensor_scalar(cv, gate_s[:, 0:CW], ffn_sw[:, f, 16:17], None, ALU.mult))
                link(e.scalar_tensor_tensor(cv, gate_s[:, 1:1 + CW], ffn_sw[:, f, 17:18], cv, ALU.mult, ALU.add))
                e.scalar_tensor_tensor(cv, gate_s[:, 2:2 + CW], ffn_sw[:, f, 18:19], cv, ALU.mult, ALU.add
                                       ).then_inc(sem("f_conv"), 1)
                e.wait_ge(sem("f_silu"), f + 1)
                e.wait_ge(sem("gu_mm"), 2 * f + 2)
                v = conv_s[:, f % 2, 0:SEQ]
                e.tensor_tensor(v, PS[:, 3:5, :].rearrange("p a b -> p (a b)"), v, ALU.mult)
                v = conv_s[:, f % 2, SB0:SB0 + DEC_B * STR].rearrange("p (b c) -> p b c", c=STR)[:, :, 0:DEC_T]
                e.tensor_tensor(v, PS[:, 5, 0:NS].rearrange("p (b c) -> p b c", c=DEC_T), v, ALU.mult
                                ).then_inc(sem("f_mul"), 1)
            for n in range(4 * NT):
                r = rows(n % NT)
                e.wait_ge(sem("down_mm"), n + 1)
                e.wait_ge(sem(f"res_ld{n % 4}"), upto(f"res_ld{n % 4}", 16 * (n // 4 + 1)))
                if n >= 4:
                    e.wait_ge(sem(f"y_st{n % 4}"), upto(f"y_st{n % 4}", 16 * (n // 4)))
                e.tensor_tensor(outb[0:r, n % 4, :], PS[0:r, n % 4, 0:256], res[0:r, n % 4, :], ALU.add
                                ).then_inc(sem("down_ev"), 1)

        @block.gpsimd
        def _(e):
            for n in range(5):
                A.split_lo(e, n)
            e.wait_ge(sem("s2_te"), NI)
            e.memset(qm_i[:, :], 0.0).then_inc(sem("qmi"), 1)
            e.wait_ge(sem("qmi"), 1)
            for p in range(4):
                e.tensor_copy(mask_view(qm_i, p), qiT[:, p, SEQ:T].rearrange("p (b c) -> p b c", c=DEC_T)
                              ).then_inc(sem("qmi"), 1)
            A.split_lo(e, 5)
            cnt = [0]

            def link(ins):
                chain(e, ins, "pool", cnt)

            def spaced(v):
                return v[:, SB0:SB0 + DEC_B * STR].rearrange("p (b c) -> p b c", c=STR)[:, :, 0:DEC_T]

            us = u_s[:, SB0:SB0 + DEC_B * STR].rearrange("p (b c) -> p b c", c=STR)

            def sample(v):
                return v[:, SEQ:T].rearrange("p (b c) -> p b c", c=DEC_T)

            last_of = {f: max(x for x, it in enumerate(L4) if it[0] == "c" and it[1] == f) for f in range(NC_T)}
            for f in range(NC_T):
                if 6 + f < len(A.chunks):
                    A.split_lo(e, 6 + f)
                e.wait_ge(sem("s4_ev"), last_of[f] + 1)
                if f == 0:
                    e.memset(u_s[:, 0:2], 0.0)
                e.tensor_copy(us[:, :, 0:2], mix_sw[:, f, 0:16].rearrange("p (b c) -> p b c", c=2))
                e.tensor_tensor(u_s[:, 2:2 + SEQ], cc_s[:, 0:SEQ], ch_s[:, 0:SEQ], ALU.mult)
                link(e.tensor_tensor(us[:, :, 2:STR], sample(cc_s), sample(ch_s), ALU.mult))
                e.tensor_copy(u_state[:, f, 0:16].rearrange("p (b c) -> p b c", c=2), us[:, :, DEC_T:STR])
                e.tensor_copy(u_state[:, f, 16:18], u_s[:, SEQ:SEQ + 2]).then_inc(sem("conv_u"), 1)
                e.wait_ge(sem("conv_t"), 3 * (f + 1))
                link(e.tensor_tensor(cc_s[:, 0:CW], cc_s[:, 0:CW], ch_s[:, 0:CW], ALU.add))
                link(e.tensor_tensor(cc_s[:, 0:CW], cc_s[:, 0:CW], tap2[:, 0:CW], ALU.add))
                e.tensor_tensor(ch_s[:, 0:SEQ], cc_s[:, 0:SEQ], cb_s[:, 0:SEQ], ALU.mult)
                e.tensor_tensor(sample(ch_s), spaced(cc_s), sample(cb_s), ALU.mult).then_inc(sem("conv_y"), 1)
                e.wait_ge(sem("conv_hi"), f + 1)
                e.tensor_tensor(ct_lo[:, f, :], ch_s[:, 0:T], ct_hi[:, f, :], ALU.subtract).then_inc(sem("conv_lo"), 1)
            e.wait_ge(sem("s4_mm"), len(L4))
            e.memset(qm_a[:, :], 0.0).then_inc(sem("qma"), 1)
            e.wait_ge(sem("qma"), 1)
            for p in range(4):
                e.tensor_copy(mask_view(qm_a, p), qT[:, p, SEQ:T].rearrange("p (b c) -> p b c", c=DEC_T)
                              ).then_inc(sem("qma"), 1)
                e.tensor_copy(kTb[:, p, :].rearrange("p (b c) -> p b c", c=S_KEYS)[:, :, PAST:S_KEYS],
                              kT[:, p, SEQ:T].rearrange("p (b c) -> p b c", c=DEC_T)).then_inc(sem("qma"), 1)
            for m in range(NA):
                n = (ATT[m][0] + 1) * P
                e.wait_ge(sem("at_rc"), m + 1)
                e.tensor_scalar(logit[:, m % 2, 0:n], logit[:, m % 2, 0:n], att_st[:, m % 2, 3:4], None, ALU.mult
                                ).then_inc(sem("at_p"), 1)
            for n in range(8):
                B.split_lo(e, n)
            e.wait_ge(sem("q7_mm"), upto("q7_mm", 2 * NT))
            link(e.memset(qm_m[:, :], 0.0))
            e.wait_ge(sem("q7_te"), upto("q7_te", len(L6)))
            for hh in range(MH):
                if hh >= 1:
                    e.wait_ge(sem("ms_qk"), hh)
                for kk in range(2):
                    x = e.tensor_copy(mask_view(qm_m, kk),
                                      mqT[:, 2 * hh + kk, SEQ:T].rearrange("p (b c) -> p b c", c=DEC_T))
                x.then_inc(sem("qmm"), 1)
            for n in range(2):
                C.split_lo(e, n)

            def gu_lo(n):
                f, g = n // 2, n % 2
                e.wait_ge(sem("fw_hi"), n + 1)
                e.tensor_tensor(fw_lo[:, f % 2, g, :], fst[:, g, :, :].rearrange("p a b -> p (a b)"),
                                fw_hi[:, f % 2, g, :], ALU.subtract).then_inc(sem("fw_lo"), 1)

            gs = gate_s[:, SB0:SB0 + DEC_B * STR].rearrange("p (b c) -> p b c", c=STR)
            gu_lo(0)
            gu_lo(1)
            e.memset(gate_s[:, 0:2], 0.0)
            for f in range(FT):
                if f >= 1:
                    e.wait_ge(sem("f_conv"), f)
                e.tensor_copy(gs[:, :, 0:2], ffn_sw[:, f, 0:16].rearrange("p (b c) -> p b c", c=2)
                              ).then_inc(sem("f_pre"), 1)
                if f + 1 < FT:
                    gu_lo(2 * f + 2)
                    gu_lo(2 * f + 3)
                e.wait_ge(sem("f_gate"), f + 1)
                e.tensor_copy(g_state[:, f, 0:16].rearrange("p (b c) -> p b c", c=2), gs[:, :, DEC_T:STR])
                e.tensor_copy(g_state[:, f, 16:18], gate_s[:, SEQ:SEQ + 2]).then_inc(sem("f_st"), 1)
                e.wait_ge(sem("f_hi"), f + 1)
                e.tensor_tensor(ffn_lo[:, f, 0:SEQ], conv_s[:, f % 2, 0:SEQ], ffn_hi[:, f, 0:SEQ], ALU.subtract)
                e.tensor_tensor(ffn_lo[:, f, SEQ:T].rearrange("p (b c) -> p b c", c=DEC_T),
                                conv_s[:, f % 2, SB0:SB0 + DEC_B * STR].rearrange("p (b c) -> p b c", c=STR)[:, :, 0:DEC_T],
                                ffn_hi[:, f, SEQ:T].rearrange("p (b c) -> p b c", c=DEC_T), ALU.subtract
                                ).then_inc(sem("f_lo"), 1)

            def down_lo(c):
                for half in range(2):
                    a = slice(half * 11 * 256, (half + 1) * 11 * 256)
                    e.wait_ge(sem("dw_hi"), upto("dw_hi", 2 * c + half + 1))
                    e.tensor_tensor(dw_lo[:, c % 2, a], dst[:, half, :, :].rearrange("p a b -> p (a b)"),
                                    dw_hi[:, c % 2, a], ALU.subtract).then_inc(sem("dw_lo"), 1)

            down_lo(0)
            down_lo(1)
            e.wait_ge(sem("gu_mm"), 2 * FT)
            for c in range(4):
                for j in range(NT):
                    n = c * NT + j
                    if n >= 4:
                        e.wait_ge(sem("down_ev"), n - 3)
                    e.dma_start(res[0:rows(j), n % 4, :],
                                h3[j * P:j * P + rows(j), c * 256:(c + 1) * 256]).then_inc(sem(f"res_ld{n % 4}"), 16)
                if c + 2 < 4:
                    down_lo(c + 2)


INPUTS = ["x_prompt", "x_sample", "cache_k", "cache_v", "cache_idx_k", "state_conv_mix", "state_conv_ffn",
          "cache_mem_k", "cache_mem_v", "page_table", "mem_prompt", "g_mix", "w_in", "conv_mix_w", "q_norm_g",
          "k_norm_g", "w_out", "g_mem", "g_mem_src", "w_q_mem", "w_kv_mem", "mq_norm_g", "mk_norm_g", "w_o_mem",
          "g_ffn", "w_gu", "conv_ffn_w", "conv_ffn_b", "w_down"]
OUTPUTS = [("o_yp", (1, SEQ, D)), ("o_ys", (DEC_B, DEC_T, D)), ("o_kp", (1, 1, SEQ, H, HD)),
           ("o_vp", (1, 1, SEQ, H, HD)), ("o_ikp", (1, 1, SEQ, HD)), ("o_cmp", (1, 1, 2, DC)),
           ("o_cfp", (1, 1, 2, DFF)), ("o_mk", (1, 1, NMEM, MH, MD)), ("o_mv", (1, 1, NMEM, MH, MD)),
           ("o_ks", (1, DEC_B, DEC_T, H, HD)), ("o_vs", (1, DEC_B, DEC_T, H, HD)), ("o_iks", (1, DEC_B, DEC_T, HD)),
           ("o_cms", (1, DEC_B, 2, DC)), ("o_cfs", (1, DEC_B, 2, DFF))]


def constants():
    pos = np.concatenate([np.arange(SEQ), np.tile(PAST + np.arange(DEC_T), P // DEC_T)]).astype(np.float32)
    inv = np.exp(np.arange(HD // 2) * (-2.0 * math.log(10000.0) / HD)).astype(np.float32)
    ang = pos[:, None] * inv[None, :]
    row = np.arange(P)
    causal = np.where(row[None, :] <= row[:, None], 0.0, MASKED).astype(np.float32)
    return {
        "c_cos": np.cos(ang).astype(np.float32),
        "c_sin": np.sin(ang).astype(np.float32),
        "c_mask": np.concatenate([np.zeros((P, P), np.float32), causal], axis=1),
        "c_smask": np.where(np.arange(DEC_T)[None, :] <= (np.arange(NS) % DEC_T)[:, None], 0.0, MASKED).astype(np.float32),
        "c_ident": np.eye(P, dtype=np.float32),
    }


def kernel(**inputs):
    import concourse.bacc as bacc
    from concourse.bass_utils import run_bass_kernel_spmd

    nc = bacc.Bacc("TRN2", target_bir_lowering=False, num_devices=1)
    arrays = {name: np.ascontiguousarray(inputs[name]) for name in INPUTS}
    arrays.update(constants())
    io = {name: nc.dram_tensor(name, a.shape, mybir.dt.from_np(a.dtype), kind="ExternalInput").ap()
          for name, a in arrays.items()}
    for name, shape in OUTPUTS:
        io[name] = nc.dram_tensor(name, shape, F32, kind="ExternalOutput").ap()
    build(nc, io)
    got = run_bass_kernel_spmd(nc, [arrays], core_ids=[0]).results[0]
    return tuple(got[name] for name, _ in OUTPUTS)
```

```python
from contextlib import ExitStack
import math

import numpy as np
import concourse.bass as bass
from concourse import mybir

F32 = mybir.dt.float32
F16 = mybir.dt.float16
BF16 = mybir.dt.bfloat16
I32 = mybir.dt.int32
ALU = mybir.AluOpType
ACT = mybir.ActivationFunctionType
AX = mybir.AxisListType

P = 128
D = 1024
KT = D // P
SEQ = 1024
DEC_B, DEC_T = 8, 8
NS = DEC_B * DEC_T
T = SEQ + NS
NT = 9
NB = SEQ // P
PAST, PAGE = 256, 128
NPG = PAST // PAGE
N_POOL = 20
H, HD = 8, 64
DA = H * HD
DC = 512
NC_T = DC // P
D_IN = 3656
MH, MD = 4, 256
NMEM = 256
DFF = 2816
FT = DFF // P
TOPK = 256
S_KEYS = PAST + DEC_T
TOPK_S = S_KEYS // 4
EPS = 1e-6
ATT_SCALE = HD ** -0.5
MEM_SCALE = MD ** -0.5
IDX_SCALE = (H * HD) ** -0.5
NEG = -3.0e38
MASKED = -1.0e30
GW = SEQ + 2 + DEC_B * (DEC_T + 2)
CW = GW - 2
SB0 = SEQ + 2
STR = DEC_T + 2
DIAG = NS + DEC_T
ROUNDS_BEFORE, ROUNDS_ITEM, ROUNDS_SAMPLE0, ROUNDS_SAMPLE, ROUNDS_TOKENS, ROUNDS_KEYS, ROUNDS_MEMORY, \
    ROUNDS_VALUES, ROUNDS_ATT = \
    116, (1, 2), 7, 3, 1, 3, 1, 13, 1
QB, KB, VB, QIB, KIB = 1536, 2048, 2560, 3072, 3584


def rows(j):
    return P if j < NB else NS


def token_chunks():
    return [(0, 512), (512, 512), (1024, NS)]


def x_group(j):
    return j if j < 3 else 2 + j // 3


def topk_cols(i):
    return sum((k + 1) * P for k in range(2, i))


def build(nc, io):
    ctx = ExitStack()
    with ctx:
        sems = {}

        on = {}
        for what in ("ss", "rt", "rc", "xn", "tp", "hi", "lo"):
            on |= {f"nm_{what}": (f"n1_{what}", NT), f"n2_{what}": (f"n1_{what}", NT + 2),
                   f"n3_{what}": (f"n1_{what}", 2 * NT + 2)}
        for what, a, b in (("hi", 18, 34), ("lo", 18, 34), ("ld0", 272, 400), ("ld1", 272, 400)):
            on |= {f"wb_{what}": (f"wa_{what}", a), f"wc_{what}": (f"wa_{what}", b)}
        on |= {"mk_rt": ("s2_rt", 2 * NT), "q7_rt": ("s2_rt", 2 * NT + 4), "q7_ss": ("mk_ss", 4)}
        for k in range(2):
            on |= {f"mkb_ld{k}": (f"kb_ld{k}", 128), f"mvb_ld{k}": (f"vb_ld{k}", 128),
                   f"dw_ld{k}": (f"vn_ld{k}", 16 * DEC_B // 2)}
        on |= {"dw_hi": ("fw_hi", 2 * FT), "dw_lo": ("fw_lo", 2 * FT), "l8_mm": ("l6_mm", 2 * NT),
               "l8_ev": ("l6_ev", 2 * NT), "mkb_tp": ("kb_tp", 16), "mkb_ev": ("kb_ev", 16),
               "q7_tp": ("s2_tp", 4 * NT), "q7_te": ("s2_te", 4 * NT), "q7_raw": ("s2_raw", 4 * NT),
               "q7_n": ("s2_roped", 4 * NT), "ffnst_tp": ("mixst_tp", 1), "ffnst_ev": ("mixst_ev", 1)}
        for what, a in (("qk", 64), ("exp", 64), ("nm", 64), ("pv", 64)):
            on[f"ma_{what}"] = (f"at_{what}", a)

        for k in range(5):
            on[f"x2_ld{k}"] = (f"x_ld{k}", 16 if k < 3 else 48)

        def sem(name):
            name = on.get(name, (name, 0))[0]
            if name not in sems:
                sems[name] = ctx.enter_context(nc.semaphore(name))
            return sems[name]

        def upto(name, count):
            return on.get(name, (name, 0))[1] + count

        def sb(name, shape, dt):
            return ctx.enter_context(nc.sbuf_tensor(name, shape, dt))

        ident = sb("ident", [P, P], F32)
        mask01 = sb("mask01", [P, 2 * P], F32)
        smask = sb("smask", [P, DEC_T], F32)
        cos_t = sb("cos_t", [P, NT, 32], F32)
        sin_t = sb("sin_t", [P, NT, 32], F32)
        gb = sb("gb", [P, D], F32)
        qkg = sb("qkg", [P, 2, HD], F32)
        mqkg = sb("mqkg", [P, 2, MD], F32)
        mix_sw = sb("mix_sw", [P, NC_T, 20], F32)
        ffn_sw = sb("ffn_sw", [P, FT, 20], F32)
        stat = sb("stat", [P, 88], F32)
        att_st = sb("att_st", [P, 3, 2], F32)
        sat_st = sb("sat_st", [NS, 4, H], F32)
        eps = sb("eps", [P, 1], F32)
        iwt = sb("iwt", [P, NT, H], F32)
        pts = sb("pts", [1, DEC_B * NPG], I32)
        m8 = sb("m8", [P, 8], F32)

        sizes = [("XA", 2 * KT * T * 2), ("H", NT * D * 4), ("QK", 2 * KT * T * 2), ("QI", 4 * T * 4),
                 ("KI", T * 4), ("CT", 2 * NC_T * T * 2), ("W", 49152), ("SP", 4416)]
        off, at = {}, 0
        for name, size in sizes:
            off[name] = at
            at += size
        arena = sb("arena", [P, at // 4], F32)

        def view(region, shift, shape, dt=F32, parts=P):
            size = {F32: 4, F16: 2, BF16: 2}[dt]
            n = int(np.prod(shape))
            a = (off[region] + shift) // 4
            v = arena[0:parts, a:a + n * size // 4]
            if dt != F32:
                v = v.bitcast(dt)
            if len(shape) == 2:
                v = v.rearrange("p (a b) -> p a b", a=shape[0])
            if len(shape) == 3:
                v = v.rearrange("p (a b c) -> p a b c", a=shape[0], b=shape[1])
            return v

        PS = ctx.enter_context(nc.psum_tensor("PS", [P, 8, 512], F32))

        xa_hi, xa_lo = view("XA", 0, [KT, T], F16), view("XA", KT * T * 2, [KT, T], BF16)
        xb_hi, xb_lo = view("QK", 0, [KT, T], F16), view("QK", KT * T * 2, [KT, T], BF16)
        ct_hi, ct_lo = view("CT", 0, [NC_T, T], F16), view("CT", NC_T * T * 2, [NC_T, T], BF16)
        h = view("H", 0, [NT, D])
        v_hi, v_lo = view("H", 0, [NT, DA], F16), view("H", NT * DA * 2, [NT, DA], BF16)
        v_f32 = gb[:, :].rearrange("p (a b) -> p a b", a=2)
        work = view("H", NT * DA * 4, [4224])
        work_s = view("H", NT * DA * 4 + 4224 * 4, [S_KEYS + 8], parts=NS)
        qT = view("QK", 0, [4, T])
        kT = view("QK", 4 * T * 4, [4, T])
        qi2 = view("QI", 0, [H, SEQ], F16)
        qiT_s = view("QI", H * SEQ * 2, [4, NS])
        ki_hi, ki_lo = view("KI", 0, [SEQ], F16), view("KI", SEQ * 2, [SEQ], F16)
        kiT_s = view("KI", SEQ * 4, [NS])
        raws = [view(r, 0, [3, 512]) for r in ("CT", "QI")]
        rope1s = [view(r, 6144, [512]) for r in ("CT", "QI")]
        rope2s = [view(r, 8192, [512]) for r in ("CT", "QI")]
        ropeds = [view(r, 10240, [3, 512]) for r in ("CT", "QI")]
        squares = view("KI", 0, [512])
        relu = view("CT", 0, [2, SEQ])
        idx_raw = view("CT", 8192, [2 * DEC_B * NPG // 2, P])
        kiTb = view("H", 0, [DEC_B, S_KEYS])
        qi_ht = view("H", 8448, [DEC_B, NS])
        sum_h = view("H", 8448 + 2048, [DEC_B, NS], parts=NS)
        w_relu = view("H", 8448 + 4096, [2, S_KEYS], parts=NS)
        w_sel = view("H", 8448 + 4096 + 2112, [NS], parts=NS)
        w_ht = view("H", 8448 + 4096 + 2112 + 256, [DEC_B], parts=NS)
        c_tt = view("H", 8448 + 4096 + 2112 + 288, [NS], parts=NS)
        c_bb = view("H", 8448 + 4096 + 2112 + 544, [DEC_B], parts=NS)
        cb_s = view("QI", 0, [CW])
        cc_s = view("QI", 4 * CW, [GW])
        ch_s = view("QI", 8 * CW, [CW])
        u_s = view("QI", 12 * CW, [GW])
        tap2 = view("SP", 0, [CW])
        u_state = view("H", NT * DA * 4 + 4224 * 4 + 1088, [NC_T, 18])
        att_sum = view("H", NT * DA * 4 + 4224 * 4 + 1088 + 288, [2, 2, H])
        logit = view("QI", 0, [3, SEQ])
        pT_hi = view("QI", 12288, [2, NB, P], F16)
        pT_lo = view("QI", 16384, [2, NB, P], BF16)
        att_n = gb[:, 0:512]
        kpage = view("SP", 0, [2, DA])
        vpage = gb[:, :].rearrange("p (a b) -> p a b", a=2)
        q_ht = view("QI", 0, [4, DEC_B, NS])
        sel = view("QI", 8192, [DEC_B, NS], parts=NS)
        p_s = view("QI", 10240, [2, S_KEYS], parts=NS)
        pT_s = view("QI", 12352, [2, 3 * NS])
        v_new = view("QI", 13888, [2, DA], parts=DEC_T)
        kTb = view("XA", KT * T * 2 + NC_T * T * 2, [2, 4 * S_KEYS])
        xm_hi, xm_lo = view("QI", 8192, [KT, NMEM], F16), view("QI", 12288, [KT, NMEM], BF16)
        g_src = view("SP", 0, [D])
        memx = view("QI", 0, [2, D])
        mraw = view("QI", 0, [4, 512])
        mtmp = gb[:, 0:512]
        mkT0 = view("XA", KT * T * 2 + NC_T * T * 2, [KT, NMEM])
        mv0 = view("XA", NC_T * T * 2, [2, D])
        mkT = view("QI", 0, [KT, NMEM])
        mv = view("QI", 8192, [2, D])
        qraw = view("CT", 8192, [3, 512])
        qtmp = view("CT", 8192 + 6144, [512])
        mat_st = view("CT", 16384, [2, 4, MH])
        mqT = view("XA", 0, [KT, T])
        mlog = view("CT", 0, [2, D])
        mpT = view("CT", 8192, [2, KT, P])
        mKT = view("W", 0, [2, DEC_B * NMEM])
        mkpages = [view("W", 16384 + 2048 * k, [2, MD]) for k in range(4)] + \
            [view("W", 32768 + 2048 * k, [2, MD]) for k in range(2)]
        MKR = len(mkpages)
        mvpage = view("W", 24576, [4, 2, MD])
        qm_m = view("W", 41472, [2 * 512 + 64])
        mpT_s = view("W", 47616, [2 * NS])
        mp_s = view("W", 48128, [NMEM], parts=NS)
        st_mix = view("QK", 0, [DC], parts=20)
        st_ffn = view("QK", 2048, [DFF], parts=20)
        ffn_hi = view("H", 0, [FT, T], F16)
        ffn_lo = view("H", FT * T * 2, [FT, T], BF16)
        fbase = 2 * FT * T * 2
        gate_s = view("H", fbase, [GW + 6])
        conv_s = view("H", fbase + 4448, [2, GW + 6])
        fst = view("H", fbase + 4448 * 3, [2, KT, P])
        fw_hi = view("H", fbase + 4448 * 3 + 8192, [2, 2, KT * P], F16)
        fw_lo = view("H", fbase + 4448 * 3 + 16384, [2, 2, KT * P], BF16)
        g_state = view("H", fbase + 67088, [FT, 18])
        dst = view("H", fbase + 37920, [2, 11, 256])
        dw_hi = view("XA", 0, [2, FT * 256], F16)
        dw_lo = view("H", fbase + 13344, [2, FT * 256], BF16)
        res = view("XA", 22528, [4, 256])
        outb = view("XA", 22528 + 4096, [4, 256])

        wst = [view("W", 8192 * k, [4, 512]) for k in range(2)]
        w_hi = [view("W", 16384 + 8192 * k, [KT, 512], F16) for k in range(2)]
        w_lo = [view("W", 32768 + 8192 * k, [KT, 512], BF16) for k in range(2)]

        def mask_view(buf, pair):
            return buf[:, pair * 512:pair * 512 + 8 * DIAG].rearrange("p (b c) -> p b c", c=DIAG)[:, :, 0:DEC_T]

        class Weights:

            def __init__(self, name, chunks, used):
                self.name, self.chunks, self.used = name, chunks, used

            def n(self, what):
                return f"{self.name}_{what}"

            def s(self, what):
                return sem(self.n(what))

            def load(self, e, n):
                src, width = self.chunks[n]
                for half in range(2):
                    if n >= 1:
                        e.wait_ge(sem(self.n("lo")), upto(self.n("lo"), 2 * (n - 1) + half + 1))
                    parts = src if isinstance(src, list) else [src]
                    c = 0
                    for k, part in enumerate(parts):
                        w = part.shape[1]
                        e.dma_start(wst[half][:, :, c:c + w],
                                    part.rearrange("(k p) n -> p k n", p=P)[:, 4 * half:4 * half + 4, :]
                                    ).then_inc(self.s(f"ld{half}"), 16)
                        c += w

            def split_hi(self, e, n):
                if n >= len(self.chunks):
                    return
                src, width = self.chunks[n]
                loads = sum(len(c[0]) if isinstance(c[0], list) else 1 for c in self.chunks[:n + 1])
                if n >= 2:
                    name, count = self.used(n - 2)
                    e.wait_ge(sem(name), upto(name, count))
                for half in range(2):
                    e.wait_ge(sem(self.n(f"ld{half}")), upto(self.n(f"ld{half}"), 16 * loads))
                    e.activation(w_hi[n % 2][:, 4 * half:4 * half + 4, 0:width], wst[half][:, :, 0:width],
                                 ACT.Copy).then_inc(self.s("hi"), 1)

            def split_lo(self, e, n, halves=(0, 1)):
                src, width = self.chunks[n]
                for half in halves:
                    e.wait_ge(sem(self.n("hi")), upto(self.n("hi"), 2 * n + half + 1))
                    e.tensor_tensor(w_lo[n % 2][:, 4 * half:4 * half + 4, 0:width], wst[half][:, :, 0:width],
                                    w_hi[n % 2][:, 4 * half:4 * half + 4, 0:width],
                                    ALU.subtract).then_inc(self.s("lo"), 1)

            def ready(self, e, n):
                e.wait_ge(sem(self.n("lo")), upto(self.n("lo"), 2 * (n + 1)))

        w_in, w_out = io["w_in"][0], io["w_out"][0]
        w_kv, w_q, w_o = io["w_kv_mem"][0], io["w_q_mem"][0], io["w_o_mem"][0]
        w_gu, w_down = io["w_gu"][0], io["w_down"][0]

        A_QI, A_KI, A_CONV, A_V, A_Q, A_K = 0, 1, 2, 6, 7, 8
        A = Weights("wa", [(w_in[:, QIB:QIB + 512], 512), (w_in[:, KIB:D_IN], D_IN - KIB)]
                    + [([w_in[:, g * DC + f * P:g * DC + (f + 1) * P] for g in range(3)], 3 * P)
                       for f in range(NC_T)]
                    + [(w_in[:, a:a + 512], 512) for a in (VB, QB, KB)],
                    lambda n: ("s2_mm", NT * (n + 1)) if n < 2 else
                    ("s4_mm", NT * (n - 1)) if n < 7 else ("s2_mm", NT * (n - 4)))
        B = Weights("wb", [(w_kv[:, c * 512:c * 512 + 512], 512) for c in range(4)]
                    + [(w_out[:, c * 512:c * 512 + 512], 512) for c in range(2)]
                    + [(w_q[:, c * 512:c * 512 + 512], 512) for c in range(2)],
                    lambda n: ("mkv_mm", 2 * (n + 1)) if n < 4 else ("l6_mm", NT * (n - 3)) if n < 6 else ("q7_mm", NT * (n - 5)))
        C = Weights("wc", [(w_o[:, c * 512:c * 512 + 512], 512) for c in range(2)], None)

        class Norm:
            def __init__(self, name, tiles, src, hi, lo, ready, junk=None, gain=None):
                self.junk = junk
                self.gain = gb if gain is None else gain
                self.name, self.tiles, self.src, self.hi, self.lo, self.ready = name, tiles, src, hi, lo, ready

            def n(self, what):
                return f"{self.name}_{what}"

            def s(self, what):
                return sem(self.n(what))

            def bank(self, j):
                return 4 + 2 * (j % 2)

            def act_root(self, e, j):
                n = self.tiles[j]
                self.ready(e, j)
                b = self.bank(j)
                if self.junk is None:
                    out = PS[0:n, b:b + 2, :].rearrange("p a b -> p (a b)")
                    if j >= 2:
                        e.wait_ge(sem(self.n("lo")), upto(self.n("lo"), j - 1))
                else:
                    out = self.junk[0:n, :]
                e.activation(out, self.src(j), ACT.Square,
                             accum_out=stat[0:n, j:j + 1]).then_inc(self.s("ss"), 1)
                e.wait_ge(sem(self.n("ss")), upto(self.n("ss"), j + 1))
                e.activation(stat[0:n, 16 + j:17 + j], stat[0:n, j:j + 1], ACT.Sqrt, bias=eps[0:n, :],
                             scale=1.0 / D).then_inc(self.s("rt"), 1)

            def dve_norm(self, e, j, out):
                n = self.tiles[j]
                e.wait_ge(sem(self.n("rt")), upto(self.n("rt"), j + 1))
                e.reciprocal(stat[0:n, 32 + j:33 + j], stat[0:n, 16 + j:17 + j]).then_inc(self.s("rc"), 1)
                e.wait_ge(sem(self.n("rc")), upto(self.n("rc"), j + 1))
                e.scalar_tensor_tensor(out(j), self.src(j), stat[0:n, 32 + j:33 + j], self.gain[0:n, :],
                                       ALU.mult, ALU.mult).then_inc(self.s("xn"), 1)

            def pe_turn(self, e, j, out):
                n = self.tiles[j]
                b = self.bank(j)
                e.wait_ge(sem(self.n("xn")), upto(self.n("xn"), j + 1))
                if self.junk is not None and j >= 2:
                    e.wait_ge(sem(self.n("lo")), upto(self.n("lo"), j - 1))
                for k in range(KT):
                    t = e.transpose(PS[:, b + k // 4, (k % 4) * P:(k % 4) * P + n], out(j)[:, k * P:(k + 1) * P],
                                    ident[0:n, 0:n])
                t.then_inc(self.s("tp"), 1)

            def parts(self, j):
                n = self.tiles[j]
                b = self.bank(j)
                t = PS[:, b:b + 2, :].rearrange("p a (c q) -> p (a c) q", q=P)[:, :, 0:n]
                return t, self.hi[:, :, j * P:j * P + n], self.lo[:, :, j * P:j * P + n]

            def act_hi(self, e, j):
                e.wait_ge(sem(self.n("tp")), upto(self.n("tp"), j + 1))
                t, hi, lo = self.parts(j)
                e.activation(hi, t, ACT.Copy).then_inc(self.s("hi"), 1)

            def dve_lo(self, e, j):
                e.wait_ge(sem(self.n("hi")), upto(self.n("hi"), j + 1))
                t, hi, lo = self.parts(j)
                e.tensor_tensor(lo, t, hi, ALU.subtract).then_inc(self.s("lo"), 1)

        tiles = [rows(j) for j in range(NT)]
        N1 = Norm("n1", tiles, lambda j: h[0:rows(j), j, :], xa_hi, xa_lo,
                  lambda e, j: e.wait_ge(sem(f"x_ld{x_group(j)}"), 16 if j < 3 else 48),
                  view("QK", 13312, [D]))

        block = ctx.enter_context(nc.Block())
        new_k = [io["o_kp"][0, 0].rearrange("t h d -> t (h d)"), io["o_ks"][0].rearrange("b t h d -> (b t) (h d)")]
        new_v = [io["o_vp"][0, 0].rearrange("t h d -> t (h d)"), io["o_vs"][0].rearrange("b t h d -> (b t) (h d)")]
        new_ki = [io["o_ikp"][0, 0], io["o_iks"][0].rearrange("b t d -> (b t) d")]
        xs = io["x_sample"].rearrange("b t d -> (b t) d")
        ys = io["o_ys"].rearrange("b t d -> (b t) d")

        def dram_rows(pair, j):
            return pair[0][j * P:(j + 1) * P, :] if j < NB else pair[1]

        ITEMS = [(c, j) for c in (A_QI, A_KI, A_Q, A_K) for j in range(NT)]
        NI = len(ITEMS)
        NI1 = 2 * NT
        STORED = [k for k, (c, j) in enumerate(ITEMS) if c in (A_KI, A_K)]

        def group(L):
            return 0 if L < NI1 else 1

        def stores_of_slot(k):
            return len([m for m in STORED if m % 3 == k % 3 and m < k])

        def split_items(L):
            return len([k for k in range(L) if k < NI1 and ITEMS[k][1] < NB])

        DOTS = [(i, hh) for i in range(2, NB) for hh in range(H)]
        ND = len(DOTS)
        L4 = [("c", f, t, g) for f in range(NC_T) for t in range(3) for g in range(3)] + [("v", j) for j in range(NT)]
        N4C = NC_T * 9
        ATT = [(i, hh) for i in range(NB) for hh in range(H)]
        NA = len(ATT)
        UNITS, units_of, out_unit = [], {}, {}
        for m in range(NA + 4):
            if 2 <= m < NA + 2:
                i = ATT[m - 2][0]
                units_of[m - 2] = []
                for c in range(0, i + 1, 4):
                    units_of[m - 2].append(len(UNITS))
                    UNITS.append((m - 2, c, min(i + 1, c + 4)))
            if m >= 4 and ATT[m - 4][1] == H - 1:
                out_unit[ATT[m - 4][0]] = len(UNITS)
                UNITS.append(("out", ATT[m - 4][0]))

        B_KV, B_OUT, B_Q = 0, 4, 6

        L6 = [(c, j) for c in range(2) for j in range(NT)]
        N2 = Norm("n2", tiles, lambda j: h[0:rows(j), j, :], xb_hi, xb_lo, None)
        N3 = Norm("n3", tiles, lambda j: h[0:rows(j), j, :], xa_hi, xa_lo, None)
        NM = Norm("nm", [P, P], lambda j: memx[:, j, :], xm_hi, xm_lo,
                  lambda e, j: e.wait_ge(sem("memx_ld"), 32), junk=view("KI", 1024, [D], BF16), gain=g_src)
        xnorm = view("QI", 0, [2, D])
        xnorm2 = view("XA", KT * T * 2 + NC_T * T * 2, [2, D])
        mixst = view("KI", 1024, [DC], parts=18)
        ffnst = view("H", fbase, [DFF], parts=18)
        h3 = nc.dram_tensor("h3_scratch", [T, D], F32, kind="Internal").ap()
        FIRSTS, CONSTS = 4, 13

        def down_store(e, c):
            for j in range(NT):
                n = c * NT + j
                e.wait_ge(sem("down_ev"), n + 1)
                dstv = io["o_yp"][0, j * P:(j + 1) * P, c * 256:(c + 1) * 256] if j < NB else ys[:, c * 256:(c + 1) * 256]
                e.dma_start(dstv, outb[0:rows(j), n % 4, :]).then_inc(sem(f"y_st{n % 4}"), 16)

        @block.sync
        def _(e):
            def const(dst, src):
                e.dma_start(dst, src).then_inc(sem("const"), 16)

            def first(dst, src):
                e.dma_start(dst, src).then_inc(sem("first"), 16)

            A.load(e, 0)
            for j in range(NT):
                e.dma_start(h[0:rows(j), j, :], dram_rows([io["x_prompt"][0], xs], j)).then_inc(sem(f"x_ld{x_group(j)}"), 16)
                if j == 0:
                    first(gb[:, :], io["g_mix"].broadcast_to([P, D]))
                    first(ident[:, :], io["c_ident"])
                if j == 1:
                    first(cos_t[:, :, :], io["c_cos"].rearrange("(j p) d -> p j d", p=P))
                    first(sin_t[:, :, :], io["c_sin"].rearrange("(j p) d -> p j d", p=P))
            A.load(e, 1)
            const(mask01[:, :], io["c_mask"])
            const(smask[0:NS, :], io["c_smask"])
            const(qkg[:, 0, :], io["q_norm_g"].broadcast_to([P, HD]))
            const(qkg[:, 1, :], io["k_norm_g"].broadcast_to([P, HD]))
            const(mqkg[:, 0, :], io["mq_norm_g"].broadcast_to([P, MD]))
            const(mqkg[:, 1, :], io["mk_norm_g"].broadcast_to([P, MD]))
            const(st_mix[0:16, :], io["state_conv_mix"][0].rearrange("b t d -> (b t) d"))
            const(st_mix[16:19, :], io["conv_mix_w"][0])
            const(st_mix[19:20, :], io["conv_mix_w"][0, 0:1, :])
            const(st_ffn[0:16, :], io["state_conv_ffn"][0].rearrange("b t d -> (b t) d"))
            const(st_ffn[16:19, :], io["conv_ffn_w"][0])
            const(st_ffn[19:20, :], io["conv_ffn_b"])
            const(pts[:, :], io["page_table"].rearrange("a b -> (a b)")[None, :])
            def store_roped(c):
                for k in STORED:
                    if ITEMS[k][0] == c:
                        j = ITEMS[k][1]
                        n = rows(j)
                        e.wait_ge(sem("s2_roped"), k + 1)
                        src = ropeds[group(k)]
                        if c == A_K:
                            e.dma_start(dram_rows(new_k, j), src[0:n, k % 3, :]).then_inc(sem(f"s2_st{k % 3}"), 16)
                        else:
                            e.dma_start(dram_rows(new_ki, j), src[0:n, k % 3, 0:HD]).then_inc(sem(f"s2_st{k % 3}"), 16)

            A.load(e, 2)
            e.wait_ge(sem("n1_lo"), NT)
            e.dma_start(sum_h[:, :, :], io["c_sum"]).then_inc(sem("selc"), 16)
            e.dma_start(c_tt[:, :], io["c_tt"]).then_inc(sem("selc"), 16)
            e.dma_start(c_bb[:, :], io["c_bb"]).then_inc(sem("selc"), 16)
            store_roped(A_KI)
            A.load(e, 3)
            e.wait_ge(sem("const"), 16 * CONSTS)
            pages = [e.value_load(pts[0:1, n:n + 1], min_val=0, max_val=N_POOL - 1) for n in range(DEC_B * NPG)]
            e.wait_ge(sem("s2_tp"), NI1)
            for k in range(3):
                e.wait_ge(sem(f"s2_st{k}"), 16 * len([m for m in STORED if m % 3 == k and m < NI1]))
            for n, page in enumerate(pages):
                for twice in range(2):
                    e.dma_start(idx_raw[:, n, twice * HD:(twice + 1) * HD],
                                io["cache_idx_k"][0][bass.ds(page, 1)].rearrange("a p d -> (a p) d")
                                ).then_inc(sem("idx_ld"), 16)
            for n in range(4, 9):
                A.load(e, n)
            for j in range(NT):
                e.wait_ge(sem("v_f32"), j + 1)
                e.dma_start(dram_rows(new_v, j), v_f32[0:rows(j), j % 2, :]).then_inc(sem(f"v_st{j % 2}"), 16)
            def key_page(n):
                if n >= 2:
                    e.wait_ge(sem("kb_tp"), n - 1)
                else:
                    e.wait_ge(sem("conv_lo"), NC_T)
                e.dma_start(kpage[:, n % 2, :],
                            io["cache_k"][0][bass.ds(pages[n], 1)].rearrange("a p h d -> (a p) (h d)")
                            ).then_inc(sem(f"kb_ld{n % 2}"), 16)

            key_page(0)
            key_page(1)
            for k in range(2):
                e.wait_ge(sem(f"v_st{k}"), 16 * len(range(k, NT, 2)))
            e.wait_ge(sem("v_lo"), NT)

            def value_page(n):
                b = n // 2
                if b >= 1:
                    e.wait_ge(sem("sv_used"), b)
                e.dma_start(vpage[:, n % 2, :],
                            io["cache_v"][0][bass.ds(pages[n], 1)].rearrange("a p h d -> (a p) (h d)")
                            ).then_inc(sem(f"vb_ld{n % 2}"), 16)

            def new_values(b):
                if b >= 2:
                    e.wait_ge(sem("sv_used"), b - 1)
                e.dma_start(v_new[0:DEC_T, b % 2, :], new_v[1][b * DEC_T:(b + 1) * DEC_T, :]
                            ).then_inc(sem(f"vn_ld{b % 2}"), 16)

            value_page(0)
            value_page(1)
            store_roped(A_K)
            e.wait_ge(sem("s2_tp"), NI)
            for k in range(3):
                e.wait_ge(sem(f"s2_st{k}"), 16 * len([m for m in STORED if m % 3 == k]))
            e.dma_start(sel[:, :, :], io["c_sel"]).then_inc(sem("sel_ld"), 16)
            new_values(0)
            new_values(1)
            e.wait_ge(sem("mixst_ev"), 1)
            e.dma_start(io["o_cmp"][0, 0], mixst[16:18, :]).then_inc(sem("st_out"), 16)
            e.dma_start(io["o_cms"][0].rearrange("b t d -> (b t) d"), mixst[0:16, :]).then_inc(sem("st_out"), 16)
            B.load(e, 0)
            for n in range(2, 6):
                key_page(n)
            for b in range(1, DEC_B):
                if b + 2 < DEC_B:
                    key_page(2 * b + 4)
                    key_page(2 * b + 5)
                if b == DEC_B - 1:
                    e.wait_ge(sem("kb_tp"), DEC_B * NPG)
                    e.dma_start(g_src[:, :], io["g_mem_src"].broadcast_to([P, D])).then_inc(sem("g_ld"), 16)
                    e.wait_ge(sem("sa_qk"), DEC_B)
                    for j in range(2):
                        e.dma_start(memx[:, j, :], io["mem_prompt"][0, j * P:(j + 1) * P, :]).then_inc(sem("memx_ld"), 16)
                value_page(2 * b)
                value_page(2 * b + 1)
                if b >= 2:
                    new_values(b)
                if b == 2:
                    B.load(e, 1)
            B.load(e, 2)
            B.load(e, 3)
            for it in range(4):
                c, j = it // 2, it % 2
                e.wait_ge(sem("mk_out"), it + 1)
                e.dma_start(io["o_mk"][0, 0, j * P:(j + 1) * P].rearrange("t h d -> t (h d)")[:, c * 512:(c + 1) * 512],
                            mraw[:, it, :]).then_inc(sem("mk_st"), 16)
            for it in range(4):
                c, j = it // 2, it % 2
                e.wait_ge(sem("mkv_ev"), 4 + it + 1)
                e.dma_start(io["o_mv"][0, 0, j * P:(j + 1) * P].rearrange("t h d -> t (h d)")[:, c * 512:(c + 1) * 512],
                            mv0[:, j, c * 512:(c + 1) * 512]).then_inc(sem("mv_st"), 16)
            for n in range(4, 7):
                B.load(e, n)
            e.wait_ge(sem("at_ulo"), len(UNITS))
            e.dma_start(gb[:, :], io["g_mem"].broadcast_to([P, D])).then_inc(sem("g_ld"), 16)
            for j in range(NT):
                e.dma_start(h[0:rows(j), j, :], dram_rows([io["x_prompt"][0], xs], j)
                            ).then_inc(sem(f"x2_ld{x_group(j)}"), 16)
            B.load(e, 7)
            e.wait_ge(sem("q7_mm"), upto("q7_mm", NT))
            for s in range(NB + 2):
                for n in range(4 * s + 2 if s else 0, 4 * s + 6):
                    if n < MH * DEC_B:
                        if n >= MKR:
                            e.wait_ge(sem("mkb_tp"), upto("mkb_tp", n - MKR + 1))
                        e.dma_start(mkpages[n % MKR],
                                    io["cache_mem_k"][0, n % DEC_B, :, n // DEC_B, :].rearrange("(c p) d -> p c d", p=P)
                                    ).then_inc(sem(f"mkb_ld{n % MKR}"), 16)
                if s == 0:
                    e.wait_ge(sem("q7_mm"), upto("q7_mm", 2 * NT))
                    e.wait_ge(sem("n2_xn"), upto("n2_xn", NT))
                    e.dma_start(gb[:, :], io["g_ffn"].broadcast_to([P, D])).then_inc(sem("g_ld"), 16)
                if s == NB + 1:
                    e.wait_ge(sem("ms_qk"), MH)
                    C.load(e, 0)
                for n in range(4 * (s - 2), 4 * (s - 2) + 4):
                    if n >= 0:
                        if n >= 4:
                            e.wait_ge(sem("mvb_used"), n - 3)
                        e.dma_start(mvpage[:, n % 4, :, :],
                                    io["cache_mem_v"][0, n % DEC_B, :, n // DEC_B, :].rearrange("(c p) d -> p c d", p=P)
                                    ).then_inc(sem(f"mvb_ld{n % 4}"), 16)
            C.load(e, 1)
            def gate_up_load(n):
                f, g = n // 2, n % 2
                if n >= 2:
                    e.wait_ge(sem("fw_lo"), n - 1)
                e.dma_start(fst[:, g, :, :],
                            w_gu[:, g * DFF + f * P:g * DFF + (f + 1) * P].rearrange("(k p) n -> p k n", p=P)
                            ).then_inc(sem(f"fw_ld{g}"), 16)

            C.ready(e, 1)
            gate_up_load(0)
            gate_up_load(1)
            for j in range(NT):
                e.wait_ge(sem("l8_ev"), upto("l8_ev", NT + j + 1))
                e.dma_start(h3[j * P:j * P + rows(j), :], h[0:rows(j), j, :]).then_inc(sem("h3_st"), 16)
            e.wait_ge(sem("h3_st"), 16 * NT)
            e.wait_ge(sem("n3_lo"), upto("n3_lo", NT))
            for n in range(2, 2 * FT):
                gate_up_load(n)
            for c in range(4):
                for half in range(2):
                    if c == 1:
                        e.wait_ge(sem("dw_lo_first"), half + 1)
                    if c >= 2:
                        e.wait_ge(sem("dw_lo"), upto("dw_lo", 2 * (c - 2) + half + 1))
                    e.dma_start(dst[:, half, :, :],
                                w_down[half * 11 * P:(half + 1) * 11 * P, c * 256:(c + 1) * 256]
                                .rearrange("(k p) n -> p k n", p=P)).then_inc(sem(f"dw_ld{half}"), 16)
                if c == 0:
                    continue
                down_store(e, c - 1)
            down_store(e, 3)
            e.wait_ge(sem("ffnst_ev"), upto("ffnst_ev", 1))
            e.dma_start(io["o_cfp"][0, 0], ffnst[16:18, :]).then_inc(sem("st_out"), 16)
            e.dma_start(io["o_cfs"][0].rearrange("b t d -> (b t) d"), ffnst[0:16, :]).then_inc(sem("st_out"), 16)
            e.wait_ge(sem("st_out"), 64)
            for k in range(4):
                e.wait_ge(sem(f"y_st{k}"), upto(f"y_st{k}", 16 * 9))
            for k in range(2):
                e.wait_ge(sem(f"v_st{k}"), 16 * len(range(k, NT, 2)))
            for k in range(3):
                e.wait_ge(sem(f"s2_st{k}"), 16 * len([m for m in STORED if m % 3 == k]))
            e.wait_ge(sem("mk_st"), 64)
            e.wait_ge(sem("mv_st"), 64)

        def own_half(odd):
            v = qi2.rearrange("p (a two) t -> p a two t", two=2)
            return v[HD * odd:HD * (odd + 1), :, odd, :]

        def other_half(odd):
            v = qi2.rearrange("p (a two) t -> p a two t", two=2)
            return v[HD * (1 - odd):HD * (2 - odd), :, odd, :]

        def down_lo(e, c):
            for half in range(2):
                a = slice(half * 11 * 256, (half + 1) * 11 * 256)
                e.wait_ge(sem("dw_hi"), upto("dw_hi", 2 * c + half + 1))
                e.tensor_tensor(dw_lo[:, c % 2, a], dst[:, half, :, :].rearrange("p a b -> p (a b)"),
                                dw_hi[:, c % 2, a], ALU.subtract
                                ).then_inc(sem("dw_lo_first" if c == 0 else "dw_lo"), 1)

        def chain(e, ins, name, count):
            ins.then_inc(sem(name), 1)
            count[0] += 1
            e.wait_ge(sem(name), upto(name, count[0]))

        def lin(e, out, x_hi, x_lo, wh, wl, ks, cols):
            n = len(ks)
            for q, k in enumerate(ks):
                e.matmul(out, x_hi(k)[:, cols], wh[:, q, :], start=(q == 0), stop=False)
                e.matmul(out, x_lo(k)[:, cols], wh[:, q, :], start=False, stop=False)
                mm = e.matmul(out, x_hi(k)[:, cols], wl[:, q, :], start=False, stop=(q == n - 1))
            return mm

        def tcols(j):
            return slice(j * P, j * P + rows(j))

        @block.tensor
        def _(e):
            e.wait_ge(sem("first"), 16 * FIRSTS)

            def turn_item(L):
                c, j = ITEMS[L]
                n = rows(j)
                e.wait_ge(sem("s2_roped"), L + 1)
                if L >= 2:
                    e.wait_ge(sem("s2_te"), L - 1)
                    e.wait_ge(sem("s2_lo"), min(split_items(L - 1), split_items(NI1)))
                for p in range(1 if c == A_KI else 4):
                    t = e.transpose(PS[:, 2 + L % 2, p * P:p * P + n],
                                    ropeds[group(L)][0:n, L % 3, p * P:(p + 1) * P], ident[0:n, 0:n])
                t.then_inc(sem("s2_tp"), 1)

            def project_items(first, end):
                for step in range(first, end + 5):
                    if 1 <= step <= NT:
                        N1.pe_turn(e, step - 1, lambda j: h[0:rows(j), j, :])
                    L = step - 3
                    if first <= L < end:
                        c, j = ITEMS[L]
                        if j == 0:
                            A.ready(e, c)
                        if L < NT:
                            e.wait_ge(sem("n1_lo"), j + 1)
                        if L >= first + 2:
                            e.wait_ge(sem("s2_raw"), L - 1)
                        w = A.chunks[c][1]
                        mm = lin(e, PS[0:rows(j), L % 2, 0:w], lambda k: xa_hi[:, k, :], lambda k: xa_lo[:, k, :],
                                 w_hi[c % 2][:, :, 0:w], w_lo[c % 2][:, :, 0:w], range(KT), tcols(j))
                        mm.then_inc(sem("s2_mm"), 1)
                    if step - 5 >= first:
                        turn_item(step - 5)

            project_items(0, NI1)
            e.wait_ge(sem("const"), 16 * CONSTS)
            e.wait_ge(sem("n1_lo"), NT)
            for f in range(NC_T):
                e.transpose(PS[:, 6, f * 20:f * 20 + 20], st_mix[:, f * P:(f + 1) * P], ident[0:20, 0:20])
            for f in range(FT):
                t = e.transpose(PS[:, 7, f * 20:f * 20 + 20], st_ffn[:, f * P:(f + 1) * P], ident[0:20, 0:20])
            t.then_inc(sem("st_tp"), 1)

            e.wait_ge(sem("s2_raw"), NI1)
            e.wait_ge(sem("s2_te"), NI1)
            e.wait_ge(sem("s2_lo"), split_items(NI1))
            for m, (i, hh) in enumerate(DOTS):
                if m >= 2:
                    e.wait_ge(sem("s3_relu"), m - 1)
                r = slice((hh % 2) * HD, (hh % 2 + 1) * HD)
                n = (i + 1) * P
                for a in range(0, n, 512):
                    b = min(n, a + 512)
                    out = PS[:, 2 * (m % 2) + a // 512, 0:b - a]
                    e.matmul(out, qi2[:, hh, i * P:(i + 1) * P], ki_hi[:, a:b], start=True, stop=False)
                    mm = e.matmul(out, qi2[r, hh, i * P:(i + 1) * P], ki_lo[r, a:b], start=False, stop=True)
                mm.then_inc(sem("s3_mm"), 1)
            e.wait_ge(sem("idx_ld"), 16 * 2 * DEC_B * NPG)
            e.wait_ge(sem("st_ev"), 2)
            for n in range(DEC_B * NPG):
                t = e.transpose(PS[:, 4 + n // 4, (n % 4) * P:(n % 4 + 1) * P], idx_raw[:, n, :], ident[:, :])
            t.then_inc(sem("ik_tp"), 1)
            e.wait_ge(sem("w_sel"), 1)
            e.wait_ge(sem("s3_relu"), ND)
            e.matmul(PS[0:NS, 0, 0:DEC_B], w_sel[:, :], c_bb[:, :], start=True, stop=True).then_inc(sem("w_mm"), 1)
            e.wait_ge(sem("ik_ev"), 2)
            e.wait_ge(sem("qi_ht"), 9)
            for b in range(DEC_B + 2):
                if b < DEC_B:
                    if b >= 2:
                        e.wait_ge(sem("w_relu"), b - 1)
                    e.matmul(PS[0:NS, 1 + b % 2, 0:S_KEYS], qi_ht[:, b, :], kiTb[:, b, :], start=True, stop=True
                             ).then_inc(sem("sd_mm"), 1)
                if b >= 1 and b - 1 < DEC_B:
                    e.wait_ge(sem("w_relu"), b)
                    e.matmul(PS[0:NS, 3, 0:S_KEYS], sum_h[:, b - 1, :], w_relu[:, (b - 1) % 2, :], start=(b == 1),
                             stop=(b == DEC_B)).then_inc(sem("sd_sum"), 1)

            e.wait_ge(sem("w_relu"), DEC_B)
            e.wait_ge(sem("ws_ev"), 1)
            for x, item in enumerate(L4):
                if x >= 8:
                    e.wait_ge(sem("s4_ev"), x - 7)
                if item[0] == "v":
                    j = item[1]
                    if j == 0:
                        A.ready(e, A_V)
                    mm = lin(e, PS[0:rows(j), x % 8, :], lambda k: xa_hi[:, k, :], lambda k: xa_lo[:, k, :],
                             w_hi[A_V % 2], w_lo[A_V % 2], range(KT), tcols(j))
                else:
                    _, f, t, g = item
                    c = A_CONV + f
                    if t == 0 and g == 0:
                        A.ready(e, c)
                    t0, tn = token_chunks()[t]
                    for k in range(KT):
                        wh, wl = (w[c % 2][:, k, g * P:(g + 1) * P] for w in (w_hi, w_lo))
                        xh, xl = xa_hi[:, k, t0:t0 + tn], xa_lo[:, k, t0:t0 + tn]
                        out = PS[:, x % 8, 0:tn]
                        e.matmul(out, wh, xh, start=(k == 0), stop=False)
                        e.matmul(out, wh, xl, start=False, stop=False)
                        mm = e.matmul(out, wl, xh, start=False, stop=(k == KT - 1))
                mm.then_inc(sem("s4_mm"), 1)
            e.wait_ge(sem("s4_ev"), len(L4))
            project_items(NI1, NI)
            e.wait_ge(sem("s2_raw"), NI)
            e.wait_ge(sem("s2_te"), NI)
            e.wait_ge(sem("conv_lo"), NC_T)
            for f in range(NC_T):
                t = e.transpose(PS[0:18, 7, f * P:(f + 1) * P], u_state[:, f, :], ident[:, :])
            t.then_inc(sem("mixst_tp"), 1)

            def turn_keys(b):
                for pg in range(NPG):
                    n = 2 * b + pg
                    e.wait_ge(sem(f"kb_ld{pg}"), 16 * (b + 1))
                    if b >= 1:
                        e.wait_ge(sem("kb_ev"), n - 1)
                    for p in range(4):
                        t = e.transpose(PS[:, 2 + pg, p * P:(p + 1) * P], kpage[:, pg, p * P:(p + 1) * P], ident[:, :])
                    t.then_inc(sem("kb_tp"), 1)

            def sample_scores(b):
                e.wait_ge(sem("kb_ev"), 2 * b + 2)
                e.wait_ge(sem("kb_new"), b + 1)
                if b >= 2:
                    e.wait_ge(sem("sa_exp"), b - 1)
                out = PS[0:NS, b % 2, 0:S_KEYS]
                e.matmul(out, sel[:, b, :], work_s[:, 0:S_KEYS], start=True, stop=False)
                for p in range(4):
                    mm = e.matmul(out, q_ht[:, p, b, :], kTb[:, b % 2, p * S_KEYS:(p + 1) * S_KEYS],
                                  start=False, stop=(p == 3))
                mm.then_inc(sem("sa_qk"), 1)

            def sample_turn_probs(b):
                e.wait_ge(sem("sa_p"), b + 1)
                if b >= 1:
                    e.wait_ge(sem("sa_pte"), 2 * b)
                for c in range(3):
                    w = min(P, S_KEYS - c * P)
                    t = e.transpose(PS[0:w, 4, c * NS:(c + 1) * NS], p_s[:, b % 2, c * P:c * P + w], ident[0:NS, 0:NS])
                t.then_inc(sem("sa_tt"), 1)

            def sample_values(b):
                e.wait_ge(sem("sa_pte"), 2 * b + 2)
                e.wait_ge(sem(f"vn_ld{b % 2}"), 16 * (b // 2 + 1))
                for s in range(2):
                    e.wait_ge(sem(f"vb_ld{s}"), 16 * (b + 1))
                for hh in range(H):
                    r = slice((hh % 2) * HD, (hh % 2 + 1) * HD)
                    out = PS[r, 5, (hh // 2) * NS + b * DEC_T:(hh // 2) * NS + (b + 1) * DEC_T]
                    d = slice(hh * HD, (hh + 1) * HD)
                    q = [slice(c * NS + hh * DEC_T, c * NS + (hh + 1) * DEC_T) for c in range(3)]
                    e.matmul(out, vpage[:, 0, d], pT_s[:, b % 2, q[0]], start=True, stop=False)
                    e.matmul(out, vpage[:, 1, d], pT_s[:, b % 2, q[1]], start=False, stop=False)
                    mm = e.matmul(out, v_new[0:DEC_T, b % 2, d], pT_s[0:DEC_T, b % 2, q[2]], start=False, stop=True)
                mm.then_inc(sem("sv_used"), 1)

            e.wait_ge(sem("q_ht"), 9)
            e.wait_ge(sem("topk"), 1)
            e.wait_ge(sem("sel_ld"), 16)
            for b in range(DEC_B + 2):
                if b < DEC_B:
                    turn_keys(b)
                    sample_scores(b)
                if 1 <= b <= DEC_B:
                    sample_turn_probs(b - 1)
                if b >= 2:
                    sample_values(b - 2)
            e.wait_ge(sem("sa_lo"), 1)
            e.wait_ge(sem("mixst_ev"), 1)

            for j in range(2):
                NM.pe_turn(e, j, lambda j: memx[:, j, :])
            for it in range(8):
                c, j = it // 2, it % 2
                if j == 0:
                    B.ready(e, B_KV + c)
                if it == 0:
                    e.wait_ge(sem("nm_lo"), upto("nm_lo", 2))
                if it >= 4:
                    e.wait_ge(sem("mkv_ev"), it - 3)
                mm = lin(e, PS[:, it % 4, :], lambda k: xm_hi[:, k, :], lambda k: xm_lo[:, k, :],
                         w_hi[c % 2], w_lo[c % 2], range(KT), tcols(j))
                mm.then_inc(sem("mkv_mm"), 1)
                if it >= 4:
                    q = it - 4
                    c, j = q // 2, q % 2
                    e.wait_ge(sem("mk_out"), q + 1)
                    if q >= 2:
                        e.wait_ge(sem("mk_te"), q - 1)
                    for p in range(4):
                        t = e.transpose(PS[:, 4 + q % 2, p * P:(p + 1) * P], mraw[:, q, p * P:(p + 1) * P], ident[:, :])
                    t.then_inc(sem("mk_tp"), 1)
            e.wait_ge(sem("mkv_ev"), 8)
            e.wait_ge(sem("mk_te"), 4)

            def scores(m):
                i, hh = ATT[m]
                if m >= 2:
                    e.wait_ge(sem("at_max"), m - 1)
                r = slice((hh % 2) * HD, (hh % 2 + 1) * HD)
                n = (i + 1) * P
                for a in range(0, n, 512):
                    b = min(n, a + 512)
                    mm = e.matmul(PS[:, 2 * (m % 2) + a // 512, 0:b - a], qT[r, hh // 2, i * P:(i + 1) * P],
                                  kT[r, hh // 2, a:b], start=True, stop=True)
                mm.then_inc(sem("at_qk"), 1)

            def turn_probs(m):
                e.wait_ge(sem("at_exp"), m + 1)
                for u in units_of[m]:
                    _, c0, c1 = UNITS[u]
                    if u >= 3:
                        e.wait_ge(sem("at_ulo"), u - 2)
                    for c in range(c0, c1):
                        t = e.transpose(PS[:, 4 + u % 3, (c - c0) * P:(c - c0 + 1) * P],
                                        logit[:, m % 3, c * P:(c + 1) * P], ident[:, :])
                    t.then_inc(sem("at_tt"), 1)

            def values(m):
                i, hh = ATT[m]
                e.wait_ge(sem("at_ulo"), units_of[m][-1] + 1)
                if hh == 0 and i >= 1:
                    e.wait_ge(sem("at_n"), i)
                out, d = PS[:, 7, hh * HD:(hh + 1) * HD], slice(hh * HD, (hh + 1) * HD)
                for c in range(i + 1):
                    e.matmul(out, pT_hi[:, m % 2, c, :], v_hi[:, c, d], start=(c == 0), stop=False)
                    e.matmul(out, pT_lo[:, m % 2, c, :], v_hi[:, c, d], start=False, stop=False)
                    mm = e.matmul(out, pT_hi[:, m % 2, c, :], v_lo[:, c, d], start=False, stop=(c == i))
                mm.then_inc(sem("at_pv"), 1)

            def turn_output(i):
                e.wait_ge(sem("at_n"), i + 1)
                u = out_unit[i]
                e.wait_ge(sem("at_ulo"), u - 2)
                for p in range(4):
                    t = e.transpose(PS[:, 4 + u % 3, p * P:(p + 1) * P], att_n[:, p * P:(p + 1) * P], ident[:, :])
                t.then_inc(sem("at_tt"), 1)

            e.wait_ge(sem("v_lo"), NT)
            for m in range(NA + 4):
                if m < NA:
                    scores(m)
                if 2 <= m < NA + 2:
                    turn_probs(m - 2)
                if 3 <= m < NA + 3:
                    values(m - 3)
                if m >= 4 and ATT[m - 4][1] == H - 1:
                    turn_output(ATT[m - 4][0])

            e.wait_ge(sem("at_ulo"), len(UNITS))
            for L in range(len(L6) + 2):
                if L < len(L6):
                    c, j = L6[L]
                    if j == 0:
                        B.ready(e, B_OUT + c)
                    if L >= 4:
                        e.wait_ge(sem("l6_ev"), L - 3)
                    mm = lin(e, PS[0:rows(j), L % 4, :], lambda k: ct_hi[:, k, :] if k < 4 else xa_hi[:, k - 4, :],
                             lambda k: ct_lo[:, k, :] if k < 4 else xa_lo[:, k - 4, :],
                             w_hi[c], w_lo[c], range(KT), tcols(j))
                    mm.then_inc(sem("l6_mm"), 1)
                if L >= NT + 2:
                    N2.pe_turn(e, L - NT - 2, lambda j: xnorm2[0:rows(j), j % 2, :])

            e.wait_ge(sem("l6_ev"), len(L6))
            for L in range(len(L6) + 2):
                if L < len(L6):
                    c, j = L6[L]
                    if j == 0:
                        B.ready(e, B_Q + c)
                    if L >= 4:
                        e.wait_ge(sem("q7_raw"), upto("q7_raw", L - 3))
                    mm = lin(e, PS[0:rows(j), L % 4, :], lambda k: xb_hi[:, k, :], lambda k: xb_lo[:, k, :],
                             w_hi[c], w_lo[c], range(KT), tcols(j))
                    mm.then_inc(sem("q7_mm"), 1)
                if L >= 2:
                    q = L - 2
                    n = rows(L6[q][1])
                    e.wait_ge(sem("q7_n"), upto("q7_n", q + 1))
                    if q >= 2:
                        e.wait_ge(sem("q7_te"), upto("q7_te", q - 1))
                    for p in range(4):
                        t = e.transpose(PS[:, 4 + q % 2, p * P:p * P + n], qraw[0:n, q % 3, p * P:(p + 1) * P],
                                        ident[0:n, 0:n])
                    t.then_inc(sem("q7_tp"), 1)
            e.wait_ge(sem("q7_raw"), upto("q7_raw", len(L6)))
            e.wait_ge(sem("q7_te"), upto("q7_te", len(L6)))
            def memory_scores(j):
                if j >= 1:
                    e.wait_ge(sem("ma_exp"), upto("ma_exp", j))
                for hh in range(MH):
                    out = PS[:, hh // 2, (hh % 2) * NMEM:(hh % 2 + 1) * NMEM]
                    e.matmul(out, mqT[:, 2 * hh, tcols(j)], mkT[:, 2 * hh, :], start=True, stop=False)
                    mm = e.matmul(out, mqT[:, 2 * hh + 1, tcols(j)], mkT[:, 2 * hh + 1, :], start=False, stop=True)
                mm.then_inc(sem("ma_qk"), 1)

            def memory_turn(q):
                e.wait_ge(sem("ma_p"), upto("ma_p", q + 1))
                if q >= 1:
                    e.wait_ge(sem("ma_pte"), upto("ma_pte", q))
                for c in range(8):
                    t = e.transpose(PS[:, 2 + c // 4, (c % 4) * P:(c % 4 + 1) * P],
                                    mlog[:, q % 2, c * P:(c + 1) * P], ident[:, :])
                t.then_inc(sem("ma_tt"), 1)

            def memory_values(q, half):
                if half == 0:
                    e.wait_ge(sem("ma_pte"), upto("ma_pte", q + 1))
                    if q >= 1:
                        e.wait_ge(sem("ma_lo"), upto("ma_lo", q))
                for c in range(4 * half, 4 * half + 4):
                    hh = c // 2
                    out = PS[:, 4 + half, (c % 4) * P:(c % 4 + 1) * P]
                    e.matmul(out, mv[:, 0, c * P:(c + 1) * P], mpT[:, q % 2, 2 * hh, :], start=True, stop=False)
                    mm = e.matmul(out, mv[:, 1, c * P:(c + 1) * P], mpT[:, q % 2, 2 * hh + 1, :], start=False, stop=True)
                if half == 1:
                    mm.then_inc(sem("ma_pv"), 1)

            def turn_memory_keys(n):
                e.wait_ge(sem(f"mkb_ld{n % MKR}"), upto(f"mkb_ld{n % MKR}", 16 * (n // MKR + 1)))
                if n >= 1:
                    e.wait_ge(sem("mkb_ev"), upto("mkb_ev", n))
                for kk in range(2):
                    for c in range(2):
                        t = e.transpose(PS[:, 6, kk * 256 + c * P:kk * 256 + (c + 1) * P],
                                        mkpages[n % MKR][:, c, kk * P:(kk + 1) * P], ident[:, :])
                t.then_inc(sem("mkb_tp"), 1)

            def sample_memory_scores(hh):
                e.wait_ge(sem("mkb_ev"), upto("mkb_ev", (hh + 1) * DEC_B))
                e.wait_ge(sem("qmm"), hh + 1)
                if hh >= 1:
                    e.wait_ge(sem("sm_lo"), hh)
                for b in range(DEC_B):
                    for kk in range(2):
                        mm = e.matmul(PS[0:NS, 7, 0:NMEM], qm_m[:, kk * 512 + b * NS:kk * 512 + (b + 1) * NS],
                                      mKT[:, kk, b * NMEM:(b + 1) * NMEM],
                                      start=(b == 0 and kk == 0), stop=(b == DEC_B - 1 and kk == 1))
                mm.then_inc(sem("ms_qk"), 1)

            def sample_memory_turn(hh):
                e.wait_ge(sem("ms_p"), hh + 1)
                for c in range(2):
                    t = e.transpose(PS[:, 7, 256 + c * NS:256 + (c + 1) * NS], mp_s[:, c * P:(c + 1) * P], ident[0:NS, 0:NS])
                t.then_inc(sem("ms_tt"), 1)

            def sample_memory_values(hh, half):
                e.wait_ge(sem("ms_pte"), hh + 1)
                for b in range(4 * half, 4 * half + 4):
                    n = hh * DEC_B + b
                    e.wait_ge(sem(f"mvb_ld{n % 4}"), upto(f"mvb_ld{n % 4}", 16 * (n // 4 + 1)))
                    for dd in range(2):
                        out = PS[:, 7, 384 + dd * NS + b * DEC_T:384 + dd * NS + (b + 1) * DEC_T]
                        for mc in range(2):
                            mm = e.matmul(out, mvpage[:, n % 4, mc, dd * P:(dd + 1) * P],
                                          mpT_s[:, mc * NS + b * DEC_T:mc * NS + (b + 1) * DEC_T],
                                          start=(mc == 0), stop=(mc == 1))
                    mm.then_inc(sem("mvb_used"), 1)

            e.wait_ge(sem("mem_moved"), 2)
            for j in range(NB + 2):
                if j < NB:
                    memory_scores(j)
                    turn_memory_keys(4 * j)
                if j % 2 == 1 and j >= 3:
                    sample_memory_values((j - 3) // 2, 1)
                if 1 <= j <= NB:
                    memory_turn(j - 1)
                if j < NB:
                    turn_memory_keys(4 * j + 1)
                if j % 2 == 0 and j >= 2:
                    sample_memory_turn(j // 2 - 1)
                if j >= 2:
                    memory_values(j - 2, 0)
                if j < NB:
                    turn_memory_keys(4 * j + 2)
                if j >= 2:
                    memory_values(j - 2, 1)
                if j < NB:
                    turn_memory_keys(4 * j + 3)
                if j % 2 == 0 and j >= 2:
                    sample_memory_values(j // 2 - 1, 0)
                if j % 2 == 1 and j < NB:
                    sample_memory_scores(j // 2)
            e.wait_ge(sem("ma_lo"), upto("ma_lo", NB))
            e.wait_ge(sem("sm_lo"), MH)
            for L in range(len(L6) + 2):
                if L < len(L6):
                    c, j = L6[L]
                    if j == 0:
                        C.ready(e, c)
                    if L >= 4:
                        e.wait_ge(sem("l8_ev"), upto("l8_ev", L - 3))
                    mm = lin(e, PS[0:rows(j), L % 4, :], lambda k: xb_hi[:, k, :], lambda k: xb_lo[:, k, :],
                             w_hi[c], w_lo[c], range(KT), tcols(j))
                    mm.then_inc(sem("l8_mm"), 1)
                if L >= NT + 2:
                    N3.pe_turn(e, L - NT - 2, lambda j: xnorm[0:rows(j), j % 2, :])

            e.wait_ge(sem("l8_ev"), upto("l8_ev", len(L6)))
            for f in range(FT):
                for g in range(2):
                    n = 2 * f + g
                    e.wait_ge(sem("fw_lo"), n + 1)
                    if f >= 1:
                        e.wait_ge(sem("f_gate" if g == 0 else "f_mul"), upto("f_gate" if g == 0 else "f_mul", f))
                    for t, (t0, tn) in enumerate(token_chunks()):
                        out = PS[:, 3 * g + t, 0:tn]
                        if n == 0:
                            e.wait_ge(sem("n3_lo"), upto("n3_lo", min(4 * (t + 1), NT)))
                        for k in range(KT):
                            wh, wl = (w[:, f % 2, g, k * P:(k + 1) * P] for w in (fw_hi, fw_lo))
                            e.matmul(out, wh, xa_hi[:, k, t0:t0 + tn], start=(k == 0), stop=False)
                            e.matmul(out, wh, xa_lo[:, k, t0:t0 + tn], start=False, stop=False)
                            mm = e.matmul(out, wl, xa_hi[:, k, t0:t0 + tn], start=False, stop=(k == KT - 1))
                    mm.then_inc(sem("gu_mm"), 1)
            for c in range(4):
                wh, wl = (w[:, c % 2, :].rearrange("p (k n) -> p k n", n=256) for w in (dw_hi, dw_lo))
                for j in range(NT):
                    n = c * NT + j
                    if n >= 2:
                        e.wait_ge(sem("down_ev"), n - 1)
                    out = PS[0:rows(j), 6 + n % 2, 0:256]
                    for k in range(FT):
                        if j == 0 and k % 11 == 0 and c == 0:
                            e.wait_ge(sem("dw_lo_first"), k // 11 + 1)
                        if j == 0 and k % 11 == 0 and c >= 1:
                            e.wait_ge(sem("dw_lo"), upto("dw_lo", 2 * (c - 1) + k // 11 + 1))
                        if n == 0:
                            e.wait_ge(sem("f_lo"), k + 1)
                        e.matmul(out, ffn_hi[:, k, tcols(j)], wh[:, k, :], start=(k == 0), stop=False)
                        e.matmul(out, ffn_lo[:, k, tcols(j)], wh[:, k, :], start=False, stop=False)
                        mm = e.matmul(out, ffn_hi[:, k, tcols(j)], wl[:, k, :], start=False, stop=(k == FT - 1))
                    mm.then_inc(sem("down_mm"), 1)
                if c == 0:
                    e.wait_ge(sem("f_mul"), FT)
                    e.wait_ge(sem("f_st"), FT)
                    for f in range(FT):
                        t = e.transpose(PS[0:18, f // 4, (f % 4) * P:(f % 4 + 1) * P], g_state[:, f, :], ident[:, :])
                    t.then_inc(sem("ffnst_tp"), 1)

        @block.scalar
        def _(e):
            def copy(out, in_, name, **kw):
                e.activation(out, in_, ACT.Copy, **kw).then_inc(sem(name), 1)

            e.wait_ge(sem("eps"), 1)
            A.split_hi(e, 0)

            def project_items(first, end):
                for step in range(first, end + 5):
                    if step < NT:
                        N1.act_root(e, step)
                    if 2 <= step <= NT + 1:
                        N1.act_hi(e, step - 2)
                    L = step - 3
                    if first <= L < end:
                        c, j = ITEMS[L]
                        n, w = rows(j), A.chunks[c][1]
                        e.wait_ge(sem("s2_mm"), L + 1)
                        if L >= first + 3:
                            e.wait_ge(sem("s2_roped"), L - 2)
                        if L >= NI1:
                            e.activation(raws[1][0:n, L % 3, 0:w], PS[0:n, L % 2, 0:w], ACT.Copy)
                            for hh in range(H):
                                d = slice(hh * HD, (hh + 1) * HD)
                                c0 = 48 + H * (L % 2) + hh
                                x = e.activation(squares[0:n, d], PS[0:n, L % 2, d], ACT.Square,
                                                 accum_out=stat[0:n, c0:c0 + 1])
                            x.then_inc(sem("s2_raw"), 1)
                            e.wait_ge(sem("s2_raw"), L + 1)
                            if L >= NI1 + 2:
                                e.wait_ge(sem("s2_n"), L - NI1 - 1)
                            c0 = H * (L % 2)
                            e.activation(stat[0:n, 64 + c0:72 + c0], stat[0:n, 48 + c0:56 + c0], ACT.Sqrt,
                                         bias=eps[0:n, :], scale=1.0 / HD).then_inc(sem("s2_rt"), 1)
                        else:
                            copy(raws[0][0:n, L % 3, 0:w], PS[0:n, L % 2, 0:w], "s2_raw")
                        if j == 0:
                            A.split_hi(e, c + 1)
                    q = step - 5
                    if first <= q < end:
                        c, j = ITEMS[q]
                        n = rows(j)
                        bank = PS[:, 2 + q % 2, :].rearrange("p (a b) -> p a b", b=P)[:, :, 0:n]
                        e.wait_ge(sem("s2_tp"), q + 1)
                        if c in (A_Q, A_K):
                            copy({A_Q: qT, A_K: kT}[c][:, :, tcols(j)], bank, "s2_te")
                        elif j == NB:
                            copy(kiT_s[:, :] if c == A_KI else qiT_s[:, :, :], bank[:, 0, :] if c == A_KI else bank, "s2_te")
                        elif c == A_KI:
                            copy(ki_hi[:, tcols(j)], bank[:, 0, :], "s2_te")
                        else:
                            e.activation(own_half(0)[:, :, tcols(j)], bank[0:HD], ACT.Copy)
                            copy(own_half(1)[:, :, tcols(j)], bank[HD:P], "s2_te")

            project_items(0, NI1)
            e.wait_ge(sem("st_tp"), 1)
            copy(mix_sw[:, :, :].rearrange("p a b -> p (a b)"), PS[:, 6, 0:NC_T * 20], "st_ev")
            copy(ffn_sw[:, :, :].rearrange("p a b -> p (a b)"), PS[:, 7, 0:FT * 20], "st_ev")
            for m in range(ND):
                e.wait_ge(sem("s3_mm"), m + 1)
                if m >= 2:
                    e.wait_ge(sem("s3_acc"), m - 1)
                n = (DOTS[m][0] + 1) * P
                e.activation(relu[:, m % 2, 0:n], PS[:, 2 * (m % 2):2 * (m % 2) + 2, :]
                             .rearrange("p a b -> p (a b)")[:, 0:n], ACT.Relu).then_inc(sem("s3_relu"), 1)
            e.wait_ge(sem("ik_tp"), 1)
            copy(kiTb[:, :, 0:PAST], PS[:, 4:8, :].rearrange("p a (b c) -> p (a b) c", c=PAST), "ik_ev")
            copy(kiTb[:, :, PAST:S_KEYS], kiT_s[:, :].rearrange("p (b c) -> p b c", c=DEC_T), "ik_ev")
            for x, item in enumerate(L4):
                if item[0] == "v":
                    j = item[1]
                    n = rows(j)
                    e.wait_ge(sem("s4_mm"), x + 1)
                    if j >= 2:
                        e.wait_ge(sem(f"v_st{j % 2}"), 16 * (j // 2))
                        e.wait_ge(sem("v_lo"), j - 1)
                    copy(v_f32[0:n, j % 2, :], PS[0:n, x % 8, :], "v_f32")
                    copy(v_hi[0:n, j, :], PS[0:n, x % 8, :], "s4_ev")
                    if j == 0:
                        A.split_hi(e, A_Q)
                    continue
                _, f, t, g = item
                t0, tn = token_chunks()[t]
                if t == 0 and g == 0:
                    if f >= 1:
                        e.wait_ge(sem("conv_lo"), f)
                e.wait_ge(sem("s4_mm"), x + 1)
                copy((cb_s, cc_s, ch_s)[g][:, t0:t0 + tn], PS[:, x % 8, 0:tn], "s4_ev")
                if t == 0 and g == 0:
                    A.split_hi(e, A_CONV + f + 1)
                if t == 2 and g == 2:
                    e.wait_ge(sem("conv_u"), f + 1)
                    for tap, out in enumerate((cc_s, ch_s, tap2)):
                        copy(out[:, 0:CW], u_s[:, tap:tap + CW], "conv_t", scale=mix_sw[:, f, 16 + tap:17 + tap])
                    e.wait_ge(sem("conv_y"), f + 1)
                    e.wait_ge(sem("s3_acc"), ND)
                    copy(ct_hi[:, f, :], ch_s[:, 0:T], "conv_hi")
            e.wait_ge(sem("conv_lo"), NC_T)
            project_items(NI1, NI)
            e.wait_ge(sem("mixst_tp"), 1)
            copy(mixst[:, :], PS[0:18, 7, :], "mixst_ev")
            def sample_keys(b):
                for pg in range(NPG):
                    e.wait_ge(sem("kb_tp"), 2 * b + pg + 1)
                    if pg == 0 and b >= 2:
                        e.wait_ge(sem("sa_qk"), b - 1)
                    copy(kTb[:, b % 2, :].rearrange("p (a b) -> p a b", b=S_KEYS)[:, :, pg * PAGE:(pg + 1) * PAGE],
                         PS[:, 2 + pg, :].rearrange("p (a b) -> p a b", b=P), "kb_ev")

            for b in range(DEC_B + 1):
                if b < DEC_B:
                    sample_keys(b)
                if b == 0:
                    B.split_hi(e, 0)
                if b == 5:
                    B.split_hi(e, 1)
                if b < DEC_B:
                    e.wait_ge(sem("sa_nm"), b + 1)
                    if b >= 2:
                        e.wait_ge(sem("sa_tt"), b - 1)
                    e.activation(p_s[:, b % 2, :], PS[0:NS, b % 2, 0:S_KEYS], ACT.Exp, bias=sat_st[:, 1, b:b + 1],
                                 scale=ATT_SCALE, accum_out=sat_st[:, 2, b:b + 1]).then_inc(sem("sa_exp"), 1)
                if b >= 1:
                    q = b - 1
                    e.wait_ge(sem("sa_tt"), q + 1)
                    if q >= 2:
                        e.wait_ge(sem("sv_used"), q - 1)
                    copy(pT_s[:, q % 2, 0:2 * NS], PS[:, 4, 0:2 * NS], "sa_pte")
                    copy(pT_s[0:DEC_T, q % 2, 2 * NS:3 * NS], PS[0:DEC_T, 4, 2 * NS:3 * NS], "sa_pte")
            e.wait_ge(sem("sv_used"), DEC_B)
            copy(xa_hi[:, 0:4, SEQ:T], PS[:, 5, 0:4 * NS].rearrange("p (a b) -> p a b", b=NS), "sa_hi")
            e.wait_ge(sem("st_out"), 32)
            for j in range(2):
                NM.act_root(e, j)
            for j in range(2):
                NM.act_hi(e, j)

            for it in range(8):
                c, j = it // 2, it % 2
                e.wait_ge(sem("mkv_mm"), it + 1)
                if c < 2:
                    copy(mraw[:, it, :], PS[:, it % 4, :], "mkv_ev")
                    e.wait_ge(sem("mk_ss"), upto("mk_ss", it + 1))
                    e.activation(stat[:, 72:74], stat[:, 64:66], ACT.Sqrt, bias=eps[:, :],
                                 scale=1.0 / MD).then_inc(sem("mk_rt"), 1)
                else:
                    copy(mv0[:, j, (c - 2) * 512:(c - 1) * 512], PS[:, it % 4, :], "mkv_ev")
                if it == 1:
                    B.split_hi(e, 2)
                if it >= 4:
                    q = it - 4
                    cq, jq = q // 2, q % 2
                    e.wait_ge(sem("mk_tp"), q + 1)
                    copy(mkT0[:, 4 * cq:4 * cq + 4, jq * P:(jq + 1) * P],
                         PS[:, 4 + q % 2, :].rearrange("p (a b) -> p a b", b=P), "mk_te")
                if it == 5:
                    B.split_hi(e, 3)
            for m in range(NA + 4):
                if m in (8, 24):
                    B.split_hi(e, 4 if m == 8 else 5)
                if 2 <= m < NA + 2:
                    q = m - 2
                    if q >= 2:
                        e.wait_ge(sem("at_pv"), q - 1)
                    for u in units_of[q]:
                        _, c0, c1 = UNITS[u]
                        e.wait_ge(sem("at_tt"), u + 1)
                        copy(pT_hi[:, q % 2, c0:c1, :].rearrange("p a b -> p (a b)"),
                             PS[:, 4 + u % 3, 0:(c1 - c0) * P], "at_uhi")
                if m >= 4 and ATT[m - 4][1] == H - 1:
                    i = ATT[m - 4][0]
                    u = out_unit[i]
                    e.wait_ge(sem("at_tt"), u + 1)
                    copy(xa_hi[:, 0:4, tcols(i)], PS[:, 4 + u % 3, :].rearrange("p (a b) -> p a b", b=P), "at_uhi")
                if m < NA:
                    i, hh = ATT[m]
                    n = (i + 1) * P
                    e.wait_ge(sem("at_nm"), m + 1)
                    e.activation(logit[:, m % 3, 0:n], logit[:, m % 3, 0:n], ACT.Exp, bias=att_st[:, m % 3, 1:2],
                                 scale=ATT_SCALE, accum_out=att_sum[:, i % 2, 0, hh:hh + 1]).then_inc(sem("at_exp"), 1)
            B.split_hi(e, 6)
            N2.ready = lambda e, j: e.wait_ge(sem("l6_ev"), NT + j + 1)
            for j in range(NT + 2):
                if j >= 2:
                    N2.act_hi(e, j - 2)
                if j < NT:
                    N2.act_root(e, j)
            B.split_hi(e, 7)
            e.wait_ge(sem("mv_st"), 64)
            e.wait_ge(sem("n2_lo"), upto("n2_lo", NT))
            e.wait_ge(sem("mem_moved"), 2)
            for L in range(len(L6) + 2):
                if L < len(L6):
                    n = rows(L6[L][1])
                    e.wait_ge(sem("q7_mm"), upto("q7_mm", L + 1))
                    if L >= 3:
                        e.wait_ge(sem("q7_tp"), upto("q7_tp", L - 2))
                    copy(qraw[0:n, L % 3, :], PS[0:n, L % 4, :], "q7_raw")
                if L >= 2:
                    q = L - 2
                    c, j = L6[q]
                    e.wait_ge(sem("q7_tp"), upto("q7_tp", q + 1))
                    copy(mqT[:, 4 * c:4 * c + 4, tcols(j)],
                         PS[:, 4 + q % 2, :].rearrange("p (a b) -> p a b", b=P)[:, :, 0:rows(j)], "q7_te")
                if L < len(L6):
                    e.wait_ge(sem("q7_ss"), upto("q7_ss", L + 1))
                    e.activation(stat[0:n, 72:74], stat[0:n, 64:66], ACT.Sqrt, bias=eps[0:n, :],
                                 scale=1.0 / MD).then_inc(sem("q7_rt"), 1)
            def memory_keys(n):
                e.wait_ge(sem("mkb_tp"), upto("mkb_tp", n + 1))
                if n % DEC_B == 0 and n > 0:
                    e.wait_ge(sem("ms_qk"), n // DEC_B)
                b = n % DEC_B
                copy(mKT[:, :, b * NMEM:(b + 1) * NMEM],
                     PS[:, 6, :].rearrange("p (a b) -> p a b", a=2), "mkb_ev")

            for j in range(NB + 2):
                hh = j // 2 - 1
                if j % 2 == 0 and j >= 2:
                    e.wait_ge(sem("ms_nm"), hh + 1)
                    if hh >= 1:
                        e.wait_ge(sem("ms_tt"), hh)
                    e.activation(mp_s[:, :], PS[0:NS, 7, 0:NMEM], ACT.Exp, bias=sat_st[:, 1, hh:hh + 1],
                                 scale=MEM_SCALE, accum_out=sat_st[:, 2, hh:hh + 1]).then_inc(sem("ms_exp"), 1)
                if j < NB:
                    memory_keys(4 * j)
                if j == 0:
                    memory_keys(1)
                if j < NB:
                    e.wait_ge(sem("ma_nm"), upto("ma_nm", j + 1))
                    if j >= 2:
                        e.wait_ge(sem("ma_tt"), upto("ma_tt", j - 1))
                    for hh in range(MH):
                        x = e.activation(mlog[:, j % 2, hh * NMEM:(hh + 1) * NMEM],
                                         PS[:, hh // 2, (hh % 2) * NMEM:(hh % 2 + 1) * NMEM], ACT.Exp,
                                         bias=mat_st[:, j % 2, 1, hh:hh + 1], scale=MEM_SCALE,
                                         accum_out=mat_st[:, j % 2, 2, hh:hh + 1])
                    x.then_inc(sem("ma_exp"), 1)
                if 1 <= j <= NB:
                    q = j - 1
                    e.wait_ge(sem("ma_tt"), upto("ma_tt", q + 1))
                    if q >= 2:
                        e.wait_ge(sem("ma_pv"), upto("ma_pv", q - 1))
                    copy(mpT[:, q % 2, :, :].rearrange("p a b -> p (a b)"),
                         PS[:, 2:4, :].rearrange("p a b -> p (a b)"), "ma_pte")
                if j % 2 == 1 and j >= 3:
                    hh = (j - 3) // 2
                    e.wait_ge(sem("mvb_used"), (hh + 1) * DEC_B)
                    copy(xb_hi[:, 2 * hh:2 * hh + 2, SEQ:T],
                         PS[:, 7, 384:512].rearrange("p (a b) -> p a b", b=NS), "sm_hi")
                if 1 <= j < NB:
                    memory_keys(4 * j + 1)
                if j % 2 == 0 and j >= 2:
                    e.wait_ge(sem("ms_tt"), j // 2)
                    if j >= 4:
                        e.wait_ge(sem("mvb_used"), (j // 2 - 1) * DEC_B)
                    copy(mpT_s[:, :], PS[:, 7, 256:256 + 2 * NS], "ms_pte")
                if j < NB:
                    for n in range(4 * j + 2, 4 * j + 4):
                        memory_keys(n)
                if j >= 2:
                    q = j - 2
                    e.wait_ge(sem("ma_pv"), upto("ma_pv", q + 1))
                    copy(xb_hi[:, :, tcols(q)], PS[:, 4:6, :].rearrange("p a (c q) -> p (a c) q", q=P), "ma_hi")
                if j == NB:
                    C.split_hi(e, 0)
            C.split_hi(e, 1)
            def gu_hi(n):
                f, g = n // 2, n % 2
                e.wait_ge(sem(f"fw_ld{g}"), upto(f"fw_ld{g}", 16 * (f + 1)))
                if n >= 4:
                    e.wait_ge(sem("gu_mm"), n - 3)
                copy(fw_hi[:, f % 2, g, :], fst[:, g, :, :].rearrange("p a b -> p (a b)"), "fw_hi")

            gu_hi(0)
            gu_hi(1)
            N3.ready = lambda e, j: e.wait_ge(sem("l8_ev"), upto("l8_ev", NT + j + 1))
            for j in range(NT + 2):
                if j >= 2:
                    N3.act_hi(e, j - 2)
                if j < NT:
                    N3.act_root(e, j)

            def down_hi(c, half):
                if c == 0:
                    e.wait_ge(sem("gu_mm"), 2 * FT)
                if c >= 2:
                    e.wait_ge(sem("down_mm"), NT * (c - 1))
                e.wait_ge(sem(f"dw_ld{half}"), upto(f"dw_ld{half}", 16 * (c + 1)))
                copy(dw_hi[:, c % 2, half * 11 * 256:(half + 1) * 11 * 256],
                     dst[:, half, :, :].rearrange("p a b -> p (a b)"), "dw_hi")

            e.wait_ge(sem("h3_st"), 16 * NT)
            for f in range(FT):
                if f + 1 < FT:
                    gu_hi(2 * f + 2)
                    gu_hi(2 * f + 3)
                e.wait_ge(sem("gu_mm"), 2 * f + 1)
                if f >= 1:
                    e.wait_ge(sem("f_conv"), f)
                    e.wait_ge(sem("f_st"), f)
                e.activation(gate_s[:, 2:2 + SEQ], PS[:, 0:2, :].rearrange("p a b -> p (a b)"), ACT.Copy)
                copy(gate_s[:, SB0:SB0 + DEC_B * STR].rearrange("p (b c) -> p b c", c=STR)[:, :, 2:STR],
                     PS[:, 2, 0:NS].rearrange("p (b c) -> p b c", c=DEC_T), "f_gate")
                e.wait_ge(sem("f_conv"), f + 1)
                e.activation(conv_s[:, f % 2, 0:CW], conv_s[:, f % 2, 0:CW], ACT.Silu,
                             bias=ffn_sw[:, f, 19:20]).then_inc(sem("f_silu"), 1)
                if f == FT - 1:
                    down_hi(0, 0)
                e.wait_ge(sem("f_mul"), f + 1)
                e.activation(ffn_hi[:, f, 0:SEQ], conv_s[:, f % 2, 0:SEQ], ACT.Copy)
                copy(ffn_hi[:, f, SEQ:T].rearrange("p (b c) -> p b c", c=DEC_T),
                     conv_s[:, f % 2, SB0:SB0 + DEC_B * STR].rearrange("p (b c) -> p b c", c=STR)[:, :, 0:DEC_T],
                     "f_hi")
            down_hi(0, 1)
            down_hi(1, 0)
            down_hi(1, 1)
            e.wait_ge(sem("ffnst_tp"), upto("ffnst_tp", 1))
            e.activation(ffnst[:, 0:2560], PS[0:18, 0:5, :].rearrange("p a b -> p (a b)"), ACT.Copy)
            copy(ffnst[:, 2560:DFF], PS[0:18, 5, 0:DFF - 2560], "ffnst_ev")
            for c in range(2, 4):
                for half in range(2):
                    down_hi(c, half)

        @block.vector
        def _(e):
            cnt = [0]

            def link(ins):
                chain(e, ins, "dve", cnt)

            e.memset(eps[:, :], EPS).then_inc(sem("eps"), 1)
            e.wait_ge(sem("first"), 16 * FIRSTS)

            def head_norm(L, n, v, heads, width, gain, tmp, s_ss, s_rt, last):
                vh = v.rearrange("p (a d) -> p a d", d=width)
                link(e.tensor_tensor(tmp[0:n, :], v, v, ALU.mult))
                e.tensor_reduce(stat[0:n, 64:64 + heads], tmp[0:n, :].rearrange("p (a d) -> p a d", d=width), AX.X,
                                ALU.add).then_inc(sem(s_ss), 1)
                e.wait_ge(sem(s_rt), upto(s_rt, L + 1))
                link(e.reciprocal(stat[0:n, 80:80 + heads], stat[0:n, 72:72 + heads]))
                link(e.tensor_tensor(vh, vh, stat[0:n, 80:80 + heads][:, :, None].broadcast_to([n, heads, width]),
                                     ALU.mult))
                e.tensor_tensor(vh, vh, gain[:, None, :].broadcast_to([n, heads, width]), ALU.mult
                                ).then_inc(sem(last), 1)

            def project_item(L):
                c, j = ITEMS[L]
                n = rows(j)
                raw, rope1, rope2, roped = (v[group(L)] for v in (raws, rope1s, rope2s, ropeds))
                e.wait_ge(sem("s2_raw"), L + 1)
                if L >= NI1:
                    c0 = 64 + H * (L % 2)
                    vh = raw[0:n, L % 3, :].rearrange("p (a d) -> p a d", d=HD)
                    e.wait_ge(sem("s2_rt"), L - NI1 + 1)
                    link(e.reciprocal(stat[0:n, 80:80 + H], stat[0:n, c0:c0 + H]))
                    link(e.tensor_tensor(vh, vh, stat[0:n, 80:80 + H][:, :, None].broadcast_to([n, H, HD]),
                                         ALU.mult))
                    e.tensor_tensor(vh, vh, qkg[0:n, int(c == A_K), :][:, None, :].broadcast_to([n, H, HD]), ALU.mult
                                    ).then_inc(sem("s2_n"), 1)
                    return
                groups = 1 if c == A_KI else H
                w = groups * HD
                r = raw[0:n, L % 3, 0:w].rearrange("p (a d) -> p a d", d=32)
                rr = raw[0:n, L % 3, 0:w].rearrange("p (a two d) -> p a two d", two=2, d=32)
                t2 = rope2[0:n, 0:w].rearrange("p (a two d) -> p a two d", two=2, d=32)
                cs = cos_t[0:n, j, :][:, None, :].broadcast_to([n, 2 * groups, 32])
                sn = sin_t[0:n, j, :][:, None, :].broadcast_to([n, groups, 32])
                e.tensor_tensor(rope1[0:n, 0:w].rearrange("p (a d) -> p a d", d=32), r, cs, ALU.mult)
                e.scalar_tensor_tensor(t2[:, :, 0, :], rr[:, :, 1, :], -1.0, sn, ALU.mult, ALU.mult)
                link(e.tensor_tensor(t2[:, :, 1, :], rr[:, :, 0, :], sn, ALU.mult))
                if L >= 3:
                    e.wait_ge(sem("s2_tp"), L - 2)
                if stores_of_slot(L):
                    e.wait_ge(sem(f"s2_st{L % 3}"), 16 * stores_of_slot(L))
                if c == A_KI:
                    link(e.tensor_scalar(iwt[0:n, j, :], raw[0:n, L % 3, HD:HD + H], IDX_SCALE, None, ALU.mult))
                    link(e.tensor_tensor(roped[0:n, L % 3, HD:2 * HD], rope1[0:n, 0:w], rope2[0:n, 0:w], ALU.add))
                e.tensor_tensor(roped[0:n, L % 3, 0:w], rope1[0:n, 0:w], rope2[0:n, 0:w], ALU.add
                                ).then_inc(sem("s2_roped"), 1)
                e.wait_ge(sem("s2_roped"), L + 1)

            def item_lo(L):
                c, j = ITEMS[L]
                if j == NB:
                    return
                bank = PS[:, 2 + L % 2, :].rearrange("p (a b) -> p a b", b=P)
                e.wait_ge(sem("s2_te"), L + 1)
                if c == A_KI:
                    e.tensor_tensor(ki_lo[:, tcols(j)], bank[:, 0, :], ki_hi[:, tcols(j)], ALU.subtract
                                    ).then_inc(sem("s2_lo"), 1)
                else:
                    for odd in range(2):
                        x = e.tensor_tensor(other_half(odd)[:, :, tcols(j)], bank[HD * odd:HD * (odd + 1)],
                                            own_half(odd)[:, :, tcols(j)], ALU.subtract)
                    x.then_inc(sem("s2_lo"), 1)

            for step in range(NI1 + 6):
                if step < NT:
                    N1.dve_norm(e, step, lambda j: h[0:rows(j), j, :])
                if 2 <= step <= NT + 1:
                    N1.dve_lo(e, step - 2)
                if 4 <= step < NI1 + 4:
                    project_item(step - 4)
                if step >= 6:
                    item_lo(step - 6)

            e.wait_ge(sem("const"), 16 * CONSTS)
            e.wait_ge(sem("selc"), 48)
            e.tensor_tensor(w_sel[:, :].rearrange("p (a b) -> p a b", b=DEC_T),
                            c_tt[:, :].rearrange("p (a b) -> p a b", b=DEC_T),
                            iwt[0:NS, NB, :][:, :, None].broadcast_to([NS, H, DEC_T]), ALU.mult
                            ).then_inc(sem("w_sel"), 1)
            for m in range(ND):
                e.wait_ge(sem("s3_relu"), m + 1)
                i, hh = DOTS[m]
                n = (i + 1) * P
                out = work[:, topk_cols(i):topk_cols(i) + n]
                src, w = relu[:, m % 2, 0:n], iwt[:, i, hh:hh + 1]
                if hh == 0:
                    x = e.tensor_scalar(out, src, w, None, ALU.mult)
                else:
                    x = e.scalar_tensor_tensor(out, src, w, out, ALU.mult, ALU.add)
                x.then_inc(sem("s3_acc"), 1)
                e.wait_ge(sem("s3_acc"), m + 1)
                if hh == H - 1:
                    d = work[:, topk_cols(i) + i * P:topk_cols(i) + n]
                    link(e.tensor_tensor(d, d, mask01[:, P:2 * P], ALU.add))
            e.wait_ge(sem("w_mm"), 1)
            link(e.tensor_copy(w_ht[:, :], PS[0:NS, 0, 0:DEC_B]))
            for b in range(DEC_B):
                e.wait_ge(sem("sd_mm"), b + 1)
                if b >= 2:
                    e.wait_ge(sem("sd_sum"), b - 1)
                e.tensor_scalar(w_relu[:, b % 2, :], PS[0:NS, 1 + b % 2, 0:S_KEYS], 0.0, w_ht[:, b:b + 1],
                                ALU.max, ALU.mult).then_inc(sem("w_relu"), 1)
            e.wait_ge(sem("sd_sum"), DEC_B)
            e.tensor_copy(work_s[:, 0:PAST], PS[0:NS, 3, 0:PAST])
            e.memset(work_s[:, S_KEYS:S_KEYS + 8], NEG)
            e.tensor_tensor(work_s[:, PAST:S_KEYS], PS[0:NS, 3, PAST:S_KEYS], smask[0:NS, :], ALU.add
                            ).then_inc(sem("ws_ev"), 1)
            e.wait_ge(sem("ws_ev"), 1)

            def take(v, n, left):
                link(e.max(m8[0:n, :], v))
                if left < 8:
                    link(e.memset(m8[0:n, left:8], NEG))
                link(e.match_replace(v, m8[0:n, :], v, NEG))

            def marked(v):
                e.tensor_scalar(v, v, NEG, MASKED, ALU.not_equal, ALU.mult).then_inc(sem("topk"), 1)

            for left in range(TOPK_S, 0, -8):
                take(work_s[:, :], NS, left)
            marked(work_s[:, :])

            def selection():
                for i in range(2, NB):
                    v = work[:, topk_cols(i):topk_cols(i) + (i + 1) * P]
                    for left in range(TOPK, 0, -8):
                        take(v, P, left)
                        taken[0] += 1
                        if left <= 8:
                            marked(v)
                        yield

            taken = [0]
            rounds = selection()

            def turn(n):
                for _ in range(n):
                    next(rounds, None)

            turn(ROUNDS_BEFORE)
            for L in range(NI1, NI):
                project_item(L)
                turn(ROUNDS_ITEM[L % 2])

            turn(ROUNDS_SAMPLE0)
            for b in range(DEC_B):
                e.wait_ge(sem("sa_qk"), b + 1)
                link(e.tensor_reduce(sat_st[:, 0, b:b + 1], PS[0:NS, b % 2, 0:S_KEYS], AX.X, ALU.max))
                e.tensor_scalar(sat_st[:, 1, b:b + 1], sat_st[:, 0, b:b + 1], -ATT_SCALE, None, ALU.mult
                                ).then_inc(sem("sa_nm"), 1)
                e.wait_ge(sem("sa_exp"), b + 1)
                link(e.reciprocal(sat_st[:, 3, b:b + 1], sat_st[:, 2, b:b + 1]))
                e.tensor_scalar(p_s[:, b % 2, :], p_s[:, b % 2, :], sat_st[:, 3, b:b + 1], None, ALU.mult
                                ).then_inc(sem("sa_p"), 1)
                turn(ROUNDS_SAMPLE)
            e.wait_ge(sem("sa_hi"), 1)
            e.tensor_tensor(xa_lo[:, 0:4, SEQ:T], PS[:, 5, 0:4 * NS].rearrange("p (a b) -> p a b", b=NS),
                            xa_hi[:, 0:4, SEQ:T], ALU.subtract).then_inc(sem("sa_lo"), 1)
            turn(ROUNDS_TOKENS)
            e.wait_ge(sem("g_ld"), 16)
            for j in range(2):
                NM.dve_norm(e, j, lambda j: memx[:, j, :])
            for j in range(2):
                NM.dve_lo(e, j)
            turn(ROUNDS_KEYS)
            for it in range(4):
                e.wait_ge(sem("mkv_ev"), it + 1)
                head_norm(it, P, mraw[:, it, :], 2, MD, mqkg[:, 1, :], mtmp, "mk_ss", "mk_rt", "mk_out")
                turn(ROUNDS_MEMORY)
            turn(ROUNDS_VALUES)
            e.wait_ge(sem("st_out"), 32)
            e.wait_ge(sem("mk_st"), 64)
            e.wait_ge(sem("mk_te"), 4)
            e.wait_ge(sem("mkv_ev"), 8)

            for m in range(NA + 4):
                if m < NA:
                    i, hh = ATT[m]
                    n = (i + 1) * P
                    mask = mask01[:, P:2 * P] if i == 0 else mask01[:, :] if i == 1 else \
                        work[:, topk_cols(i):topk_cols(i) + n]
                    if i >= 2 and hh == 0:
                        turn(max(0, TOPK // 8 * (i - 1) - taken[0]))
                        e.wait_ge(sem("topk"), i)
                    e.wait_ge(sem("at_qk"), m + 1)
                    if m >= 3:
                        e.wait_ge(sem("at_tt"), units_of[m - 3][-1] + 1)
                    e.tensor_tensor_reduce(logit[:, m % 3, 0:n],
                                           PS[:, 2 * (m % 2):2 * (m % 2) + 2, :].rearrange("p a b -> p (a b)")[:, 0:n],
                                           mask, 1.0, NEG, ALU.add, ALU.max,
                                           att_st[:, m % 3, 0:1]).then_inc(sem("at_max"), 1)
                    e.wait_ge(sem("at_max"), m + 1)
                    e.tensor_scalar(att_st[:, m % 3, 1:2], att_st[:, m % 3, 0:1], -ATT_SCALE, None, ALU.mult
                                    ).then_inc(sem("at_nm"), 1)
                if m >= 4 and ATT[m - 4][1] == H - 1:
                    i = ATT[m - 4][0]
                    link(e.reciprocal(att_sum[:, i % 2, 1, :], att_sum[:, i % 2, 0, :]))
                    e.wait_ge(sem("at_pv"), H * (i + 1))
                    if i >= 1:
                        e.wait_ge(sem("at_tt"), out_unit[i - 1] + 1)
                    e.tensor_tensor(att_n.rearrange("p (a b) -> p a b", b=HD),
                                    PS[:, 7, :].rearrange("p (a b) -> p a b", b=HD),
                                    att_sum[:, i % 2, 1, :][:, :, None].broadcast_to([P, H, HD]), ALU.mult
                                    ).then_inc(sem("at_n"), 1)
                if 2 <= m < NA + 2:
                    q = m - 2
                    for u in units_of[q]:
                        _, c0, c1 = UNITS[u]
                        e.wait_ge(sem("at_uhi"), u + 1)
                        e.tensor_tensor(pT_lo[:, q % 2, c0:c1, :].rearrange("p a b -> p (a b)"),
                                        PS[:, 4 + u % 3, 0:(c1 - c0) * P],
                                        pT_hi[:, q % 2, c0:c1, :].rearrange("p a b -> p (a b)"), ALU.subtract
                                        ).then_inc(sem("at_ulo"), 1)
                if m >= 4 and ATT[m - 4][1] == H - 1:
                    i = ATT[m - 4][0]
                    u = out_unit[i]
                    e.wait_ge(sem("at_uhi"), u + 1)
                    e.tensor_tensor(xa_lo[:, 0:4, tcols(i)], PS[:, 4 + u % 3, :].rearrange("p (a b) -> p a b", b=P),
                                    xa_hi[:, 0:4, tcols(i)], ALU.subtract).then_inc(sem("at_ulo"), 1)
                turn(ROUNDS_ATT)

            def residual(name, norm, normed, first_ready, gsem):
                for L in range(len(L6) + 2):
                    if L < len(L6):
                        c, j = L6[L]
                        n = rows(j)
                        e.wait_ge(sem(f"{name}_mm"), upto(f"{name}_mm", L + 1))
                        first_ready(L, j)
                        v = h[0:n, j, c * 512:(c + 1) * 512]
                        e.tensor_tensor(v, PS[0:n, L % 4, :], v, ALU.add).then_inc(sem(f"{name}_ev"), 1)
                    if NT + 1 <= L <= 2 * NT:
                        if L == NT + 1:
                            e.wait_ge(sem("g_ld"), gsem)
                        norm.dve_norm(e, L - NT - 1, lambda j: normed[0:rows(j), j % 2, :])
                    if L >= NT + 2:
                        norm.dve_lo(e, L - NT - 2)

            e.wait_ge(sem("mem_moved"), 2)
            residual("l6", N2, xnorm2, lambda L, j: e.wait_ge(sem(f"x2_ld{x_group(j)}"), upto(f"x2_ld{x_group(j)}", 16 if j < 3 else 48)), 32)
            for L in range(len(L6)):
                n = rows(L6[L][1])
                e.wait_ge(sem("q7_raw"), upto("q7_raw", L + 1))
                head_norm(L, n, qraw[0:n, L % 3, :], 2, MD, mqkg[0:n, 0, :], qtmp, "q7_ss", "q7_rt", "q7_n")
            for j in range(NB + 2):
                hh = j // 2 - 1
                if j % 2 == 0 and j >= 2:
                    e.wait_ge(sem("ms_qk"), hh + 1)
                    link(e.tensor_reduce(sat_st[:, 0, hh:hh + 1], PS[0:NS, 7, 0:NMEM], AX.X, ALU.max))
                    e.tensor_scalar(sat_st[:, 1, hh:hh + 1], sat_st[:, 0, hh:hh + 1], -MEM_SCALE, None, ALU.mult
                                    ).then_inc(sem("ms_nm"), 1)
                if j < NB:
                    e.wait_ge(sem("ma_qk"), upto("ma_qk", j + 1))
                    link(e.tensor_reduce(mat_st[:, j % 2, 0, :],
                                         PS[:, 0:2, :].rearrange("p a (b c) -> p (a b) c", b=2), AX.X, ALU.max))
                    e.tensor_scalar(mat_st[:, j % 2, 1, :], mat_st[:, j % 2, 0, :], -MEM_SCALE, None, ALU.mult
                                    ).then_inc(sem("ma_nm"), 1)
                if j % 2 == 0 and j >= 2:
                    e.wait_ge(sem("ms_exp"), hh + 1)
                    link(e.reciprocal(sat_st[:, 3, hh:hh + 1], sat_st[:, 2, hh:hh + 1]))
                    e.tensor_scalar(mp_s[:, :], mp_s[:, :], sat_st[:, 3, hh:hh + 1], None, ALU.mult
                                    ).then_inc(sem("ms_p"), 1)
                if j < NB:
                    e.wait_ge(sem("ma_exp"), upto("ma_exp", j + 1))
                    link(e.reciprocal(mat_st[:, j % 2, 3, :], mat_st[:, j % 2, 2, :]))
                    v = mlog[:, j % 2, :].rearrange("p (a b) -> p a b", b=NMEM)
                    e.tensor_tensor(v, v, mat_st[:, j % 2, 3, :][:, :, None].broadcast_to([P, MH, NMEM]), ALU.mult
                                    ).then_inc(sem("ma_p"), 1)
                if j % 2 == 1 and j >= 3:
                    hh = (j - 3) // 2
                    e.wait_ge(sem("sm_hi"), hh + 1)
                    e.tensor_tensor(xb_lo[:, 2 * hh:2 * hh + 2, SEQ:T],
                                    PS[:, 7, 384:512].rearrange("p (a b) -> p a b", b=NS),
                                    xb_hi[:, 2 * hh:2 * hh + 2, SEQ:T], ALU.subtract).then_inc(sem("sm_lo"), 1)
                if j >= 2:
                    q = j - 2
                    e.wait_ge(sem("ma_hi"), upto("ma_hi", q + 1))
                    e.tensor_tensor(xb_lo[:, :, tcols(q)], PS[:, 4:6, :].rearrange("p a (c q) -> p (a c) q", q=P),
                                    xb_hi[:, :, tcols(q)], ALU.subtract).then_inc(sem("ma_lo"), 1)
            residual("l8", N3, xnorm, lambda L, j: None, 48)
            for f in range(FT):
                e.wait_ge(sem("f_gate"), f + 1)
                e.wait_ge(sem("f_pre"), f + 1)
                if f >= 2:
                    e.wait_ge(sem("f_lo"), f - 1)
                cv = conv_s[:, f % 2, 0:CW]
                link(e.tensor_scalar(cv, gate_s[:, 0:CW], ffn_sw[:, f, 16:17], None, ALU.mult))
                link(e.scalar_tensor_tensor(cv, gate_s[:, 1:1 + CW], ffn_sw[:, f, 17:18], cv, ALU.mult, ALU.add))
                e.scalar_tensor_tensor(cv, gate_s[:, 2:2 + CW], ffn_sw[:, f, 18:19], cv, ALU.mult, ALU.add
                                       ).then_inc(sem("f_conv"), 1)
                e.wait_ge(sem("f_silu"), f + 1)
                e.wait_ge(sem("gu_mm"), 2 * f + 2)
                v = conv_s[:, f % 2, 0:SEQ]
                e.tensor_tensor(v, PS[:, 3:5, :].rearrange("p a b -> p (a b)"), v, ALU.mult)
                v = conv_s[:, f % 2, SB0:SB0 + DEC_B * STR].rearrange("p (b c) -> p b c", c=STR)[:, :, 0:DEC_T]
                e.tensor_tensor(v, PS[:, 5, 0:NS].rearrange("p (b c) -> p b c", c=DEC_T), v, ALU.mult
                                ).then_inc(sem("f_mul"), 1)
            down_lo(e, 0)
            for n in range(4 * NT):
                r = rows(n % NT)
                e.wait_ge(sem("down_mm"), n + 1)
                e.wait_ge(sem(f"res_ld{n % 4}"), upto(f"res_ld{n % 4}", 16 * (n // 4 + 1)))
                if n >= 4:
                    e.wait_ge(sem(f"y_st{n % 4}"), upto(f"y_st{n % 4}", 16 * (n // 4)))
                e.tensor_tensor(outb[0:r, n % 4, :], PS[0:r, 6 + n % 2, 0:256], res[0:r, n % 4, :], ALU.add
                                ).then_inc(sem("down_ev"), 1)

        @block.gpsimd
        def _(e):
            for n in range(3):
                A.split_lo(e, n)

            def by_head(out, src, name):
                for hh in range(H):
                    r = slice((hh % 2) * HD, (hh % 2 + 1) * HD)
                    e.tensor_copy(out(hh)[r, :, hh * DEC_T:(hh + 1) * DEC_T],
                                  src[r, hh // 2, :].rearrange("p (b c) -> p b c", c=DEC_T)
                                  ).then_inc(sem(name), 1)

            e.wait_ge(sem("s2_te"), NI1)
            e.memset(qi_ht[:, :, :], 0.0).then_inc(sem("qi_ht"), 1)
            e.wait_ge(sem("qi_ht"), 1)
            by_head(lambda hh: qi_ht, qiT_s, "qi_ht")
            e.wait_ge(sem("qi_ht"), H + 1)
            cnt = [0]

            def link(ins):
                chain(e, ins, "pool", cnt)

            def spaced(v):
                return v[:, SB0:SB0 + DEC_B * STR].rearrange("p (b c) -> p b c", c=STR)[:, :, 0:DEC_T]

            us = u_s[:, SB0:SB0 + DEC_B * STR].rearrange("p (b c) -> p b c", c=STR)

            def sample(v):
                return v[:, SEQ:T].rearrange("p (b c) -> p b c", c=DEC_T)

            last_of = {f: max(x for x, it in enumerate(L4) if it[0] == "c" and it[1] == f) for f in range(NC_T)}
            for f in range(NC_T):
                A.split_lo(e, A_CONV + f + 1)
                e.wait_ge(sem("s4_ev"), last_of[f] + 1)
                if f == 0:
                    e.memset(u_s[:, 0:2], 0.0)
                e.tensor_copy(us[:, :, 0:2], mix_sw[:, f, 0:16].rearrange("p (b c) -> p b c", c=2))
                e.tensor_tensor(u_s[:, 2:2 + SEQ], cc_s[:, 0:SEQ], ch_s[:, 0:SEQ], ALU.mult)
                link(e.tensor_tensor(us[:, :, 2:STR], sample(cc_s), sample(ch_s), ALU.mult))
                e.tensor_copy(u_state[:, f, 0:16].rearrange("p (b c) -> p b c", c=2), us[:, :, DEC_T:STR])
                e.tensor_copy(u_state[:, f, 16:18], u_s[:, SEQ:SEQ + 2]).then_inc(sem("conv_u"), 1)
                e.wait_ge(sem("conv_t"), 3 * (f + 1))
                link(e.tensor_tensor(cc_s[:, 0:CW], cc_s[:, 0:CW], ch_s[:, 0:CW], ALU.add))
                link(e.tensor_tensor(cc_s[:, 0:CW], cc_s[:, 0:CW], tap2[:, 0:CW], ALU.add))
                e.tensor_tensor(ch_s[:, 0:SEQ], cc_s[:, 0:SEQ], cb_s[:, 0:SEQ], ALU.mult)
                e.tensor_tensor(sample(ch_s), spaced(cc_s), sample(cb_s), ALU.mult).then_inc(sem("conv_y"), 1)
                e.wait_ge(sem("conv_hi"), f + 1)
                e.tensor_tensor(ct_lo[:, f, :], ch_s[:, 0:T], ct_hi[:, f, :], ALU.subtract).then_inc(sem("conv_lo"), 1)
            A.split_lo(e, A_Q)
            for j in range(NT):
                n = rows(j)
                e.wait_ge(sem("s4_ev"), N4C + j + 1)
                e.tensor_tensor(v_lo[0:n, j, :], v_f32[0:n, j % 2, :], v_hi[0:n, j, :], ALU.subtract
                                ).then_inc(sem("v_lo"), 1)
            for L in range(NI1, NI):
                c, j = ITEMS[L]
                n = rows(j)
                if L in (NI1 + 1, NI1 + 4):
                    A.split_lo(e, A_K, [int(L == NI1 + 4)])
                e.wait_ge(sem("s2_n"), L - NI1 + 1)
                pair = raws[1][0:n, L % 3, :].rearrange("p (a two d) -> p a two d", two=2, d=32)
                r = raws[1][0:n, L % 3, :].rearrange("p (a d) -> p a d", d=32)
                t1 = rope1s[1][0:n, :].rearrange("p (a two d) -> p a two d", two=2, d=32)
                t2 = rope2s[1][0:n, :].rearrange("p (a two d) -> p a two d", two=2, d=32)
                cs = cos_t[0:n, j, :][:, None, :].broadcast_to([n, 2 * H, 32])
                sn = sin_t[0:n, j, :][:, None, :].broadcast_to([n, H, 32])
                e.tensor_tensor(rope1s[1][0:n, :].rearrange("p (a d) -> p a d", d=32), r, cs, ALU.mult)
                e.tensor_tensor(t2[:, :, 0, :], pair[:, :, 1, :], sn, ALU.mult)
                link(e.tensor_tensor(t2[:, :, 1, :], pair[:, :, 0, :], sn, ALU.mult))
                if L >= 3:
                    e.wait_ge(sem("s2_tp"), L - 2)
                if stores_of_slot(L):
                    e.wait_ge(sem(f"s2_st{L % 3}"), 16 * stores_of_slot(L))
                out = ropeds[1][0:n, L % 3, :].rearrange("p (a two d) -> p a two d", two=2, d=32)
                e.tensor_tensor(out[:, :, 0, :], t1[:, :, 0, :], t2[:, :, 0, :], ALU.subtract)
                e.tensor_tensor(out[:, :, 1, :], t1[:, :, 1, :], t2[:, :, 1, :], ALU.add
                                ).then_inc(sem("s2_roped"), 1)
                e.wait_ge(sem("s2_roped"), L + 1)
            e.wait_ge(sem("s2_te"), NI)
            for k in range(3):
                e.wait_ge(sem(f"s2_st{k}"), 16 * len([m for m in STORED if m % 3 == k]))
            e.memset(q_ht[:, :, :, :], 0.0).then_inc(sem("q_ht"), 1)
            e.wait_ge(sem("q_ht"), 1)
            by_head(lambda hh: q_ht[:, hh // 2, :, :], qT[:, :, SEQ:T], "q_ht")
            e.wait_ge(sem("q_ht"), H + 1)
            for b in range(DEC_B):
                if b >= 2:
                    e.wait_ge(sem("sa_qk"), b - 1)
                e.tensor_copy(kTb[:, b % 2, :].rearrange("p (a b) -> p a b", b=S_KEYS)[:, :, PAST:S_KEYS],
                              kT[:, :, SEQ + b * DEC_T:SEQ + (b + 1) * DEC_T]).then_inc(sem("kb_new"), 1)
                if b == 1:
                    B.split_lo(e, 0)
                if b == 6:
                    B.split_lo(e, 1)
            for n in range(2, 6):
                B.split_lo(e, n)
            e.wait_ge(sem("at_pv"), NA)
            e.wait_ge(sem("at_ulo"), len(UNITS))
            e.tensor_copy(mkT[:, :, :], mkT0[:, :, :]).then_inc(sem("mem_moved"), 1)
            e.tensor_copy(mv[:, :, :], mv0[:, :, :]).then_inc(sem("mem_moved"), 1)
            for n in range(6, 8):
                B.split_lo(e, n)
            e.wait_ge(sem("q7_mm"), upto("q7_mm", 2 * NT))
            link(e.memset(qm_m[:, :], 0.0))
            e.wait_ge(sem("q7_te"), upto("q7_te", len(L6)))
            for hh in range(MH):
                if hh >= 1:
                    e.wait_ge(sem("ms_qk"), hh)
                for kk in range(2):
                    x = e.tensor_copy(mask_view(qm_m, kk),
                                      mqT[:, 2 * hh + kk, SEQ:T].rearrange("p (b c) -> p b c", c=DEC_T))
                x.then_inc(sem("qmm"), 1)
            for n in range(2):
                C.split_lo(e, n)

            def gu_lo(n):
                f, g = n // 2, n % 2
                e.wait_ge(sem("fw_hi"), n + 1)
                e.tensor_tensor(fw_lo[:, f % 2, g, :], fst[:, g, :, :].rearrange("p a b -> p (a b)"),
                                fw_hi[:, f % 2, g, :], ALU.subtract).then_inc(sem("fw_lo"), 1)

            gs = gate_s[:, SB0:SB0 + DEC_B * STR].rearrange("p (b c) -> p b c", c=STR)
            e.wait_ge(sem("l8_mm"), upto("l8_mm", NT))
            gu_lo(0)
            gu_lo(1)
            e.memset(gate_s[:, 0:2], 0.0)
            for f in range(FT):
                if f >= 1:
                    e.wait_ge(sem("f_conv"), f)
                e.tensor_copy(gs[:, :, 0:2], ffn_sw[:, f, 0:16].rearrange("p (b c) -> p b c", c=2)
                              ).then_inc(sem("f_pre"), 1)
                if f + 1 < FT:
                    gu_lo(2 * f + 2)
                    gu_lo(2 * f + 3)
                e.wait_ge(sem("f_gate"), f + 1)
                e.tensor_copy(g_state[:, f, 0:16].rearrange("p (b c) -> p b c", c=2), gs[:, :, DEC_T:STR])
                e.tensor_copy(g_state[:, f, 16:18], gate_s[:, SEQ:SEQ + 2]).then_inc(sem("f_st"), 1)
                e.wait_ge(sem("f_hi"), f + 1)
                e.tensor_tensor(ffn_lo[:, f, 0:SEQ], conv_s[:, f % 2, 0:SEQ], ffn_hi[:, f, 0:SEQ], ALU.subtract)
                e.tensor_tensor(ffn_lo[:, f, SEQ:T].rearrange("p (b c) -> p b c", c=DEC_T),
                                conv_s[:, f % 2, SB0:SB0 + DEC_B * STR].rearrange("p (b c) -> p b c", c=STR)[:, :, 0:DEC_T],
                                ffn_hi[:, f, SEQ:T].rearrange("p (b c) -> p b c", c=DEC_T), ALU.subtract
                                ).then_inc(sem("f_lo"), 1)

            e.wait_ge(sem("gu_mm"), 2 * FT)
            for c in range(4):
                for j in range(NT):
                    n = c * NT + j
                    if n >= 4:
                        e.wait_ge(sem("down_ev"), n - 3)
                    e.dma_start(res[0:rows(j), n % 4, :],
                                h3[j * P:j * P + rows(j), c * 256:(c + 1) * 256]).then_inc(sem(f"res_ld{n % 4}"), 16)
                    if j == 3 and c + 1 < 4:
                        down_lo(e, c + 1)


INPUTS = ["x_prompt", "x_sample", "cache_k", "cache_v", "cache_idx_k", "state_conv_mix", "state_conv_ffn",
          "cache_mem_k", "cache_mem_v", "page_table", "mem_prompt", "g_mix", "w_in", "conv_mix_w", "q_norm_g",
          "k_norm_g", "w_out", "g_mem", "g_mem_src", "w_q_mem", "w_kv_mem", "mq_norm_g", "mk_norm_g", "w_o_mem",
          "g_ffn", "w_gu", "conv_ffn_w", "conv_ffn_b", "w_down"]
OUTPUTS = [("o_yp", (1, SEQ, D)), ("o_ys", (DEC_B, DEC_T, D)), ("o_kp", (1, 1, SEQ, H, HD)),
           ("o_vp", (1, 1, SEQ, H, HD)), ("o_ikp", (1, 1, SEQ, HD)), ("o_cmp", (1, 1, 2, DC)),
           ("o_cfp", (1, 1, 2, DFF)), ("o_mk", (1, 1, NMEM, MH, MD)), ("o_mv", (1, 1, NMEM, MH, MD)),
           ("o_ks", (1, DEC_B, DEC_T, H, HD)), ("o_vs", (1, DEC_B, DEC_T, H, HD)), ("o_iks", (1, DEC_B, DEC_T, HD)),
           ("o_cms", (1, DEC_B, 2, DC)), ("o_cfs", (1, DEC_B, 2, DFF))]


def constants():
    pos = np.concatenate([np.arange(SEQ), np.tile(PAST + np.arange(DEC_T), P // DEC_T)]).astype(np.float32)
    inv = np.exp(np.arange(HD // 2) * (-2.0 * math.log(10000.0) / HD)).astype(np.float32)
    ang = pos[:, None] * inv[None, :]
    row = np.arange(P)
    r = np.arange(NS)
    same_t = r[:, None] % DEC_T == r[None, :] % DEC_T
    sel = ((r[:, None] // DEC_T == np.arange(DEC_B)[None, :])[:, :, None] & same_t[:, None, :]).astype(np.float32)
    causal = np.where(row[None, :] <= row[:, None], 0.0, MASKED).astype(np.float32)
    return {
        "c_cos": np.cos(ang).astype(np.float32),
        "c_sin": np.sin(ang).astype(np.float32),
        "c_mask": np.concatenate([np.zeros((P, P), np.float32), causal], axis=1),
        "c_smask": np.where(np.arange(DEC_T)[None, :] <= (np.arange(NS) % DEC_T)[:, None], 0.0, MASKED).astype(np.float32),
        "c_ident": np.eye(P, dtype=np.float32),
        "c_sel": sel,
        "c_sum": np.ascontiguousarray(sel.transpose(2, 1, 0)),
        "c_tt": same_t.astype(np.float32),
        "c_bb": (r[:, None] // DEC_T == np.arange(DEC_B)[None, :]).astype(np.float32),
    }


def kernel(**inputs):
    import concourse.bacc as bacc
    from concourse.bass_utils import run_bass_kernel_spmd

    nc = bacc.Bacc("TRN2", target_bir_lowering=False, num_devices=1)
    arrays = {name: np.ascontiguousarray(inputs[name]) for name in INPUTS}
    arrays.update(constants())
    io = {name: nc.dram_tensor(name, a.shape, mybir.dt.from_np(a.dtype), kind="ExternalInput").ap()
          for name, a in arrays.items()}
    for name, shape in OUTPUTS:
        io[name] = nc.dram_tensor(name, shape, F32, kind="ExternalOutput").ap()
    build(nc, io)
    got = run_bass_kernel_spmd(nc, [arrays], core_ids=[0]).results[0]
    return tuple(got[name] for name, _ in OUTPUTS)
```
